# Optimizing a Trainium2 kernel written in Bass

```python
import math
import jax, jax.numpy as jnp
from jax import lax
import numpy as np

D_MODEL = 1024
BATCH = 1
SEQ = 256
DEPTH = 2
DEC_BATCH = 8
DEC_SEQ = 8
PAST_LEN = 1024
PAGE_SIZE = 128

N_A_LAYERS = DEPTH // 2
N_B_LAYERS = DEPTH - N_A_LAYERS
POOL_WINDOWS = (2, 4, 8, 16)
N_POOL_GROUPS = len(POOL_WINDOWS)
POOL_GROUP_DIM = D_MODEL // N_POOL_GROUPS
POOL_STATE = max(POOL_WINDOWS) - 1
N_HEADS = 16
HEAD_DIM = D_MODEL // N_HEADS
N_KV_HEADS = 4
HEADS_PER_KV = N_HEADS // N_KV_HEADS
CMP_BLOCK = 32
CMP_STRIDE = 16
CMP_HIDDEN = 2 * HEAD_DIM
SEL_BLOCK = 64
N_SEL = 16
WINDOW = 512
Q_BLOCK = 128
SEL_Q_BLOCK = 64
N_PAGED_SLOTS = 4
ROPE_THETA = 10000.0
SCALE = HEAD_DIM ** -0.5
N_GROUPS = 4
EXPERTS_PER_GROUP = 4
N_EXPERTS = N_GROUPS * EXPERTS_PER_GROUP
D_EXPERT = 512
TOP_K_INNER = 2

EPS = 1e-6
NEG = -1e30
TINY = 1e-30
BIG = 1e4

kernel_name = 'yoco_pool_nsa_hmoe_step'

def rms_norm(x, g):
    xf = x.astype(jnp.float32)
    y = xf * lax.rsqrt(jnp.mean(xf * xf, axis=-1, keepdims=True) + EPS) * g.astype(jnp.float32)
    return y.astype(x.dtype)

def rope(x, pos):
    half = HEAD_DIM // 2
    inv = 1.0 / (ROPE_THETA ** (jnp.arange(half, dtype=jnp.float32) * (2.0 / HEAD_DIM)))
    ang = pos.astype(jnp.float32)[:, None] * inv[None, :]
    c = jnp.cos(ang)[None, :, None, :]
    s = jnp.sin(ang)[None, :, None, :]
    xf = x.astype(jnp.float32)
    x1, x2 = xf[..., :half], xf[..., half:]
    return jnp.concatenate([x1 * c - x2 * s, x2 * c + x1 * s], axis=-1).astype(x.dtype)

def masked_softmax(s, mask):
    s = jnp.where(mask, s.astype(jnp.float32), NEG)
    m = jnp.max(s, axis=-1, keepdims=True)
    p = jnp.where(mask, jnp.exp(s - m), 0.0)
    return p / jnp.maximum(jnp.sum(p, axis=-1, keepdims=True), TINY)

def pool_mix(ext, n_prev, w_pool, scale):
    T = ext.shape[1] - n_prev
    cs = jnp.pad(jnp.cumsum(ext.astype(jnp.float32), axis=1), ((0, 0), (1, 0), (0, 0)))
    end = jnp.arange(T) + (n_prev + 1)
    x_new = ext[:, n_prev:].astype(jnp.float32)
    outs = []
    for g, w in enumerate(POOL_WINDOWS):
        lo, hi = g * POOL_GROUP_DIM, (g + 1) * POOL_GROUP_DIM
        start = jnp.maximum(end - w, 0)
        cnt = (end - start).astype(jnp.float32)[None, :, None]
        mean = (cs[:, end, lo:hi] - cs[:, start, lo:hi]) / cnt
        outs.append(jnp.einsum('btc,cd->btd', (mean - x_new[..., lo:hi]).astype(ext.dtype), w_pool[g]))
    return (jnp.concatenate(outs, axis=-1) * scale).astype(ext.dtype)

def hmoe(xn, r_group, r_expert, w_gu, w_down):
    B, T, D = xn.shape
    x2 = xn.reshape(B * T, D)
    n = x2.shape[0]
    pg = jax.nn.softmax((x2 @ r_group).astype(jnp.float32), axis=-1)
    g_val, g_idx = lax.top_k(pg, 1)
    le = (x2 @ r_expert).astype(jnp.float32).reshape(n, N_GROUPS, EXPERTS_PER_GROUP)
    le_g = le[jnp.arange(n), g_idx[:, 0]]
    pe = jax.nn.softmax(le_g, axis=-1)
    e_val, e_idx = lax.top_k(pe, TOP_K_INNER)
    wts = g_val * (e_val / jnp.sum(e_val, axis=-1, keepdims=True))
    eid = g_idx * EXPERTS_PER_GROUP + e_idx
    comb = jnp.sum(jax.nn.one_hot(eid, N_EXPERTS, dtype=jnp.float32) * wts[..., None], axis=1)
    y = jnp.zeros((n, D), jnp.float32)
    for e in range(N_EXPERTS):
        gu = x2 @ w_gu[e]
        hdn = jax.nn.silu(gu[:, :D_EXPERT]) * gu[:, D_EXPERT:]
        y = y + comb[:, e:e + 1] * (hdn @ w_down[e]).astype(jnp.float32)
    return y.astype(xn.dtype).reshape(B, T, D)

def compress(raw, pe, w1, b1, w2):
    B, L = raw.shape[:2]
    n_chunk = L // CMP_STRIDE
    ratio = CMP_BLOCK // CMP_STRIDE
    nc = n_chunk - ratio + 1
    ch = raw[:, :n_chunk * CMP_STRIDE].reshape(B, n_chunk, CMP_STRIDE, N_KV_HEADS, HEAD_DIM)
    blocks = jnp.concatenate([ch[:, r:r + nc] for r in range(ratio)], axis=2)
    blocks = blocks + pe[None, None, :, None, :]
    flat = blocks.transpose(0, 1, 3, 2, 4).reshape(B, nc, N_KV_HEADS, CMP_BLOCK * HEAD_DIM)
    out = jax.nn.gelu(flat @ w1 + b1) @ w2
    return out.transpose(0, 2, 1, 3)

def sel_block_view(k_full):
    B, L = k_full.shape[:2]
    n_sb = -(-L // SEL_BLOCK)
    kp = jnp.pad(k_full, ((0, 0), (0, n_sb * SEL_BLOCK - L), (0, 0), (0, 0)))
    return kp.reshape(B, n_sb, SEL_BLOCK, N_KV_HEADS, HEAD_DIM).transpose(0, 3, 1, 2, 4).reshape(
        B, N_KV_HEADS, n_sb, SEL_BLOCK * HEAD_DIM)

def build_shared_kv(h, pos, kv_past, win_prev, kv_norm, w_kv, k_norm, cmp_pe, cmp_w1, cmp_b1, cmp_w2):
    B, T, _ = h.shape
    kv = (rms_norm(h, kv_norm) @ w_kv).reshape(B, T, 6, N_KV_HEADS, HEAD_DIM)
    k_sel = rope(rms_norm(kv[:, :, 2], k_norm[1]), pos)
    k_win = rope(rms_norm(kv[:, :, 4], k_norm[2]), pos)
    kv_new = jnp.stack([kv[:, :, 0], kv[:, :, 1], k_sel, kv[:, :, 3]], axis=2)
    win_rows = jnp.stack([k_win, kv[:, :, 5]], axis=2)
    if kv_past is None:
        kv_full = kv_new
    else:
        kv_full = jnp.concatenate([kv_past.astype(kv_new.dtype), kv_new], axis=1)
    ck = rms_norm(compress(kv_full[:, :, 0], cmp_pe[0], cmp_w1[0], cmp_b1[0], cmp_w2[0]), k_norm[0])
    cv = compress(kv_full[:, :, 1], cmp_pe[1], cmp_w1[1], cmp_b1[1], cmp_w2[1])
    cend = jnp.arange(ck.shape[2]) * CMP_STRIDE + (CMP_BLOCK - 1)
    ksb = sel_block_view(kv_full[:, :, 2])
    vsb = sel_block_view(kv_full[:, :, 3])
    if win_prev is None:
        win_new = win_rows[:, -min(WINDOW, T):]
        wk, wv, wpos = win_rows[:, :, 0], win_rows[:, :, 1], None
    else:
        nbuf = win_prev.shape[1]
        wfull = jnp.concatenate([win_prev.astype(win_rows.dtype), win_rows], axis=1)
        win_new = wfull[:, -nbuf:]
        wk, wv = wfull[:, :, 0], wfull[:, :, 1]
        wpos = jnp.concatenate([pos[0] - nbuf + jnp.arange(nbuf), pos])
    return {'ck': ck, 'cv': cv, 'cend': cend, 'ksb': ksb, 'vsb': vsb, 'wk': wk, 'wv': wv,
            'wpos': wpos, 'kv_new': kv_new, 'win_new': win_new}

def select_blocks(p_cmp, qpos, n_sb):
    pg = jnp.sum(p_cmp, axis=2)
    nc = pg.shape[-1]
    offs = jnp.arange(1 - CMP_BLOCK // CMP_STRIDE, SEL_BLOCK // CMP_STRIDE)
    ci = (SEL_BLOCK // CMP_STRIDE) * jnp.arange(n_sb)[:, None] + offs[None, :]
    ok = (ci >= 0) & (ci < nc)
    gathered = jnp.take(pg, jnp.clip(ci, 0, nc - 1), axis=-1)
    score = jnp.sum(jnp.where(ok, gathered, 0.0), axis=-1)
    j = jnp.arange(n_sb)[None, :]
    cur = (qpos // SEL_BLOCK)[:, None]
    selectable = j * SEL_BLOCK <= qpos[:, None]
    forced = (j == 0) | (j == cur) | (j == cur - 1)
    score = jnp.where(selectable, score + jnp.where(forced, BIG, 0.0), -BIG)
    _, idx = lax.top_k(score, min(N_SEL, n_sb))
    return idx

def sel_attend_chunk(q, idx, qpos, ksb, vsb):
    B, G, HP, Tq, _ = q.shape
    k = idx.shape[-1]
    flat = idx.reshape(B, G, Tq * k)
    bi = jnp.arange(B)[:, None, None]
    gi = jnp.arange(G)[None, :, None]
    kg = ksb[bi, gi, flat].reshape(B, G, Tq, k, SEL_BLOCK, HEAD_DIM)
    vg = vsb[bi, gi, flat].reshape(B, G, Tq, k, SEL_BLOCK, HEAD_DIM)
    s = jnp.einsum('bghtd,bgtksd->bghtks', q, kg).astype(jnp.float32) * SCALE
    kpos = idx[..., None] * SEL_BLOCK + jnp.arange(SEL_BLOCK)
    mask = (kpos <= qpos[:, None, None])[:, :, None]
    p = masked_softmax(s.reshape(B, G, HP, Tq, k * SEL_BLOCK), mask.reshape(B, G, 1, Tq, k * SEL_BLOCK))
    p = p.reshape(B, G, HP, Tq, k, SEL_BLOCK).astype(vg.dtype)
    return jnp.einsum('bghtks,bgtksd->bghtd', p, vg)

def sel_attend(q, idx, qpos, ksb, vsb):
    B, G, HP, T, DH = q.shape
    if T <= SEL_Q_BLOCK or T % SEL_Q_BLOCK:
        return sel_attend_chunk(q, idx, qpos, ksb, vsb)
    nq = T // SEL_Q_BLOCK
    qc = q.reshape(B, G, HP, nq, SEL_Q_BLOCK, DH).transpose(3, 0, 1, 2, 4, 5)
    ic = idx.reshape(B, G, nq, SEL_Q_BLOCK, idx.shape[-1]).transpose(2, 0, 1, 3, 4)
    pc = qpos.reshape(nq, SEL_Q_BLOCK)
    out = lax.map(lambda a: sel_attend_chunk(a[0], a[1], a[2], ksb, vsb), (qc, ic, pc))
    return out.transpose(1, 2, 3, 0, 4, 5).reshape(B, G, HP, T, DH)

def window_banded(q, k, v):
    B, G, HP, T, DH = q.shape
    nb = T // Q_BLOCK
    wb = WINDOW // Q_BLOCK

    def bands(x):
        xt = x.transpose(0, 2, 1, 3)
        xp = jnp.pad(xt, ((0, 0), (0, 0), (WINDOW, 0), (0, 0))).reshape(B, G, nb + wb, Q_BLOCK, DH)
        return jnp.concatenate([xp[:, :, w:w + nb] for w in range(wb + 1)], axis=3)

    kb, vb = bands(k), bands(v)
    qb = q.reshape(B, G, HP, nb, Q_BLOCK, DH)
    s = jnp.einsum('bghnqd,bgnkd->bghnqk', qb, kb).astype(jnp.float32) * SCALE
    qpos = jnp.arange(nb)[:, None] * Q_BLOCK + jnp.arange(Q_BLOCK)[None, :]
    kpos = jnp.arange(nb)[:, None] * Q_BLOCK - WINDOW + jnp.arange((wb + 1) * Q_BLOCK)[None, :]
    dq = qpos[:, :, None] - kpos[:, None, :]
    mask = (kpos[:, None, :] >= 0) & (dq >= 0) & (dq < WINDOW)
    p = masked_softmax(s, mask).astype(vb.dtype)
    return jnp.einsum('bghnqk,bgnkd->bghnqd', p, vb).reshape(B, G, HP, T, DH)

def window_buffer(q, qpos, k, v, kpos):
    s = jnp.einsum('bghtd,bkgd->bghtk', q, k).astype(jnp.float32) * SCALE
    dq = qpos[:, None] - kpos[None, :]
    p = masked_softmax(s, (dq >= 0) & (dq < WINDOW)).astype(v.dtype)
    return jnp.einsum('bghtk,bkgd->bghtd', p, v)

def to_groups(a):
    B, T = a.shape[:2]
    return a.reshape(B, T, N_KV_HEADS, HEADS_PER_KV, HEAD_DIM).transpose(0, 2, 3, 1, 4)

def from_groups(a):
    B, T = a.shape[0], a.shape[3]
    return a.transpose(0, 3, 1, 2, 4).reshape(B, T, N_HEADS, HEAD_DIM)

def nsa_mix(xn, qpos, ctx, w_qg, q_norm, w_o):
    B, T, _ = xn.shape
    qg = xn @ w_qg
    q = rms_norm(qg[..., :N_HEADS * HEAD_DIM].reshape(B, T, N_HEADS, HEAD_DIM), q_norm)
    gates = jax.nn.sigmoid(qg[..., N_HEADS * HEAD_DIM:].astype(jnp.float32)).reshape(B, T, 3, N_HEADS)
    qn_g = to_groups(q)
    qr_g = to_groups(rope(q, qpos))
    s = jnp.einsum('bghtd,bgnd->bghtn', qn_g, ctx['ck']).astype(jnp.float32) * SCALE
    p_cmp = masked_softmax(s, ctx['cend'][None, :] <= qpos[:, None])
    o_cmp = jnp.einsum('bghtn,bgnd->bghtd', p_cmp.astype(ctx['cv'].dtype), ctx['cv'])
    idx = select_blocks(p_cmp, qpos, ctx['ksb'].shape[2])
    o_sel = sel_attend(qr_g, idx, qpos, ctx['ksb'], ctx['vsb'])
    if ctx['wpos'] is None:
        o_win = window_banded(qr_g, ctx['wk'], ctx['wv'])
    else:
        o_win = window_buffer(qr_g, qpos, ctx['wk'], ctx['wv'], ctx['wpos'])
    o = (gates[:, :, 0, :, None] * from_groups(o_cmp).astype(jnp.float32)
         + gates[:, :, 1, :, None] * from_groups(o_sel).astype(jnp.float32)
         + gates[:, :, 2, :, None] * from_groups(o_win).astype(jnp.float32))
    return o.astype(xn.dtype).reshape(B, T, N_HEADS * HEAD_DIM) @ w_o

def trunk(x, pos, pool_prev, kv_past, win_prev, params):
    (norm_mix, norm_ffn, pool_w, pool_scale, kv_norm, w_kv, k_norm, cmp_pe, cmp_w1, cmp_b1, cmp_w2,
     w_qg, q_norm, w_o, router_group, router_expert, w_gate_up, w_down) = params
    h = x
    new_pool = []
    ctx = None
    for layer in range(DEPTH):
        if layer < N_A_LAYERS:
            xn = rms_norm(h, norm_mix[layer])
            if pool_prev is None:
                ext, n_prev = xn, 0
            else:
                ext, n_prev = jnp.concatenate([pool_prev[layer].astype(xn.dtype), xn], axis=1), POOL_STATE
            h = h + pool_mix(ext, n_prev, pool_w[layer], pool_scale[layer])
            new_pool.append(ext[:, -POOL_STATE:])
        else:
            if ctx is None:
                ctx = build_shared_kv(h, pos, kv_past, win_prev, kv_norm, w_kv, k_norm,
                                      cmp_pe, cmp_w1, cmp_b1, cmp_w2)
            bi = layer - N_A_LAYERS
            xn = rms_norm(h, norm_mix[layer])
            h = h + nsa_mix(xn, pos, ctx, w_qg[bi], q_norm[bi], w_o[bi])
        h = h + hmoe(rms_norm(h, norm_ffn[layer]), router_group[layer], router_expert[layer],
                     w_gate_up[layer], w_down[layer])
    return h, jnp.stack(new_pool), ctx['kv_new'], ctx['win_new']

def setup_inputs(seed: int = 0) -> dict:
    key = jax.random.key(seed)
    ks = jax.random.split(key, 24)
    f32 = jnp.float32

    def nrm(k, shape, scale):
        return jax.random.normal(k, shape, f32) * scale

    def gain(k, shape):
        return 1.0 + 0.02 * jax.random.normal(k, shape, f32)

    n_pages = PAST_LEN // PAGE_SIZE
    n_pool_pages = (DEC_BATCH * n_pages * 5) // 4
    page_table = jax.random.permutation(ks[4], n_pool_pages)[:DEC_BATCH * n_pages].reshape(
        DEC_BATCH, n_pages).astype(jnp.int32)
    qg_width = N_HEADS * HEAD_DIM + 3 * N_HEADS
    return {
        'x_prompt': nrm(ks[0], (BATCH, SEQ, D_MODEL), 1.0),
        'x_sample': nrm(ks[1], (DEC_BATCH, DEC_SEQ, D_MODEL), 1.0),
        'state_pool': nrm(ks[2], (N_A_LAYERS, DEC_BATCH, POOL_STATE, D_MODEL), 1.0),
        'cache_kv': nrm(ks[3], (n_pool_pages, PAGE_SIZE, N_PAGED_SLOTS, N_KV_HEADS, HEAD_DIM), 1.0),
        'page_table': page_table,
        'state_win': nrm(ks[5], (DEC_BATCH, min(WINDOW, PAST_LEN), 2, N_KV_HEADS, HEAD_DIM), 1.0),
        'norm_mix': gain(ks[6], (DEPTH, D_MODEL)),
        'norm_ffn': gain(ks[7], (DEPTH, D_MODEL)),
        'pool_w': nrm(ks[8], (N_A_LAYERS, N_POOL_GROUPS, POOL_GROUP_DIM, POOL_GROUP_DIM), POOL_GROUP_DIM ** -0.5),
        'pool_scale': gain(ks[9], (N_A_LAYERS, D_MODEL)),
        'kv_norm': gain(ks[10], (D_MODEL,)),
        'w_kv': nrm(ks[11], (D_MODEL, 6 * N_KV_HEADS * HEAD_DIM), D_MODEL ** -0.5),
        'k_norm': gain(ks[12], (3, HEAD_DIM)),
        'cmp_pe': nrm(ks[13], (2, CMP_BLOCK, HEAD_DIM), 0.1),
        'cmp_w1': nrm(ks[14], (2, CMP_BLOCK * HEAD_DIM, CMP_HIDDEN), (CMP_BLOCK * HEAD_DIM) ** -0.5),
        'cmp_b1': nrm(ks[15], (2, CMP_HIDDEN), 0.02),
        'cmp_w2': nrm(ks[16], (2, CMP_HIDDEN, HEAD_DIM), CMP_HIDDEN ** -0.5),
        'w_qg': nrm(ks[17], (N_B_LAYERS, D_MODEL, qg_width), D_MODEL ** -0.5),
        'q_norm': gain(ks[18], (N_B_LAYERS, HEAD_DIM)),
        'w_o': nrm(ks[19], (N_B_LAYERS, N_HEADS * HEAD_DIM, D_MODEL), (N_HEADS * HEAD_DIM) ** -0.5),
        'router_group': nrm(ks[20], (DEPTH, D_MODEL, N_GROUPS), D_MODEL ** -0.5),
        'router_expert': nrm(ks[21], (DEPTH, D_MODEL, N_EXPERTS), D_MODEL ** -0.5),
        'w_gate_up': nrm(ks[22], (DEPTH, N_EXPERTS, D_MODEL, 2 * D_EXPERT), D_MODEL ** -0.5),
        'w_down': nrm(ks[23], (DEPTH, N_EXPERTS, D_EXPERT, D_MODEL), D_EXPERT ** -0.5),
    }

def reference(x_prompt, x_sample, state_pool, cache_kv, page_table, state_win, norm_mix, norm_ffn,
              pool_w, pool_scale, kv_norm, w_kv, k_norm, cmp_pe, cmp_w1, cmp_b1, cmp_w2, w_qg, q_norm,
              w_o, router_group, router_expert, w_gate_up, w_down):
    params = (norm_mix, norm_ffn, pool_w, pool_scale, kv_norm, w_kv, k_norm, cmp_pe, cmp_w1, cmp_b1,
              cmp_w2, w_qg, q_norm, w_o, router_group, router_expert, w_gate_up, w_down)
    pos_p = jnp.arange(x_prompt.shape[1])
    y_prompt, new_pool_prompt, new_kv_prompt, new_win_prompt = trunk(
        x_prompt, pos_p, None, None, None, params)
    n_seq, n_pages = page_table.shape
    kv_past = cache_kv[page_table].reshape(n_seq, n_pages * PAGE_SIZE, N_PAGED_SLOTS, N_KV_HEADS, HEAD_DIM)
    pos_s = PAST_LEN + jnp.arange(x_sample.shape[1])
    y_sample, new_pool_sample, new_kv_sample, new_win_sample = trunk(
        x_sample, pos_s, state_pool, kv_past, state_win, params)
    return (y_prompt, y_sample, new_pool_prompt, new_pool_sample, new_kv_prompt, new_kv_sample,
            new_win_prompt, new_win_sample)


_drawn_inputs = setup_inputs


def setup_inputs(seed=0):
    import zlib

    import numpy as np

    out = dict(_drawn_inputs(seed))
    spreads = {}
    factors = {'kv_norm': 2.924, 'k_norm': 3.691, 'cmp_b1': 6.447, 'q_norm': 8.0}
    for name, (base, spread) in spreads.items():
        noise = np.random.default_rng([zlib.crc32(name.encode()), seed]).standard_normal(out[name].shape)
        drawn = base * np.exp(spread * noise) if base else spread * noise
        out[name] = __import__('jax').numpy.asarray(drawn.astype(out[name].dtype))
    for name, factor in factors.items():
        out[name] = (out[name] * factor).astype(out[name].dtype)
    return out
```

```python
from contextlib import ExitStack

import concourse.bass as bass
from concourse import mybir

F32 = mybir.dt.float32
I32 = mybir.dt.int32
ALU = mybir.AluOpType
ACT = mybir.ActivationFunctionType
AX = mybir.AxisListType

P = 128
D = 1024
KD = D // P
SEQ, NSEQ, STEPS = 256, 8, 8
NEWTOK = NSEQ * STEPS
TOK = SEQ + NEWTOK
TILE_ROWS = (P, P, NEWTOK)
NT = len(TILE_ROWS)
PAST, PAGE = 1024, 128
NPAGE = PAST // PAGE
WIN = 512
POOL_WINDOWS = (2, 4, 8, 16)
NPOOL = len(POOL_WINDOWS)
STATE = max(POOL_WINDOWS) - 1
GD = D // NPOOL
HD, NH, NKV = 64, 16, 4
HPG = NH // NKV
CHUNK = 16
HID = 2 * HD
NCP = SEQ // CHUNK - 1
NCS = PAST // CHUNK - 1
SELB = 64
NSB = PAST // SELB + 1
NE, NG, EPG, FE = 16, 4, 4, 512
SCALE = HD ** -0.5
EPS = 1e-6
NEG = -1e30

CONST = {}
_c = 0
for _name, _w in (("ident", P), ("blockones", P), ("headsum", P), ("causal", 2 * SEQ), ("cmpadd", 2 * NCP),
                  ("cmpmul", 2 * NCP), ("newmask", NSEQ * NEWTOK), ("winmask", STEPS), ("iota", NSB - 3),
                  ("stepsel", STEPS), ("seqsel", NSEQ), ("cos", NT * HD // 2), ("sin", NT * HD // 2),
                  ("first", NG)):
    CONST[_name] = (_c, _w)
    _c += _w
NCONST = _c
NPM = SEQ * 2 + NEWTOK * 2


ARENA = 44288


class Map:
    WKV, WQG = 0, 12288
    HEADS = 20864
    KVROWS = HEADS + NT * 24 * HD
    WINROWS = KVROWS + NT * 4 * NKV * HD
    QROPE = 31248
    XT2 = 35344
    GAIN24 = XT2 + KD * TOK
    SQ = GAIN24 + 24 * HD
    ROT = SQ + 24 * HD
    QNT, QRT = 0, 2048
    QSN, QSR = 4096, 4608
    QB = 5120
    KTP = 8192
    KTN = KTP + 2 * 2 * SEQ
    VP = KTN + 2 * 2 * NEWTOK
    GS = VP + 2 * 2 * NKV * 3 * HD
    CKP = GS + 3 * NSEQ
    CVP = CKP + 2 * CHUNK
    W1 = 13600
    W2 = W1 + 2 * 2 * 8 * HID
    BIAS = W2 + 2 * 3 * HD
    PE = BIAS + 2 * HID
    ONES = PE + 32
    VNEW = 18700
    CVB = VNEW + NKV * HD
    SMALL = CVB + 2 * NKV * HD
    GATEL = SMALL + 256
    CV = HEADS
    PC = CV + NSEQ * NKV * HD
    BM = PC + NSEQ * HD
    RP = BM + NSEQ * 16
    CHUNKS = 33664
    PAGES = 33664
    HIDB = 30080
    CKB = HIDB + 4 * 256
    WINB = W1
    PT0, PT1 = 30080, 30080 + 14 * P
    PROW0, PROW1 = 5632, PAGES + 8192
    WO = 33664
    PTC = HEADS
    PTP = PTC + 16 * P
    PP = 30080


class Steps:

    def __init__(self, eng, sem, base=0):
        self.eng, self.sem, self.n, self.base = eng, sem, 0, base

    def add(self, ins):
        ins.then_inc(self.sem, 1)
        self.n += 1
        self.eng.wait_ge(self.sem, self.base + self.n)


def build(nc, I, O):
    with ExitStack() as ctx:
        def sb(name, shape):
            return ctx.enter_context(nc.sbuf_tensor(name, shape, F32))

        M = {}
        M["H"] = sb("residual", [P, NT, D])
        M["XT"] = sb("normedT", [P, KD, TOK])
        M["C"] = sb("constants", [P, NCONST])
        M["gT"] = sb("gainsT", [P, 5, KD])
        M["comb"] = sb("combine_weights", [P, NT, NE])
        M["stat"] = sb("row_stats", [P, 64])
        M["gates"] = sb("gates", [P, NT, 3 * NH])
        M["A"] = sb("arena", [P, ARENA])
        M["pages"] = ctx.enter_context(nc.sbuf_tensor("page_ids", [1, NSEQ * NPAGE], I32))
        M["ps"] = [ctx.enter_context(nc.psum_tensor(f"bank{i}", [P, 512], F32)) for i in range(8)]
        M["kgain"] = sb("compressed_key_gain", [P, 1])
        M["wo_in"] = ctx.enter_context(nc.semaphore("w_o_landed"))

        load_constants(nc, I, M)
        pool_mixer(nc, I, O, M)
        norm_transpose(nc, M, "ffn0", [(1, M["XT"])])
        route(nc, I, M, 0)
        moe(nc, I, M, 0)
        stage_attention(nc, I, O, M)
        norm_transpose(nc, M, "ffn1", [(4, M["XT"])])
        route(nc, I, M, 1)
        moe(nc, I, M, 1)
        store_result(nc, O, M)


def const(M, name, rows=P):
    at, w = CONST[name]
    return M["C"][0:rows, at:at + w]


def load_constants(nc, I, M):
    with ExitStack() as ctx:
        landed = ctx.enter_context(nc.semaphore("constants_landed"))
        block = ctx.enter_context(nc.Block())

        @block.sync
        def _(sp):
            sp.dma_start(M["C"][:, :], I["consts"]).then_inc(landed, 16)
            sp.dma_start(M["gT"][:, :, :], I["gainsT"]).then_inc(landed, 16)
            sp.dma_start(M["pages"][:, :], I["page_ids"]).then_inc(landed, 16)
            for i, rows in enumerate(TILE_ROWS):
                src = I["x_prompt"][0, i * P:(i + 1) * P, :] if i < 2 else \
                    I["x_sample"].rearrange("b t d -> (b t) d")
                sp.dma_start(M["H"][0:rows, i, :], src).then_inc(landed, 16)
            sp.wait_ge(landed, 16 * 6)

        @block.vector
        def _(dve):
            nc.vector.memset(M["gates"][:, :, :], 0.0)
            nc.vector.memset(M["stat"][:, :], 1.0)


def row_sums(act, scratch, stat, src, summed, rooted, scaled):
    for i, rows in enumerate(TILE_ROWS):
        act.activation(scratch[0:rows, :], src[0:rows, i, :], ACT.Square,
                       accum_out=stat[0:rows, i:i + 1]).then_inc(summed, 1)
        act.wait_ge(summed, i + 1)
    act.wait_ge(scaled, 1)
    act.activation(stat[:, 8:8 + NT], stat[:, 4:4 + NT], ACT.Sqrt).then_inc(rooted, 1)


def pool_mixer(nc, I, O, M):
    A, H, XT, ps = M["A"], M["H"], M["XT"], M["ps"]
    gain = A[:, 0:D]
    pscale = A[:, D:2 * D]
    XN = A[:, 2 * D:5 * D].rearrange("p (i n) -> p i n", i=NT)
    SP = A[:, 5 * D:6 * D]
    PM = A[:, 6 * D:6 * D + NPOOL * NPM].rearrange("p (g n) -> p g n", g=NPOOL)
    at = 6 * D + NPOOL * NPM
    PW = A[:, at:at + NPOOL * 2 * GD].rearrange("p (g k n) -> p g k n", g=NPOOL, k=2)
    at += NPOOL * 2 * GD
    scratch = A[:, at:at + D]
    prod = A[:, at + D:at + 2 * D]
    stat = M["stat"]
    S = STATE * NSEQ
    with ExitStack() as ctx:
        sem = lambda n: ctx.enter_context(nc.semaphore(n))
        rows_in, mats_in = sem("pool_rows_landed"), sem("pool_mats_landed")
        summed, scaled, rooted = sem("pool_summed"), sem("pool_scaled"), sem("pool_rooted")
        chain, xn_ready = sem("pool_chain"), sem("pool_xn_ready")
        mixed, mix_copied = sem("pool_mixed"), sem("pool_mix_copied")
        projected, added, stored = sem("pool_projected"), sem("pool_added"), sem("pool_stored")
        block = ctx.enter_context(nc.Block())

        @block.sync
        def _(sp):
            sp.dma_start(gain, I["norm_mix"][0:1, :].broadcast_to([P, D])).then_inc(rows_in, 16)
            sp.dma_start(pscale, I["pool_scale"][0:1, :].broadcast_to([P, D])).then_inc(rows_in, 16)
            sp.dma_start(SP[0:S, :], I["state_pool"][0].rearrange("b r d -> (b r) d")).then_inc(mats_in, 16)
            sp.dma_start(PM, I["pool_mats"]).then_inc(mats_in, 16)
            sp.dma_start(PW, I["pool_w"][0].rearrange("g (k p) n -> p g k n", p=P)).then_inc(mats_in, 16)
            sp.dma_start(O["new_pool_sample"][0, :, 0:STATE - STEPS, :],
                         I["state_pool"][0, :, STEPS:STATE, :]).then_inc(stored, 16)
            sp.wait_ge(xn_ready, NT)
            sp.dma_start(O["new_pool_prompt"][0, 0], XN[P - STATE:P, 1, :]).then_inc(stored, 16)
            for b in range(NSEQ):
                sp.dma_start(O["new_pool_sample"][0, b, STATE - STEPS:STATE, :],
                             XN[b * STEPS:(b + 1) * STEPS, 2, :]).then_inc(stored, 16)
            sp.wait_ge(stored, 16 * (2 + NSEQ))

        @block.scalar
        def _(act):
            row_sums(act, scratch, stat, H, summed, rooted, scaled)
            for c in range(KD):
                act.wait_ge(mixed, c + 1)
                nc.scalar.copy(XT[:, c, :], ps[c % 2][:, 0:TOK]).then_inc(mix_copied, 1)

        @block.vector
        def _(dve):
            st = Steps(dve, chain)
            row_rstd(nc, dve, st, stat, summed, scaled, rooted, D)
            dve.wait_ge(rows_in, 32)
            for i, rows in enumerate(TILE_ROWS):
                nc.vector.scalar_tensor_tensor(XN[0:rows, i, :], H[0:rows, i, :], stat[0:rows, 12 + i:13 + i],
                                               gain[0:rows, :], ALU.mult, ALU.mult).then_inc(xn_ready, 1)
            for i, rows in enumerate(TILE_ROWS):
                for half in range(2):
                    dve.wait_ge(projected, 2 * i + half + 1)
                    cols = slice(half * 512, half * 512 + 512)
                    st.add(nc.vector.tensor_tensor(prod[0:rows, cols], ps[2 + (2 * i + half) % 4][0:rows, :],
                                                   pscale[0:rows, cols], ALU.mult))
                    nc.vector.tensor_tensor(H[0:rows, i, cols], H[0:rows, i, cols], prod[0:rows, cols],
                                            ALU.add).then_inc(added, 1)
            dve.wait_ge(added, 2 * NT)

        @block.tensor
        def _(pe):
            pe.wait_ge(mats_in, 48)
            pe.wait_ge(xn_ready, NT)
            for c in range(KD):
                if c >= 2:
                    pe.wait_ge(mix_copied, c - 1)
                cs, g, bank = slice(c * P, c * P + P), c * P // GD, ps[c % 2]
                pe.matmul(bank[:, 0:SEQ], XN[:, 0, cs], PM[:, g, 0:SEQ], start=True, stop=False)
                pe.matmul(bank[:, 0:SEQ], XN[:, 1, cs], PM[:, g, SEQ:2 * SEQ], start=False, stop=True)
                pe.matmul(bank[:, SEQ:TOK], SP[0:S, cs], PM[0:S, g, 2 * SEQ:2 * SEQ + NEWTOK],
                          start=True, stop=False)
                pe.matmul(bank[:, SEQ:TOK], XN[0:NEWTOK, 2, cs], PM[0:NEWTOK, g, 2 * SEQ + NEWTOK:NPM],
                          start=False, stop=True).then_inc(mixed, 1)
            pe.wait_ge(mix_copied, KD)
            for i, rows in enumerate(TILE_ROWS):
                for half in range(2):
                    n = 2 * i + half
                    if n >= 4:
                        pe.wait_ge(added, n - 3)
                    for g in (2 * half, 2 * half + 1):
                        for k in range(2):
                            last = pe.matmul(ps[2 + n % 4][0:rows, (g % 2) * GD:(g % 2 + 1) * GD],
                                             XT[:, 2 * g + k, i * P:i * P + rows], PW[:, g, k, :],
                                             start=(k == 0), stop=(k == 1))
                    last.then_inc(projected, 1)


def row_rstd(nc, dve, st, stat, summed, scaled, rooted, width):
    dve.wait_ge(summed, NT)
    nc.vector.tensor_scalar(stat[:, 4:4 + NT], stat[:, 0:NT], 1.0 / width, EPS, ALU.mult, ALU.add)\
        .then_inc(scaled, 1)
    dve.wait_ge(rooted, 1)
    st.add(nc.vector.reciprocal(stat[:, 12:12 + NT], stat[:, 8:8 + NT]))


def norm_transpose(nc, M, tag, targets):
    H, ps, stat, gT = M["H"], M["ps"], M["stat"], M["gT"]
    Z = M["A"][:, 31248:31248 + NT * D].rearrange("p (i n) -> p i n", i=NT)
    scratch = M["A"][:, 31248 + NT * D:31248 + (NT + 1) * D]
    ident = const(M, "ident")
    with ExitStack() as ctx:
        sem = lambda n: ctx.enter_context(nc.semaphore(tag + n))
        summed, scaled, rooted, chain = sem("_summed"), sem("_scaled"), sem("_rooted"), sem("_chain")
        z_ready, turned, copied = sem("_z_ready"), sem("_turned"), sem("_copied")
        block = ctx.enter_context(nc.Block())

        @block.scalar
        def _(act):
            row_sums(act, scratch, stat, H, summed, rooted, scaled)

        @block.vector
        def _(dve):
            st = Steps(dve, chain)
            row_rstd(nc, dve, st, stat, summed, scaled, rooted, D)
            for i, rows in enumerate(TILE_ROWS):
                nc.vector.tensor_scalar(Z[0:rows, i, :], H[0:rows, i, :], stat[0:rows, 12 + i:13 + i], None,
                                        ALU.mult).then_inc(z_ready, 1)
            n = 0
            for i, rows in enumerate(TILE_ROWS):
                for half in range(2):
                    dve.wait_ge(turned, n + 1)
                    for gi, T in targets:
                        last = nc.vector.tensor_tensor(
                            T[:, 4 * half:4 * half + 4, i * P:i * P + rows],
                            ps[n % 4][:, 0:4 * rows].rearrange("p (k t) -> p k t", k=4),
                            gT[:, gi, 4 * half:4 * half + 4].unsqueeze(2).broadcast_to([P, 4, rows]), ALU.mult)
                    last.then_inc(copied, 1)
                    n += 1
            dve.wait_ge(copied, n)

        @block.tensor
        def _(pe):
            n = 0
            for i, rows in enumerate(TILE_ROWS):
                pe.wait_ge(z_ready, i + 1)
                for half in range(2):
                    if n >= 4:
                        pe.wait_ge(copied, n - 3)
                    for k in range(4):
                        c = 4 * half + k
                        last = pe.transpose(ps[n % 4][:, k * rows:(k + 1) * rows],
                                            Z[0:rows, i, c * P:(c + 1) * P], ident[0:rows, 0:rows])
                    last.then_inc(turned, 1)
                    n += 1


def route(nc, I, M, layer):
    XT, A, ps, comb = M["XT"], M["A"], M["ps"], M["comb"]
    at = [0]

    def take(n, k=1):
        v = A[:, at[0]:at[0] + NT * n * k]
        at[0] += NT * n * k
        return v.rearrange("p (i n) -> p i n", i=NT)

    WR = A[:, 4096:4096 + KD * 20].rearrange("p (k n) -> p k n", k=KD)
    L = take(NG + NE)
    gbest, ghot, gkey, gkmax, gexp, gsum, gval = (take(1), take(NG), take(NG), take(1), take(NG), take(1), take(1))
    le, prod = take(EPG), take(NE)
    m1, m2, hot1, hot2, key, kmax, le2 = take(1), take(1), take(EPG), take(EPG), take(EPG), take(1), take(EPG)
    diff, ratio, den, w1, w2, share = take(1), take(1), take(1), take(1), take(1), take(EPG)
    first = const(M, "first")

    def wide(x, n):
        return x.broadcast_to([P, NT, n])

    with ExitStack() as ctx:
        sem = lambda n: ctx.enter_context(nc.semaphore(f"route{layer}_{n}"))
        w_in, logits, chain = sem("weights_landed"), sem("logits_ready"), sem("chain")
        exp_in, exp_out = sem("exp_asked"), sem("exp_done")
        block = ctx.enter_context(nc.Block())

        @block.sync
        def _(sp):
            sp.dma_start(WR[:, :, 0:NG], I["router_group"][layer].rearrange("(k p) n -> p k n", p=P)).then_inc(w_in, 16)
            sp.dma_start(WR[:, :, NG:], I["router_expert"][layer].rearrange("(k p) n -> p k n", p=P)).then_inc(w_in, 16)

        @block.tensor
        def _(pe):
            pe.wait_ge(w_in, 32)
            for i, rows in enumerate(TILE_ROWS):
                for k in range(KD):
                    last = pe.matmul(ps[0][0:rows, 32 * i:32 * i + NG + NE], XT[:, k, i * P:i * P + rows], WR[:, k, :],
                                     start=(k == 0), stop=(k == KD - 1))
            last.then_inc(logits, 1)

        @block.scalar
        def _(act):
            act.wait_ge(exp_in, 1)
            act.activation(gexp, gkey, ACT.Exp).then_inc(exp_out, 1)
            act.wait_ge(exp_in, 2)
            act.activation(ratio, diff, ACT.Exp).then_inc(exp_out, 1)

        @block.vector
        def _(dve):
            st = Steps(dve, chain)
            V = nc.vector
            st.add(V.memset(L, 0.0))
            dve.wait_ge(logits, 1)
            for i, rows in enumerate(TILE_ROWS):
                st.add(V.tensor_copy(L[0:rows, i, :], ps[0][0:rows, 32 * i:32 * i + NG + NE]))
            lg = L[:, :, 0:NG]

            def hot_of(out, src, best, keyt, kmaxt, n):
                st.add(V.tensor_reduce(best, src, AX.X, ALU.max))
                st.add(V.tensor_tensor(keyt, src, wide(best, n), ALU.is_equal))
                st.add(V.tensor_tensor(keyt, keyt, first.unsqueeze(1).broadcast_to([P, NT, n]), ALU.mult))
                st.add(V.tensor_reduce(kmaxt, keyt, AX.X, ALU.max))
                st.add(V.tensor_tensor(out, wide(kmaxt, n), first.unsqueeze(1).broadcast_to([P, NT, n]), ALU.is_equal))

            hot_of(ghot, lg, gbest, gkey, gkmax, NG)
            V.tensor_tensor(gkey, lg, wide(gbest, NG), ALU.subtract).then_inc(exp_in, 1)
            dve.wait_ge(exp_out, 1)
            st.add(V.tensor_reduce(gsum, gexp, AX.X, ALU.add))
            st.add(V.reciprocal(gval, gsum))
            st.add(V.tensor_tensor(prod.rearrange("p i (g e) -> p i g e", g=NG),
                                   L[:, :, NG:].rearrange("p i (g e) -> p i g e", g=NG),
                                   ghot.unsqueeze(3).broadcast_to([P, NT, NG, EPG]), ALU.mult))
            st.add(V.tensor_reduce(le, prod.rearrange("p i (g e) -> p i e g", g=NG), AX.X, ALU.add))
            hot_of(hot1, le, m1, key, kmax, EPG)
            st.add(V.tensor_scalar(le2, hot1, NEG, None, ALU.mult))
            st.add(V.tensor_tensor(le2, le2, le, ALU.add))
            hot_of(hot2, le2, m2, key, kmax, EPG)
            V.tensor_tensor(diff, m2, m1, ALU.subtract).then_inc(exp_in, 1)
            dve.wait_ge(exp_out, 2)
            st.add(V.tensor_scalar(den, ratio, 1.0, None, ALU.add))
            st.add(V.reciprocal(den, den))
            st.add(V.tensor_tensor(w1, den, gval, ALU.mult))
            st.add(V.tensor_tensor(w2, w1, ratio, ALU.mult))
            st.add(V.tensor_tensor(share, hot1, wide(w1, EPG), ALU.mult))
            st.add(V.tensor_tensor(hot2, hot2, wide(w2, EPG), ALU.mult))
            st.add(V.tensor_tensor(share, share, hot2, ALU.add))
            st.add(V.tensor_tensor(comb[:, :, :].rearrange("p i (g e) -> p i g e", g=NG),
                                   ghot.unsqueeze(3).broadcast_to([P, NT, NG, EPG]),
                                   share.unsqueeze(2).broadcast_to([P, NT, NG, EPG]), ALU.mult))


def moe(nc, I, M, layer):
    H, XT, A, ps, comb = M["H"], M["XT"], M["A"], M["ps"], M["comb"]
    NF = FE // P
    GU, DN = KD * 2 * FE, NF * D
    gu = [A[:, s * (GU + DN):s * (GU + DN) + GU].rearrange("p (k n) -> p k n", k=KD) for s in range(2)]
    dn = [A[:, s * (GU + DN) + GU:(s + 1) * (GU + DN)].rearrange("p (k n) -> p k n", k=NF) for s in range(2)]
    at = 2 * (GU + DN)
    hdn = [A[:, at + s * NF * TOK:at + (s + 1) * NF * TOK].rearrange("p (f t) -> p f t", f=NF) for s in range(2)]
    at += 2 * NF * TOK
    sil = [A[:, at + s * TOK:at + (s + 1) * TOK] for s in range(2)]
    with ExitStack() as ctx:
        sem = lambda n: ctx.enter_context(nc.semaphore(f"moe{layer}_{n}"))
        gu_in = [sem(f"gate_up_landed{s}") for s in range(2)]
        dn_in = [sem(f"down_landed{s}") for s in range(2)]
        pair, silu, hid = sem("gate_up_ready"), sem("silu_ready"), sem("hidden_ready")
        y_ready, y_added = sem("y_ready"), sem("y_added")
        block = ctx.enter_context(nc.Block())
        NY = 2 * NT

        @block.sync
        def _(sp):
            def load(e, s, ahead):
                if ahead is not None:
                    sp.wait_ge(pair, ahead * NF)
                sp.dma_start(gu[s], I["w_gate_up"][layer][bass.ds(e, 1)].rearrange("a (k p) n -> p (a k) n", p=P))\
                    .then_inc(gu_in[s], 16)
                if ahead is not None:
                    sp.wait_ge(y_ready, ahead * NY)
                sp.dma_start(dn[s], I["w_down"][layer][bass.ds(e, 1)].rearrange("a (k p) n -> p (a k) n", p=P))\
                    .then_inc(dn_in[s], 16)
            load(0, 0, None)
            load(1, 1, None)
            with sp.Fori(1, NE // 2) as i:
                for s in range(2):
                    load(i * 2 + s, s, i * 2 + (s - 1))

        @block.tensor
        def _(pe):
            def expert(i, s, peeled):
                e = i * 2 + s
                pe.wait_ge(gu_in[s], i * 16 + 16)
                for f in range(NF):
                    n = e * NF + f
                    if not peeled or s * NF + f >= 2:
                        pe.wait_ge(hid, n - 1)
                    for u in range(2):
                        bank = ps[2 * (f % 2) + u]
                        for k in range(KD):
                            last = pe.matmul(bank[:, 0:TOK], gu[s][:, k, u * FE + f * P:u * FE + (f + 1) * P],
                                             XT[:, k, :], start=(k == 0), stop=(k == KD - 1))
                    last.then_inc(pair, 1)
                pe.wait_ge(dn_in[s], i * 16 + 16)
                pe.wait_ge(hid, e * NF + NF)
                for t, rows in enumerate(TILE_ROWS):
                    for half in range(2):
                        m = t * 2 + half
                        if not peeled or s * NY + m >= 4:
                            pe.wait_ge(y_added, e * NY + (m - 3))
                        for f in range(NF):
                            last = pe.matmul(ps[4 + (s * NY + m) % 4][0:rows, :], hdn[s][:, f, t * P:t * P + rows],
                                             dn[s][:, f, half * 512:(half + 1) * 512],
                                             start=(f == 0), stop=(f == NF - 1))
                        last.then_inc(y_ready, 1)
            expert(0, 0, True)
            expert(0, 1, True)
            with pe.Fori(1, NE // 2) as i:
                for s in range(2):
                    expert(i, s, False)

        @block.scalar
        def _(act):
            def expert(i, s, peeled):
                for f in range(NF):
                    n = (i * 2 + s) * NF + f
                    act.wait_ge(pair, n + 1)
                    if not peeled or s * NF + f >= 2:
                        act.wait_ge(hid, n - 1)
                    act.activation(sil[f % 2], ps[2 * (f % 2)][:, 0:TOK], ACT.Silu).then_inc(silu, 1)
            expert(0, 0, True)
            expert(0, 1, True)
            with act.Fori(1, NE // 2) as i:
                for s in range(2):
                    expert(i, s, False)

        @block.vector
        def _(dve):
            def expert(i, s, peeled):
                e = i * 2 + s
                for f in range(NF):
                    n = e * NF + f
                    dve.wait_ge(silu, n + 1)
                    if not peeled and f == 0:
                        dve.wait_ge(y_ready, e * NY - NY)
                    nc.vector.tensor_tensor(hdn[s][:, f, :], ps[2 * (f % 2) + 1][:, 0:TOK], sil[f % 2],
                                            ALU.mult).then_inc(hid, 1)
                for t, rows in enumerate(TILE_ROWS):
                    for half in range(2):
                        m = t * 2 + half
                        dve.wait_ge(y_ready, e * NY + (m + 1))
                        if not (peeled and s == 0):
                            dve.wait_ge(y_added, e * NY + (m + 1 - NY))
                        hv = H[0:rows, t, half * 512:(half + 1) * 512]
                        c = comb[0:rows, t, bass.ds(e, 1)]
                        nc.vector.scalar_tensor_tensor(hv, ps[4 + (s * NY + m) % 4][0:rows, :], c, hv,
                                                       ALU.mult, ALU.add).then_inc(y_added, 1)
            expert(0, 0, True)
            expert(0, 1, True)
            with dve.Fori(1, NE // 2) as i:
                for s in range(2):
                    expert(i, s, False)
            dve.wait_ge(y_added, NE * NY)


def store_result(nc, O, M):
    with ExitStack() as ctx:
        stored = ctx.enter_context(nc.semaphore("y_stored"))
        block = ctx.enter_context(nc.Block())

        @block.sync
        def _(sp):
            for i, rows in enumerate(TILE_ROWS):
                dst = O["y_prompt"][0, i * P:(i + 1) * P, :] if i < 2 else O["y_sample"].rearrange("b t d -> (b t) d")
                sp.dma_start(dst, M["H"][0:rows, i, :]).then_inc(stored, 16)
            sp.wait_ge(stored, 16 * NT)


def view(M, at, *dims):
    n = 1
    for d in dims:
        n *= d
    names = "abcd"[:len(dims)]
    v = M["A"][:, at:at + n]
    if len(dims) == 1:
        return v
    return v.rearrange(f"p ({' '.join(names)}) -> p {' '.join(names)}", **dict(zip(names, dims)))


def stage_attention(nc, I, O, M):
    norm_transpose(nc, M, "mix1", [(2, M["XT"]), (3, view(M, Map.XT2, KD, TOK))])
    project(nc, I, O, M)
    turn_heads(nc, I, M)
    compress_prompt(nc, I, O, M)
    compress_samples(nc, I, M)
    attend_samples(nc, I, M)
    attend_prompt(nc, I, M)
    output_projection(nc, M)


def project(nc, I, O, M):
    XT, XT2, ps, stat = M["XT"], view(M, Map.XT2, KD, TOK), M["ps"], M["stat"]
    WKV, WQG = view(M, Map.WKV, KD, 6 * NKV * HD), view(M, Map.WQG, KD, NH * HD + 3 * NH)
    HEADS = view(M, Map.HEADS, NT, 24, HD)
    KV, WN = view(M, Map.KVROWS, NT, 4 * NKV * HD), view(M, Map.WINROWS, NT, 2 * NKV * HD)
    QR = view(M, Map.QROPE, NT, NH, HD)
    GAIN, SQ = view(M, Map.GAIN24, 24, HD), view(M, Map.SQ, 24, HD)
    t1, t2 = view(M, Map.ROT, 24, HD // 2), view(M, Map.ROT + 24 * HD // 2, 24, HD // 2)
    gates = M["gates"]
    cos = const(M, "cos").rearrange("p (i d) -> p i d", i=NT)
    sin = const(M, "sin").rearrange("p (i d) -> p i d", i=NT)
    KW = NKV * HD
    chunks = [(XT2, WKV, 0, 512), (XT2, WKV, 512, 512), (XT2, WKV, 1024, 512),
              (XT, WQG, 0, 512), (XT, WQG, 512, 512), (XT, WQG, 1024, 3 * NH)]
    NC = len(chunks)
    with ExitStack() as ctx:
        sem = lambda n: ctx.enter_context(nc.semaphore("proj_" + n))
        kv_in, q_in, gains_in = sem("kv_weights_landed"), sem("q_weights_landed"), sem("gains_landed")
        product, copied, parts = sem("product_ready"), sem("product_copied"), sem("part_copied")
        squared, scaled, rooted = sem("squares_ready"), sem("mean_ready"), sem("root_ready")
        chain, roped, stored = sem("chain"), sem("rows_roped"), sem("rows_stored")
        block = ctx.enter_context(nc.Block())

        @block.sync
        def _(sp):
            for h in range(2):
                ks = slice(4 * h, 4 * h + 4)
                sp.dma_start(WKV[:, ks, :], I["w_kv"].rearrange("(k p) n -> p k n", p=P)[:, ks, :]).then_inc(kv_in, 16)
            sp.dma_start(WQG, I["w_qg"][0].rearrange("(k p) n -> p k n", p=P)).then_inc(q_in, 16)
            for lo, hi, src in ((0, 4, I["k_norm"][1:2, :]), (4, 8, I["k_norm"][2:3, :]), (8, 24, I["q_norm"][0:1, :])):
                sp.dma_start(GAIN[:, lo:hi, :], src.unsqueeze(1).broadcast_to([1, hi - lo, HD])
                             .broadcast_to([P, hi - lo, HD])).then_inc(gains_in, 16)
            sp.dma_start(O["new_win_sample"][:, 0:WIN - STEPS], I["state_win"][:, STEPS:WIN]).then_inc(stored, 16)
            for i in range(NT):
                sp.wait_ge(roped, i + 1)
                if i < 2:
                    sp.dma_start(O["new_kv_prompt"][0, i * P:(i + 1) * P].rearrange("t s g d -> t (s g d)"),
                                 KV[:, i, :]).then_inc(stored, 16)
                    sp.dma_start(O["new_win_prompt"][0, i * P:(i + 1) * P].rearrange("t s g d -> t (s g d)"),
                                 WN[:, i, :]).then_inc(stored, 16)
                else:
                    sp.dma_start(O["new_kv_sample"].rearrange("b t s g d -> (b t) (s g d)"),
                                 KV[0:NEWTOK, i, :]).then_inc(stored, 16)
                    for b in range(NSEQ):
                        sp.dma_start(O["new_win_sample"][b, WIN - STEPS:WIN].rearrange("t s g d -> t (s g d)"),
                                     WN[b * STEPS:(b + 1) * STEPS, i, :]).then_inc(stored, 16)
            sp.wait_ge(stored, 16 * (6 + NSEQ))

        @block.tensor
        def _(pe):
            n = 0
            for i, rows in enumerate(TILE_ROWS):
                for c, (T, W, at, w) in enumerate(chunks):
                    if i == 0 and c == 0:
                        pe.wait_ge(kv_in, 32)
                    if i == 0 and c == 3:
                        pe.wait_ge(q_in, 16)
                    if n >= 8:
                        pe.wait_ge(copied, n - 7)
                    for k in range(KD):
                        last = pe.matmul(ps[n % 8][0:rows, 0:w], T[:, k, i * P:i * P + rows], W[:, k, at:at + w],
                                         start=(k == 0), stop=(k == KD - 1))
                    last.then_inc(product, 1)
                    n += 1

        @block.scalar
        def _(act):
            for i, rows in enumerate(TILE_ROWS):
                flat = HEADS[0:rows, i].rearrange("p h d -> p (h d)")
                dests = [[(KV[0:rows, i, 0:512], 0)],
                         [(flat[:, 0:KW], 0), (KV[0:rows, i, 3 * KW:4 * KW], KW)],
                         [(flat[:, KW:2 * KW], 0), (WN[0:rows, i, KW:2 * KW], KW)],
                         [(HEADS[0:rows, i, 8:16].rearrange("p (h g) d -> p g h d", g=2), 0)],
                         [(HEADS[0:rows, i, 16:24].rearrange("p (h g) d -> p g h d", g=2), 0)],
                         [(gates[0:rows, i, :], 0)]]
                for c in range(NC):
                    n = i * NC + c
                    act.wait_ge(product, n + 1)
                    for m, (dst, at) in enumerate(dests[c]):
                        if len(dst.shape) == 4:
                            src = ps[n % 8][0:rows, :].rearrange("p (g h d) -> p g h d", g=2, h=HPG)
                        else:
                            src = ps[n % 8][0:rows, at:at + dst.shape[1]]
                        ins = nc.scalar.copy(dst, src)
                        ins.then_inc(copied if m == len(dests[c]) - 1 else parts, 1)
                act.wait_ge(copied, (i + 1) * NC)
                act.wait_ge(parts, 2 * (i + 1))
                if i:
                    act.wait_ge(scaled, i)
                act.activation(SQ[0:rows].rearrange("p h d -> p (h d)"), flat, ACT.Square).then_inc(squared, 1)
                act.wait_ge(scaled, i + 1)
                act.activation(stat[0:rows, 16:40], stat[0:rows, 40:64], ACT.Sqrt).then_inc(rooted, 1)
            act.activation(gates[:, :, :], gates[:, :, :], ACT.Sigmoid).then_inc(parts, 1)

        @block.vector
        def _(dve):
            V = nc.vector
            st = Steps(dve, chain)
            dve.wait_ge(gains_in, 48)
            for i, rows in enumerate(TILE_ROWS):
                r = slice(0, rows)
                dve.wait_ge(squared, i + 1)
                st.add(V.tensor_reduce(stat[r, 16:40], SQ[r], AX.X, ALU.add))
                V.tensor_scalar(stat[r, 40:64], stat[r, 16:40], 1.0 / HD, EPS, ALU.mult, ALU.add).then_inc(scaled, 1)
                dve.wait_ge(rooted, i + 1)
                st.add(V.reciprocal(stat[r, 40:64], stat[r, 16:40]))
                x = HEADS[r, i]
                st.add(V.tensor_tensor(x, x, stat[r, 40:64].unsqueeze(2).broadcast_to([rows, 24, HD]), ALU.mult))
                st.add(V.tensor_tensor(x, x, GAIN[r], ALU.mult))
                x1, x2 = x[:, :, 0:HD // 2], x[:, :, HD // 2:HD]
                c = cos[r, i].unsqueeze(1).broadcast_to([rows, 24, HD // 2])
                s = sin[r, i].unsqueeze(1).broadcast_to([rows, 24, HD // 2])
                dst = [(0, 4, KV[r, i, 2 * KW:3 * KW].rearrange("p (g d) -> p g d", g=NKV)),
                       (4, 8, WN[r, i, 0:KW].rearrange("p (g d) -> p g d", g=NKV)), (8, 24, QR[r, i])]
                for lo, first, second, op in ((0, x1, x2, ALU.subtract), (HD // 2, x2, x1, ALU.add)):
                    st.add(V.tensor_tensor(t1[r], first, c, ALU.mult))
                    st.add(V.tensor_tensor(t2[r], second, s, ALU.mult))
                    for m, (a, b, d) in enumerate(dst):
                        ins = V.tensor_tensor(d[:, :, lo:lo + HD // 2], t1[r, a:b], t2[r, a:b], op)
                        if lo and m == 2:
                            ins.then_inc(roped, 1)
                            dve.wait_ge(roped, i + 1)
                        else:
                            st.add(ins)


def turn_heads(nc, I, M):
    ps, gates = M["ps"], M["gates"]
    HEADS, QR = view(M, Map.HEADS, NT, 24, HD), view(M, Map.QROPE, NT, NH, HD)
    KV, WN = view(M, Map.KVROWS, NT, 4, NKV * HD), view(M, Map.WINROWS, NT, 2, NKV * HD)
    QT = [view(M, Map.QNT, 2, HPG, SEQ), view(M, Map.QRT, 2, HPG, SEQ)]
    QS = [view(M, Map.QSN, 2, HPG, NEWTOK), view(M, Map.QSR, 2, HPG, NEWTOK)]
    KTP, KTN = view(M, Map.KTP, 4, SEQ), view(M, Map.KTN, 4, NEWTOK)
    VP, VNEW = view(M, Map.VP, 2, 2, NKV, 3 * HD), view(M, Map.VNEW, NKV * HD)
    GS, GL = view(M, Map.GS, 3, NSEQ), view(M, Map.GATEL, 3, NH, STEPS)
    ident, stepsel, seqsel = const(M, "ident"), const(M, "stepsel", NEWTOK), const(M, "seqsel", NEWTOK)

    def query_pair(which, i, j, h):
        rows = TILE_ROWS[i]
        src, at = ((HEADS, 8), (QR, 0))[which]
        a = at + 2 * HPG * j + 2 * h
        return src[0:rows, i, a:a + 2, :].rearrange("p g d -> p (g d)")

    def key_pair(br, i, j):
        rows = TILE_ROWS[i]
        src = KV[0:rows, i, 2] if br == 0 else WN[0:rows, i, 0]
        return src[:, j * P:(j + 1) * P]

    batches = []
    for i in range(2):
        for which in range(2):
            for j in range(2):
                batches.append(([query_pair(which, i, j, h) for h in range(HPG)], P,
                                QT[which][:, j, :, i * P:(i + 1) * P]))
        batches.append(([key_pair(br, i, j) for br in range(2) for j in range(2)], P, KTP[:, :, i * P:(i + 1) * P]))
    for which in range(2):
        for j in range(2):
            batches.append(([query_pair(which, 2, j, h) for h in range(HPG)], NEWTOK, QS[which][:, j]))
    batches.append(([key_pair(br, 2, j) for br in range(2) for j in range(2)], NEWTOK, KTN))
    NB = len(batches)
    with ExitStack() as ctx:
        sem = lambda n: ctx.enter_context(nc.semaphore("turn_" + n))
        turned, by_dve, by_act = sem("batch_turned"), sem("copied_by_dve"), sem("copied_by_act")
        zeroed, gl, gsum = sem("zeroed"), sem("gate_rows_spread"), sem("gates_summed")
        block = ctx.enter_context(nc.Block())

        @block.tensor
        def _(pe):
            for n, (srcs, w, dst) in enumerate(batches):
                if n >= 6:
                    pe.wait_ge(by_act if n % 2 else by_dve, (n - 6) // 2 + 1)
                for m, src in enumerate(srcs):
                    last = pe.transpose(ps[n % 6][:, m * w:(m + 1) * w], src, ident[0:w, 0:w])
                last.then_inc(turned, 1)
            pe.wait_ge(gl, 3)
            for br in range(3):
                last = pe.matmul(ps[6][:, br * NSEQ:(br + 1) * NSEQ], GL[0:NEWTOK, br].rearrange("p h t -> p (h t)"),
                                 seqsel, start=True, stop=True)
            last.then_inc(gsum, 1)

        def copy(n, on_act):
            srcs, w, dst = batches[n]
            src = ps[n % 6][:, 0:4 * w].rearrange("p (m t) -> p m t", m=4)
            return nc.scalar.copy(dst, src) if on_act else nc.vector.tensor_copy(dst, src)

        @block.scalar
        def _(act):
            for n in range(1, NB, 2):
                act.wait_ge(turned, n + 1)
                copy(n, True).then_inc(by_act, 1)

        @block.vector
        def _(dve):
            for br in range(3):
                nc.vector.tensor_tensor(GL[0:NEWTOK, br], gates[0:NEWTOK, 2, br * NH:(br + 1) * NH].unsqueeze(2)
                                        .broadcast_to([NEWTOK, NH, STEPS]),
                                        stepsel.unsqueeze(1).broadcast_to([NEWTOK, NH, STEPS]), ALU.mult)\
                    .then_inc(gl, 1)
            for n in range(0, NB, 2):
                dve.wait_ge(turned, n + 1)
                copy(n, False).then_inc(by_dve, 1)
            dve.wait_ge(gsum, 1)
            nc.vector.tensor_copy(GS, ps[6][:, 0:3 * NSEQ].rearrange("p (a b) -> p a b", a=3))
            nc.vector.tensor_copy(VNEW[0:NEWTOK], KV[0:NEWTOK, 2, 3])
            nc.vector.tensor_copy(VNEW[NEWTOK:P], WN[0:NEWTOK, 2, 1])

        @block.gpsimd
        def _(pool):
            nc.gpsimd.memset(view(M, Map.QB, 512), 0.0)
            nc.gpsimd.memset(view(M, Map.W2, 2 * 3 * HD), 0.0)
            nc.gpsimd.memset(view(M, Map.ONES, 260), 1.0)
            nc.gpsimd.memset(view(M, Map.CVP, NKV * 3 * HD), 0.0)
            nc.gpsimd.memset(view(M, Map.VP, 2 * 2 * NKV * 3 * HD), 0.0).then_inc(zeroed, 1)
            pool.wait_ge(zeroed, 1)
            for i in range(2):
                nc.gpsimd.tensor_copy(VP[:, i, 0, :, HD:2 * HD], KV[:, i, 3].rearrange("p (g d) -> p g d", g=NKV))
                nc.gpsimd.tensor_copy(VP[:, i, 1, :, HD:2 * HD], WN[:, i, 1].rearrange("p (g d) -> p g d", g=NKV))


def compress_prompt(nc, I, O, M):
    ps, stat = M["ps"], M["stat"]
    W1, W2 = view(M, Map.W1, 2, 2, 8, HID), view(M, Map.W2, 2, 3 * HD)
    PEC, BIAS, ONES = view(M, Map.PE, 2, 2, 8), view(M, Map.BIAS, 2, HID), view(M, Map.ONES, 260)
    CR = view(M, Map.CHUNKS, 2, 8 * NKV, 2, HD)
    RP = view(M, Map.RP, 2, 8, NKV, CHUNK)
    HIDP = view(M, Map.HIDB, 2, NKV, NCP)
    CKP, CVP = view(M, Map.CKP, 2, CHUNK), view(M, Map.CVP, NKV, 3 * HD)
    SQ, RS = view(M, Map.CKB, 2, NCP), view(M, Map.CKB + 64, 2, NCP)
    B1 = view(M, Map.CKB + 128, 2, HID)
    KG = M["kgain"]
    ident, blockones = const(M, "ident"), const(M, "blockones")
    NCH = NCP + 1
    with ExitStack() as ctx:
        sem = lambda n: ctx.enter_context(nc.semaphore("cmpp_" + n))
        w_in, rows_in, small_in = sem("weights_landed"), sem("rows_landed"), sem("small_landed")
        turned, copied, biased = sem("rows_turned"), sem("rows_copied"), sem("bias_ready")
        product, gelu, ck, sq, ss = sem("hidden_ready"), sem("gelu_ready"), sem("ck_ready"), sem("ck_squared"), sem("ck_summed")
        cv, mean, root, chain, bias_mm = sem("cv_ready"), sem("mean_ready"), sem("root_ready"), sem("chain"), sem("bias_summed")
        block = ctx.enter_context(nc.Block())

        @block.sync
        def _(sp):
            src = O["new_kv_prompt"][0].rearrange("(c i r) k g d -> k r c i g d", r=2, i=CHUNK // 2)
            for kind in range(2):
                for r in range(2):
                    sp.dma_start(CR[0:NCH, kind, :, r, :].rearrange("c (i g) d -> c i g d", g=NKV), src[kind, r])\
                        .then_inc(rows_in, 16)
            for kind in range(2):
                sp.dma_start(W1[:, kind], I["cmp_w1"][kind].rearrange("(h i p) n -> p h i n", p=P, h=2)).then_inc(w_in, 16)
            sp.dma_start(W2[:, :, HD:2 * HD], I["cmp_w2"].rearrange("k p n -> p k n")).then_inc(small_in, 16)
            sp.dma_start(PEC, I["cmp_pe"]).then_inc(small_in, 16)
            sp.dma_start(B1[0:1], I["cmp_b1"].unsqueeze(0)).then_inc(small_in, 16)
            sp.dma_start(KG[:, :], I["k_gainT"]).then_inc(small_in, 16)

        @block.tensor
        def _(pe):
            pe.wait_ge(rows_in, 64)
            for kind in range(2):
                for i in range(8):
                    for g in range(NKV):
                        last = pe.transpose(ps[kind][:, (i * NKV + g) * NCH:(i * NKV + g + 1) * NCH],
                                            CR[0:NCH, kind, i * NKV + g].rearrange("c r d -> c (r d)"),
                                            ident[0:NCH, 0:NCH])
                last.then_inc(turned, 1)
            pe.wait_ge(w_in, 32)
            pe.wait_ge(small_in, 64)
            for kind in range(2):
                for half in range(2):
                    for i in range(8):
                        last = pe.matmul(ps[2][0:1, kind * HID:(kind + 1) * HID], PEC[:, kind, half, i:i + 1],
                                         W1[:, kind, half, i, :], start=(half + i == 0), stop=(half + i == 8))
            last.then_inc(bias_mm, 1)
            pe.wait_ge(biased, 1)
            pe.wait_ge(copied, 2)
            for kind in range(2):
                bank = ps[3 + kind][:, 0:NKV * NCP].rearrange("p (g c) -> p g c", g=NKV)
                pe.matmul(ps[3 + kind][:, 0:NKV * NCP], BIAS[0:1, kind, :], ONES[0:1, 0:NKV * NCP], start=True, stop=False)
                for half in range(2):
                    for i in range(8):
                        last = pe.matmul(bank, W1[:, kind, half, i, :], RP[:, kind, i, :, half:half + NCP],
                                         start=False, stop=(half + i == 8))
                last.then_inc(product, 1)
            pe.wait_ge(gelu, 2)
            for j in range(2):
                out = ps[5][:, j * NCP:(j + 1) * NCP]
                pe.matmul(out, W2[:, 0, HD:3 * HD], HIDP[:, 0, 2 * j, :], start=True, stop=False)
                last = pe.matmul(out, W2[:, 0, 0:2 * HD], HIDP[:, 0, 2 * j + 1, :], start=False, stop=True)
            last.then_inc(ck, 1)
            for g in range(NKV):
                last = pe.matmul(ps[6][0:NCP, g * HD:(g + 1) * HD], HIDP[:, 1, g, :], W2[:, 1, HD:2 * HD],
                                 start=True, stop=True)
            last.then_inc(cv, 1)
            pe.wait_ge(sq, 1)
            pe.matmul(ps[7][:, 0:2 * NCP], blockones, SQ.rearrange("p j c -> p (j c)"), start=True, stop=True).then_inc(ss, 1)

        @block.scalar
        def _(act):
            for kind in range(2):
                act.wait_ge(product, kind + 1)
                act.activation(HIDP[:, kind].rearrange("p g c -> p (g c)"), ps[3 + kind][:, 0:NKV * NCP],
                               ACT.Gelu_apprx_tanh).then_inc(gelu, 1)
            act.wait_ge(ck, 1)
            act.activation(SQ.rearrange("p j c -> p (j c)"), ps[5][:, 0:2 * NCP], ACT.Square).then_inc(sq, 1)
            act.wait_ge(mean, 1)
            act.activation(RS, RS, ACT.Sqrt).then_inc(root, 1)

        @block.vector
        def _(dve):
            V = nc.vector
            st = Steps(dve, chain)
            for kind in range(2):
                dve.wait_ge(turned, kind + 1)
                V.tensor_copy(RP[:, kind].rearrange("p i g c -> p (i g c)"), ps[kind][:, :]).then_inc(copied, 1)
            dve.wait_ge(bias_mm, 1)
            dve.wait_ge(small_in, 64)
            V.tensor_tensor(BIAS[0:1].rearrange("p k n -> p (k n)"), ps[2][0:1, 0:2 * HID],
                            B1[0:1].rearrange("p k n -> p (k n)"), ALU.add).then_inc(biased, 1)
            dve.wait_ge(cv, 1)
            st.add(V.tensor_copy(CVP[0:NCP, :, HD:2 * HD], ps[6][0:NCP, 0:NKV * HD].rearrange("p (g d) -> p g d", g=NKV)))
            dve.wait_ge(ss, 1)
            V.tensor_scalar(RS, ps[7][:, 0:2 * NCP].rearrange("p (j c) -> p j c", j=2), 1.0 / HD, EPS, ALU.mult, ALU.add)\
                .then_inc(mean, 1)
            dve.wait_ge(root, 1)
            st.add(V.reciprocal(RS, RS))
            st.add(V.scalar_tensor_tensor(CKP[:, :, 0:NCP], ps[5][:, 0:2 * NCP].rearrange("p (j c) -> p j c", j=2),
                                          KG[:, 0:1], RS, ALU.mult, ALU.mult))


def queries_of(nc, QS, QB, b, s, done):
    for par in range(2):
        half = slice(par * HD, (par + 1) * HD)
        for j in range(2):
            at = (2 * j + par) * HPG * STEPS
            dst = QB[half, s, j, at:at + HPG * STEPS].rearrange("p (h t) -> p h t", h=HPG)
            nc.gpsimd.tensor_copy(dst, QS[half, j, :, bass.ds(b * STEPS, STEPS)]).then_inc(done, 1)


def compress_samples(nc, I, M):
    ps, stat = M["ps"], M["stat"]
    W1, W2 = view(M, Map.W1, 2, 2, 8, HID), view(M, Map.W2, 2, 3 * HD)
    BIAS, ONES, KG = view(M, Map.BIAS, 2, HID), view(M, Map.ONES, 260), M["kgain"]
    RAW = view(M, Map.PAGES, 2, NPAGE, 2, 256)
    HIDB = view(M, Map.HIDB, 2, 2, 256)
    NB = NCS + 1
    SQ = view(M, Map.CKB, 2, NB)
    RS = view(M, Map.CKB + 128, 2, NB)
    CKT = view(M, Map.CKB + 256, 2, NB)
    PR = view(M, Map.CKB + 384, NB)
    SCORE, KEY = view(M, Map.CKB + 448, NSB - 3), view(M, Map.CKB + 464, NSB - 3)
    CV, PC, BM = view(M, Map.CV, NSEQ, NKV * HD), view(M, Map.PC, NSEQ, NB), view(M, Map.BM, NSEQ, 16)
    GS = view(M, Map.GS, 3, NSEQ)
    QS, QB = view(M, Map.QSN, 2, HPG, NEWTOK), view(M, Map.QB, 2, 2, P)
    sm = view(M, Map.SMALL, 16)
    blockones, headsum, iota = const(M, "blockones"), const(M, "headsum"), const(M, "iota")
    NBLK = NPAGE * (PAGE // CHUNK) * NKV
    with ExitStack() as ctx:
        sem = lambda n: ctx.enter_context(nc.semaphore("cmps_" + n))
        raw_in = [sem(f"pages_landed{s}") for s in range(2)]
        hidden, gelu, ck, cv = sem("hidden_ready"), sem("gelu_ready"), sem("ck_ready"), sem("cv_ready")
        squared, ss, mean, root, ckt = sem("ck_squared"), sem("ck_summed"), sem("mean_ready"), sem("root_ready"), sem("ckT_ready")
        cv_out, qb, score, negmax = sem("cv_copied"), sem("queries_ready"), sem("scores_ready"), sem("negmax_ready")
        expd, prob, pooled, chain = sem("exp_ready"), sem("probs_ready"), sem("group_sums_ready"), sem("chain")
        chosen = sem("blocks_chosen")
        block = ctx.enter_context(nc.Block())
        DCH = 11

        def over_sequences(eng, body):
            for s in range(2):
                body(s, s, True, False)
            with eng.Fori(1, NSEQ // 2 - 1) as i:
                for s in range(2):
                    body(i * 2 + s, s, False, False)
            for s in range(2):
                body(NSEQ - 2 + s, s, False, s == 1)

        @block.sync
        def _(sp):
            def load(b, s, first, last):
                if not first:
                    sp.wait_ge(hidden, b * 2 - 2)
                for pg in range(NPAGE):
                    with_id = sp.value_load(M["pages"][0:1, bass.ds(b * NPAGE + pg, 1)], min_val=0,
                                            max_val=I["pages_raw"].shape[0] - 1)
                    sp.dma_start(RAW[:, s, pg].rearrange("p k n -> p (k n)"),
                                 I["pages_raw"][bass.ds(with_id, 1)].rearrange("a p n -> p (a n)")).then_inc(raw_in[s], 16)
            over_sequences(sp, load)

        @block.gpsimd
        def _(pool):
            def queries(b, s, first, last):
                if not first:
                    pool.wait_ge(score, b - 1)
                queries_of(nc, QS, QB, b, s, qb)
            over_sequences(pool, queries)

        @block.tensor
        def _(pe):
            def hide(b, s, kind, half):
                bank = ps[2 * s + kind]
                out = bank[:, 1 - half:1 - half + NBLK].rearrange("p (g n c) -> p g n c", g=NKV, n=NPAGE)
                for i in range(8):
                    rhs = RAW[:, s, :, kind, i * 32:(i + 1) * 32].rearrange("p n (g c) -> p g n c", g=NKV)
                    pe.matmul(out, W1[:, kind, half, i, :], rhs, start=(half + i == 0), stop=False,
                              skip_group_check=True)
                if half == 1:
                    pe.matmul(bank[:, 1:1 + NBLK], BIAS[0:1, kind, :], ONES[0:1, 0:NBLK], start=False, stop=True,
                              skip_group_check=True).then_inc(hidden, 1)

            def hide_after(b, s, kind, half, first):
                if kind == 0 and half == 0:
                    pe.wait_ge(raw_in[s], landed_pages(b, s))
                if half == 0 and not first:
                    pe.wait_ge(gelu, b * 2 + (kind - 3))
                hide(b, s, kind, half)

            def landed_pages(b, s):
                return (b - s) * (16 * NPAGE // 2) + 16 * NPAGE

            def seq(b, s, first, last):
                nxt = lambda kind, half: None if last else hide_after(b + 1, 1 - s, kind, half, first and s == 0)
                nxt(0, 0)
                pe.wait_ge(gelu, b * 2 + 2)
                if not (first and s == 0):
                    pe.wait_ge(ckt, b)
                    pe.wait_ge(cv_out, b)
                for j in range(2):
                    out = ps[4][:, j * NB:(j + 1) * NB]
                    pe.matmul(out, W2[:, 0, HD:3 * HD], HIDB[:, s, 0, 2 * j * NB:(2 * j + 1) * NB], start=True, stop=False)
                    last_mm = pe.matmul(out, W2[:, 0, 0:2 * HD], HIDB[:, s, 0, (2 * j + 1) * NB:(2 * j + 2) * NB],
                                        start=False, stop=True)
                last_mm.then_inc(ck, 1)
                for g in range(NKV):
                    last_mm = pe.matmul(ps[5][0:NB, g * HD:(g + 1) * HD], HIDB[:, s, 1, g * NB:(g + 1) * NB],
                                        W2[:, 1, HD:2 * HD], start=True, stop=True)
                last_mm.then_inc(cv, 1)
                nxt(0, 1)
                pe.wait_ge(squared, b + 1)
                pe.matmul(ps[4][:, 2 * NB:4 * NB], blockones, SQ.rearrange("p j c -> p (j c)"), start=True, stop=True)\
                    .then_inc(ss, 1)
                nxt(1, 0)
                pe.wait_ge(ckt, b + 1)
                pe.wait_ge(qb, b * 4 + 4)
                if not (first and s == 0):
                    pe.wait_ge(chosen, b)
                for j in range(2):
                    last_mm = pe.matmul(ps[6][:, 0:NB], QB[:, s, j, :], CKT[:, j, :], start=(j == 0), stop=(j == 1))
                last_mm.then_inc(score, 1)
                nxt(1, 1)
                pe.wait_ge(prob, b + 1)
                pe.matmul(ps[6][:, NB:2 * NB], headsum, PR, start=True, stop=True).then_inc(pooled, 1)

            for kind in range(2):
                for half in range(2):
                    hide_after(0, 0, kind, half, True)
            over_sequences(pe, seq)

        @block.scalar
        def _(act):
            def take_gelu(b, s, first):
                for kind in range(2):
                    act.wait_ge(hidden, b * 2 + (kind + 1))
                    if not first:
                        act.wait_ge(cv, b - 1)
                    act.activation(HIDB[:, s, kind, :], ps[2 * s + kind][:, 1:NBLK + 1], ACT.Gelu_apprx_tanh)\
                        .then_inc(gelu, 1)

            def seq(b, s, first, last):
                act.wait_ge(ck, b + 1)
                if not (first and s == 0):
                    act.wait_ge(ss, b)
                act.activation(SQ.rearrange("p j c -> p (j c)"), ps[4][:, 0:2 * NB], ACT.Square).then_inc(squared, 1)
                act.wait_ge(mean, b + 1)
                act.activation(RS, RS, ACT.Sqrt).then_inc(root, 1)
                act.wait_ge(negmax, b + 1)
                act.activation(PR, ps[6][:, 0:NB], ACT.Exp, bias=sm[:, 0:1], scale=SCALE,).then_inc(expd, 1)
                if not last:
                    take_gelu(b + 1, 1 - s, first and s == 0)
            take_gelu(0, 0, True)
            over_sequences(act, seq)

        @block.vector
        def _(dve):
            V = nc.vector

            def seq(b, s, first, last):
                st = Steps(dve, chain, b * DCH)
                dve.wait_ge(cv, b + 1)
                V.tensor_copy(CV[0:NB, bass.ds(b, 1), :], ps[5][0:NB, 0:NKV * HD].unsqueeze(1)).then_inc(cv_out, 1)
                dve.wait_ge(ss, b + 1)
                V.tensor_scalar(RS, ps[4][:, 2 * NB:4 * NB].rearrange("p (j c) -> p j c", j=2), 1.0 / HD, EPS,
                                ALU.mult, ALU.add).then_inc(mean, 1)
                dve.wait_ge(root, b + 1)
                st.add(V.reciprocal(RS, RS))
                if not (first and s == 0):
                    dve.wait_ge(score, b)
                V.scalar_tensor_tensor(CKT, ps[4][:, 0:2 * NB].rearrange("p (j c) -> p j c", j=2), KG[:, 0:1], RS,
                                       ALU.mult, ALU.mult).then_inc(ckt, 1)
                dve.wait_ge(score, b + 1)
                st.add(V.tensor_reduce(sm[:, 1:2], ps[6][:, 0:NCS], AX.X, ALU.max))
                V.tensor_scalar(sm[:, 0:1], sm[:, 1:2], -SCALE, None, ALU.mult).then_inc(negmax, 1)
                dve.wait_ge(expd, b + 1)
                st.add(V.tensor_reduce(sm[:, 2:3], PR[:, 0:NCS], AX.X, ALU.add))
                st.add(V.reciprocal(sm[:, 3:4], sm[:, 2:3]))
                V.tensor_scalar(PR, PR, sm[:, 3:4], None, ALU.mult).then_inc(prob, 1)
                dve.wait_ge(prob, b + 1)
                V.tensor_scalar(PC[:, bass.ds(b, 1), :], PR.unsqueeze(1), GS[:, 0, bass.ds(b, 1)], None, ALU.mult)
                dve.wait_ge(pooled, b + 1)
                pg = ps[6][:, NB + 4:NB + 4 * (NSB - 2)].rearrange("p (j o) -> p j o", o=4)
                prev = ps[6][:, NB + 3:NB + 3 + 4 * (NSB - 3)].rearrange("p (j o) -> p j o", o=4)[:, :, 0]
                st.add(V.tensor_reduce(SCORE, pg, AX.X, ALU.add))
                st.add(V.tensor_tensor(SCORE, SCORE, prev, ALU.add))
                st.add(V.tensor_reduce(sm[:, 4:5], SCORE, AX.X, ALU.min))
                st.add(V.scalar_tensor_tensor(KEY, SCORE, sm[:, 4:5], iota, ALU.is_equal, ALU.mult))
                st.add(V.tensor_reduce(sm[:, 5:6], KEY, AX.X, ALU.max))
                st.add(V.tensor_scalar(KEY, iota, sm[:, 5:6], NEG, ALU.is_equal, ALU.mult))
                V.tensor_copy(BM[:, bass.ds(b, 1), 1:NSB - 2], KEY.unsqueeze(1)).then_inc(chosen, 1)
                st.add(V.memset(sm[:, 6:7], 0.0))
                assert st.n == DCH - 1 + 0 or True
                DCHN[0] = st.n

            DCHN = [0]
            over_sequences(dve, seq)
            assert DCHN[0] == DCH, DCHN

    with ExitStack() as ctx:
        block = ctx.enter_context(nc.Block())

        @block.vector
        def _(dve):
            nc.vector.memset(BM[:, :, 0:1], 0.0)
            nc.vector.memset(BM[:, :, NSB - 2:16], 0.0)


def attend_samples(nc, I, M):
    ps, OT = M["ps"], M["XT"]
    SEL = view(M, Map.PAGES, 2, NPAGE, 512)
    WB = view(M, Map.WINB, 2, 2048)
    QS, QB = view(M, Map.QSR, 2, HPG, NEWTOK), view(M, Map.QB, 2, 2, P)
    KTN = view(M, Map.KTN, 2, 2, NEWTOK)
    VNEW, CVB = view(M, Map.VNEW, NKV * HD), view(M, Map.CVB, 2, NKV * HD)
    CV, PC, BM = view(M, Map.CV, NSEQ, NKV * HD), view(M, Map.PC, NSEQ, NCS + 1), view(M, Map.BM, NSEQ, 16)
    GS = view(M, Map.GS, 3, NSEQ)
    NEW = PAST
    WCOL = PAST + 2 * NEWTOK
    CCOL = WCOL + WIN
    NCOL = CCOL + NCS + 1
    NTILE = 14
    PR = [view(M, Map.PROW0, NCOL), view(M, Map.PROW1, NCOL)]
    PT = [view(M, Map.PT0, NTILE, P), view(M, Map.PT1, NTILE, P)]
    sm = view(M, Map.SMALL, 2, 32)
    newmask = const(M, "newmask").rearrange("p (b t) -> p b t", b=NSEQ)
    winmask, ident = const(M, "winmask"), const(M, "ident")
    tiles = [(i * P, P) for i in range(NPAGE + 1)] + [(WCOL + i * P, P) for i in range(WIN // P)] + [(CCOL, NCS)]
    with ExitStack() as ctx:
        sem = lambda n: ctx.enter_context(nc.semaphore("atts_" + n))
        sel_in = [sem(f"pages_landed{s}") for s in range(2)]
        win_in = [sem(f"window_landed{s}") for s in range(2)]
        qb, cvb, bmb = sem("queries_ready"), sem("cvalues_ready"), sem("blockmask_ready")
        score, masked, negmax, expd = sem("scores_ready"), sem("scores_read"), sem("negmax_ready"), sem("exp_ready")
        weighted, turned, by_dve, by_act = sem("probs_ready"), sem("probs_turned"), sem("turned_by_dve"), sem("turned_by_act")
        summed, out, chain, wread = sem("values_summed"), sem("out_copied"), sem("chain"), sem("window_masked")
        block = ctx.enter_context(nc.Block())
        DCH = 10

        def over_sequences(eng, body):
            for s in range(2):
                body(s, s, True, False)
            with eng.Fori(1, NSEQ // 2 - 1) as i:
                for s in range(2):
                    body(i * 2 + s, s, False, False)
            for s in range(2):
                body(NSEQ - 2 + s, s, False, s == 1)

        @block.sync
        def _(sp):
            def load(b, s, first, last):
                if not first:
                    sp.wait_ge(summed, b - 1)
                for pg in range(NPAGE):
                    pid = sp.value_load(M["pages"][0:1, bass.ds(b * NPAGE + pg, 1)], min_val=0,
                                        max_val=I["pages_sel"].shape[0] - 1)
                    sp.dma_start(SEL[:, s, pg], I["pages_sel"][bass.ds(pid, 1)].rearrange("a p n -> p (a n)"))\
                        .then_inc(sel_in[s], 16)
                sp.dma_start(WB[:, s, 0:2 * WIN], I["win_keysT"][bass.ds(b, 1)].rearrange("a p n -> p (a n)"))\
                    .then_inc(win_in[s], 16)
                sp.dma_start(WB[:, s, 2 * WIN:].rearrange("p (k n) -> p k n", k=WIN // P),
                             I["state_win"][bass.ds(b, 1), :, 1].rearrange("a (k p) g d -> p (a k) (g d)", p=P))\
                    .then_inc(win_in[s], 16)
            over_sequences(sp, load)

        @block.gpsimd
        def _(pool):
            def prepare(b, s, first, last):
                if not first:
                    pool.wait_ge(score, b - 1)
                queries_of(nc, QS, QB, b, s, qb)
                pool.wait_ge(qb, b * 4 + 4)
                if not first:
                    pool.wait_ge(masked, b * 4 - 4)
                nc.gpsimd.tensor_copy(sm[:, s, 16:32].unsqueeze(1), BM[:, bass.ds(b, 1), :]).then_inc(bmb, 1)
                pool.wait_ge(bmb, b + 1)
                if not first:
                    pool.wait_ge(summed, b - 1)
                nc.gpsimd.tensor_copy(CVB[0:NCS + 1, s].unsqueeze(1), CV[0:NCS + 1, bass.ds(b, 1), :]).then_inc(cvb, 1)
            over_sequences(pool, prepare)

        @block.tensor
        def _(pe):
            def scores(b, s, first):
                pe.wait_ge(qb, b * 4 + 4)
                pe.wait_ge(sel_in[s], (b - s) * (16 * NPAGE // 2) + 16 * NPAGE)
                if not first:
                    pe.wait_ge(masked, b * 4)
                    pe.wait_ge(expd, b * 4)
                for bank in range(2):
                    for j in range(2):
                        pe.matmul(ps[bank][:, :], QB[:, s, j, :],
                                  SEL[:, s, 4 * bank:4 * bank + 4, j * PAGE:(j + 1) * PAGE], start=(j == 0), stop=(j == 1))
                for br in range(2):
                    for j in range(2):
                        pe.matmul(ps[3][:, br * NEWTOK:(br + 1) * NEWTOK], QB[:, s, j, :], KTN[:, br, j, :],
                                  start=(j == 0), stop=(j == 1))
                pe.wait_ge(win_in[s], (b - s) * 16 + 32)
                for j in range(2):
                    last = pe.matmul(ps[2][:, :], QB[:, s, j, :], WB[:, s, j * WIN:(j + 1) * WIN],
                                     start=(j == 0), stop=(j == 1))
                last.then_inc(score, 1)

            def turn(b, s):
                pe.wait_ge(weighted, b * 3 + 3)
                for q in range(4):
                    if q >= 2:
                        pe.wait_ge((by_dve, by_act)[q % 2], b * 2 + 1)
                    elif True:
                        wait_prev(b, s, q)
                    for m, (at, w) in enumerate(tiles[4 * q:4 * q + 4]):
                        last = pe.transpose(ps[4 + q % 2][0:w, m * P:(m + 1) * P], PR[s][:, at:at + w], ident)
                    last.then_inc(turned, 1)

            def wait_prev(b, s, q):
                if not first_turn[0]:
                    pe.wait_ge((by_dve, by_act)[q % 2], b * 2)

            def values(b, s, first):
                pe.wait_ge(by_dve, b * 2 + 2)
                pe.wait_ge(by_act, b * 2 + 2)
                pe.wait_ge(cvb, b + 1)
                if not first:
                    pe.wait_ge(out, b * 2 - 2)
                for g in range(NKV):
                    gd = slice(g * HD, (g + 1) * HD)
                    for t in range(NTILE):
                        if t < NPAGE:
                            v = SEL[:, s, t, 2 * PAGE + g * HD:2 * PAGE + (g + 1) * HD]
                        elif t == NPAGE:
                            v = VNEW[:, gd]
                        elif t < NTILE - 1:
                            at = 2 * WIN + (t - NPAGE - 1) * NKV * HD + g * HD
                            v = WB[:, s, at:at + HD]
                        else:
                            v = CVB[0:NCS, s, gd]
                        k = NCS if t == NTILE - 1 else P
                        q = g * HPG * STEPS
                        last = pe.matmul(ps[6 + s][0:HD, q:q + HPG * STEPS], v, PT[s][0:k, t, q:q + HPG * STEPS],
                                         start=(t == 0), stop=(t == NTILE - 1))
                last.then_inc(summed, 1)

            first_turn = [True]

            def seq(b, s, first, last):
                if not last:
                    scores(b + 1, 1 - s, False)
                first_turn[0] = first and s == 0
                turn(b, s)
                values(b, s, first)
            scores(0, 0, True)
            over_sequences(pe, seq)

        def copy_turned(eng, copy, b, s, half, first, done, other):
            for q in (half, half + 2):
                eng.wait_ge(turned, b * 4 + (q + 1))
                if q == half and not first:
                    eng.wait_ge(summed, b - 1)
                if q == 3:
                    copy(PT[s][:, 12, :], ps[4 + q % 2][:, 0:P]).then_inc(other, 1)
                    copy(PT[s][0:NCS, 13, :], ps[4 + q % 2][0:NCS, P:2 * P]).then_inc(done, 1)
                else:
                    copy(PT[s][:, 4 * q:4 * q + 4, :].rearrange("p m t -> p (m t)"), ps[4 + q % 2][:, :]).then_inc(done, 1)

        tail = ctx.enter_context(nc.semaphore("atts_tail_copied"))

        @block.scalar
        def _(act):
            def softmax(b, s, first):
                act.wait_ge(negmax, b + 1)
                if not first:
                    act.wait_ge(turned, b * 4 - 4)
                for n, (dst, src, br) in enumerate(((slice(0, PAST), PR[s][:, 0:PAST], 0),
                                                    (slice(NEW, NEW + NEWTOK), PR[s][:, NEW:NEW + NEWTOK], 0),
                                                    (slice(NEW + NEWTOK, WCOL), PR[s][:, NEW + NEWTOK:WCOL], 1),
                                                    (slice(WCOL, CCOL), ps[2][:, :], 1))):
                    act.activation(PR[s][:, dst], src, ACT.Exp, bias=sm[:, s, br:br + 1], scale=SCALE,
                                   accum_out=sm[:, s, 4 + n:5 + n]).then_inc(expd, 1)

            def seq(b, s, first, last):
                if not last:
                    softmax(b + 1, 1 - s, first and s == 0)
                copy_turned(act, nc.scalar.copy, b, s, 1, first, by_act, tail)
            softmax(0, 0, True)
            over_sequences(act, seq)

        @block.vector
        def _(dve):
            V = nc.vector

            def softmax(b, s, first):
                st = Steps(dve, chain, b * DCH)
                dve.wait_ge(score, b + 1)
                dve.wait_ge(bmb, b + 1)
                if not first:
                    dve.wait_ge(turned, b * 4 - 4)
                V.tensor_tensor(PR[s][:, NEW:WCOL].rearrange("p (r t) -> p r t", r=2),
                                ps[3][:, 0:2 * NEWTOK].rearrange("p (r t) -> p r t", r=2),
                                newmask[:, bass.ds(b, 1), :].broadcast_to([P, 2, NEWTOK]), ALU.add).then_inc(masked, 1)
                for bank in range(2):
                    V.tensor_tensor_reduce(
                        PR[s][:, bank * 512:(bank + 1) * 512].rearrange("p (k c) -> p k c", c=SELB),
                        ps[bank][:, :].rearrange("p (k c) -> p k c", c=SELB),
                        sm[:, s, 16 + 8 * bank:24 + 8 * bank].unsqueeze(2).broadcast_to([P, 8, SELB]),
                        1.0, -3e38, ALU.add, ALU.max, sm[:, s, 8 + bank:9 + bank]).then_inc(masked, 1)
                V.tensor_tensor(ps[2][:, 0:STEPS], ps[2][:, 0:STEPS], winmask, ALU.add).then_inc(masked, 1)
                dve.wait_ge(masked, b * 4 + 4)
                st.add(V.tensor_reduce(sm[:, s, 10:12], PR[s][:, NEW:WCOL].rearrange("p (r t) -> p r t", r=2), AX.X, ALU.max))
                st.add(V.tensor_reduce(sm[:, s, 12:13], ps[2][:, :], AX.X, ALU.max))
                st.add(V.tensor_tensor(sm[:, s, 13:14], sm[:, s, 8:9], sm[:, s, 9:10], ALU.max))
                st.add(V.tensor_tensor(sm[:, s, 14:15], sm[:, s, 10:11], sm[:, s, 13:14], ALU.max))
                st.add(V.tensor_tensor(sm[:, s, 15:16], sm[:, s, 11:12], sm[:, s, 12:13], ALU.max))
                V.tensor_scalar(sm[:, s, 0:2], sm[:, s, 14:16], -SCALE, None, ALU.mult).then_inc(negmax, 1)
                dve.wait_ge(expd, b * 4 + 4)
                st.add(V.tensor_tensor(sm[:, s, 8:9], sm[:, s, 4:5], sm[:, s, 5:6], ALU.add))
                st.add(V.tensor_tensor(sm[:, s, 9:10], sm[:, s, 6:7], sm[:, s, 7:8], ALU.add))
                st.add(V.reciprocal(sm[:, s, 10:12], sm[:, s, 8:10]))
                st.add(V.tensor_tensor(sm[:, s, 12:14].unsqueeze(2), sm[:, s, 10:12].unsqueeze(2),
                                       GS[:, 1:3, bass.ds(b, 1)], ALU.mult))
                V.tensor_scalar(PR[s][:, 0:NEW + NEWTOK], PR[s][:, 0:NEW + NEWTOK], sm[:, s, 12:13], None, ALU.mult)\
                    .then_inc(weighted, 1)
                V.tensor_scalar(PR[s][:, NEW + NEWTOK:CCOL], PR[s][:, NEW + NEWTOK:CCOL], sm[:, s, 13:14], None, ALU.mult)\
                    .then_inc(weighted, 1)
                V.tensor_copy(PR[s][:, CCOL:NCOL].unsqueeze(1), PC[:, bass.ds(b, 1), :]).then_inc(weighted, 1)
                assert st.n == 9, st.n
                st.add(V.memset(sm[:, s, 3:4], 0.0))

            def seq(b, s, first, last):
                if not last:
                    softmax(b + 1, 1 - s, first and s == 0)
                copy_turned(dve, V.tensor_copy, b, s, 0, first, by_dve, None)
                dve.wait_ge(summed, b + 1)
                for par in range(2):
                    src = ps[6 + s][0:HD, 0:P].rearrange("p (k r t) -> p k r t", r=2, t=STEPS)[:, :, par, :]
                    V.tensor_copy(OT[par * HD:(par + 1) * HD, :, bass.ds(b * STEPS + SEQ, STEPS)], src).then_inc(out, 1)
            softmax(0, 0, True)
            over_sequences(dve, seq)


def attend_prompt(nc, I, M):
    ps, OT, gates = M["ps"], M["XT"], M["gates"]
    QN, QR = view(M, Map.QNT, 2, HPG, SEQ), view(M, Map.QRT, 2, HPG, SEQ)
    KT, CKP = view(M, Map.KTP, 2, 2, SEQ), view(M, Map.CKP, 2, CHUNK)
    VP, CVP = view(M, Map.VP, 2, 2, NKV, 3 * HD), view(M, Map.CVP, NKV, 3 * HD)
    PTC = view(M, Map.PTC, NH, P)
    PTP = view(M, Map.PTP, 2, 4, P)
    PP = view(M, Map.PP, 3, 2, SEQ)
    PCM = view(M, Map.PP + 6 * SEQ, NH, CHUNK)
    sm = view(M, Map.SMALL, 3, 16)
    csm = view(M, Map.SMALL + 64, 4, NH)
    causal = const(M, "causal").rearrange("p (t k) -> p t k", t=2)
    cadd = const(M, "cmpadd").rearrange("p (t k) -> p t k", t=2)
    cmul = const(M, "cmpmul").rearrange("p (t k) -> p t k", t=2)
    ident = const(M, "ident")
    WO = view(M, Map.WO, KD, D)
    units = [(t, hd) for t in range(2) for hd in range(NH)]
    NU = len(units)
    wo_in = M["wo_in"]

    def part(hd):
        g, h = hd // HPG, hd % HPG
        return slice((g % 2) * HD, (g % 2) * HD + HD), g // 2, h

    def v_cols(hd):
        return slice(0, 2 * HD) if hd % 2 else slice(HD, 3 * HD)

    with ExitStack() as ctx:
        sem = lambda n: ctx.enter_context(nc.semaphore("attp_" + n))
        cscore, cprob, cturned, ccopied, cneg, cexp = (sem("cmp_scores_ready"), sem("cmp_probs_ready"), sem("cmp_turned"),
                                                       sem("cmp_copied"), sem("cmp_shifted"), sem("cmp_exp_ready"))
        score, negmax, expd, weighted = sem("scores_ready"), sem("negmax_ready"), sem("exp_ready"), sem("probs_ready")
        masked, turned, copied, summed, out, chain = (sem("scores_masked"), sem("probs_turned"), sem("turned_copied"),
                                                      sem("values_summed"), sem("out_copied"), sem("chain"))
        block = ctx.enter_context(nc.Block())

        @block.sync
        def _(sp):
            sp.dma_start(WO, I["w_o"][0].rearrange("(k p) n -> p k n", p=P)).then_inc(wo_in, 16)

        @block.tensor
        def _(pe):
            def scores(n):
                t, hd = units[n]
                pp, j, h = part(hd)
                if n >= 3:
                    pe.wait_ge(masked, 2 * (n - 2))
                K = P * (t + 1)
                for br in range(2):
                    last = pe.matmul(ps[n % 3][:, br * K:(br + 1) * K], QR[pp, j, h, t * P:(t + 1) * P],
                                     KT[pp, br, j, 0:K], start=True, stop=True)
                last.then_inc(score, 1)

            def turn(n):
                t, hd = units[n]
                pe.wait_ge(weighted, 2 * (n + 1))
                if n >= 2:
                    pe.wait_ge(copied, n - 1)
                m = 0
                for br in range(2):
                    for kt in range(t + 1):
                        last = pe.transpose(ps[3 + n % 2][:, m * P:(m + 1) * P], PP[:, n % 3, br, kt * P:(kt + 1) * P], ident)
                        m += 1
                last.then_inc(turned, 1)

            def values(n):
                t, hd = units[n]
                g, pair = hd // HPG, n // 2
                pe.wait_ge(copied, n + 1)
                if n == 0 or n == NH:
                    pe.wait_ge(ccopied, 4 * (t + 1))
                if hd % 2 == 0 and pair >= 2:
                    pe.wait_ge(out, pair - 1)
                bank = ps[5 + pair % 2][:, 0:P]
                m = 0
                for br in range(2):
                    for kt in range(t + 1):
                        pe.matmul(bank, VP[:, kt, br, g, v_cols(hd)], PTP[:, n % 2, m, :],
                                  start=(hd % 2 == 0 and m == 0), stop=False)
                        m += 1
                pe.matmul(bank, CVP[0:NCP, g, v_cols(hd)], PTC[0:NCP, hd, :], start=False, stop=(hd % 2 == 1))\
                    .then_inc(summed, 1)

            def compressed(t):
                for par in range(2):
                    for hd in [x for x in range(NH) if x // HPG % 2 == par]:
                        pp, j, h = part(hd)
                        last = pe.matmul(ps[7][:, hd * CHUNK:hd * CHUNK + NCP], QN[pp, j, h, t * P:(t + 1) * P],
                                         CKP[pp, j, 0:NCP], start=True, stop=True)
                    last.then_inc(cscore, 1)
                    pe.wait_ge(cscore, 2 * t + par + 1)

            def turn_compressed(t):
                pe.wait_ge(cprob, t + 1)
                if t:
                    pe.wait_ge(summed, NH)
                for q in range(4):
                    if q or t:
                        pe.wait_ge(ccopied, 4 * t + q)
                    for m in range(4):
                        last = pe.transpose(ps[7][0:NCP, m * P:(m + 1) * P], PCM[:, 4 * q + m, 0:NCP], ident)
                    last.then_inc(cturned, 1)

            compressed(0)
            scores(0)
            scores(1)
            turn_compressed(0)
            compressed_at = NH - 2
            for n in range(NU + 1):
                if n + 2 < NU:
                    scores(n + 2)
                if n < NU:
                    turn(n)
                if n >= 1:
                    values(n - 1)
                if n == NH:
                    compressed(1)
                    turn_compressed(1)

        @block.scalar
        def _(act):
            def unit(n):
                t, hd = units[n]
                K = P * (t + 1)
                act.wait_ge(negmax, n + 1)
                for br in range(2):
                    act.activation(PP[:, n % 3, br, 0:K], PP[:, n % 3, br, 0:K], ACT.Exp, bias=sm[:, n % 3, br:br + 1],
                                   scale=SCALE, accum_out=sm[:, n % 3, 4 + br:5 + br]).then_inc(expd, 1)

            def copy_turned(n):
                t, hd = units[n]
                act.wait_ge(turned, n + 1)
                if n >= 2:
                    act.wait_ge(summed, n - 1)
                w = 2 * (t + 1)
                nc.scalar.copy(PTP[:, n % 2, 0:w, :].rearrange("p m q -> p (m q)"), ps[3 + n % 2][:, 0:w * P])\
                    .then_inc(copied, 1)

            def exp_compressed(t):
                act.wait_ge(cneg, t + 1)
                act.activation(PCM[:, :, 0:NCP], PCM[:, :, 0:NCP], ACT.Exp, scale=SCALE).then_inc(cexp, 1)

            def copy_compressed(t):
                for q in range(4):
                    act.wait_ge(cturned, 4 * t + q + 1)
                    nc.scalar.copy(PTC[0:NCP, 4 * q:4 * q + 4, :].rearrange("p m q -> p (m q)"), ps[7][0:NCP, :])\
                        .then_inc(ccopied, 1)

            exp_compressed(0)
            unit(0)
            copy_compressed(0)
            for n in range(NU):
                if n + 1 < NU:
                    unit(n + 1)
                copy_turned(n)
                if n == NH:
                    exp_compressed(1)
                    copy_compressed(1)

        @block.vector
        def _(dve):
            V = nc.vector
            st = Steps(dve, chain)

            def compressed(t):
                dve.wait_ge(cscore, 2 * (t + 1))
                s = ps[7][:, 0:NH * CHUNK].rearrange("p (h c) -> p h c", h=NH)[:, :, 0:NCP]
                x = PCM[:, :, 0:NCP]
                if t:
                    dve.wait_ge(cturned, 4)
                add = cadd[:, t].unsqueeze(1).broadcast_to([P, NH, NCP])
                mul = cmul[:, t].unsqueeze(1).broadcast_to([P, NH, NCP])
                st.add(V.tensor_tensor(x, s, add, ALU.add))
                st.add(V.tensor_reduce(csm[:, 0], x, AX.X, ALU.max))
                V.tensor_tensor(x, x, csm[:, 0].unsqueeze(2).broadcast_to([P, NH, NCP]), ALU.subtract).then_inc(cneg, 1)
                dve.wait_ge(cexp, t + 1)
                st.add(V.tensor_tensor(x, x, mul, ALU.mult))
                st.add(V.tensor_reduce(csm[:, 1], x, AX.X, ALU.add))
                st.add(V.tensor_scalar(csm[:, 1], csm[:, 1], 1e-30, None, ALU.max))
                st.add(V.reciprocal(csm[:, 2], csm[:, 1]))
                st.add(V.tensor_tensor(csm[:, 2], csm[:, 2], gates[:, t, 0:NH], ALU.mult))
                V.tensor_tensor(x, x, csm[:, 2].unsqueeze(2).broadcast_to([P, NH, NCP]), ALU.mult).then_inc(cprob, 1)

            def before(n):
                t, hd = units[n]
                K = P * (t + 1)
                s = n % 3
                dve.wait_ge(score, n + 1)
                if n >= 3:
                    dve.wait_ge(turned, n - 2)
                for br in range(2):
                    V.tensor_tensor_reduce(PP[:, s, br, 0:K], ps[n % 3][:, br * K:(br + 1) * K], causal[:, t, 0:K],
                                           1.0, -3e38, ALU.add, ALU.max, sm[:, s, 2 + br:3 + br]).then_inc(masked, 1)
                dve.wait_ge(masked, 2 * (n + 1))
                V.tensor_scalar(sm[:, s, 0:2], sm[:, s, 2:4], -SCALE, None, ALU.mult).then_inc(negmax, 1)

            def after(n):
                t, hd = units[n]
                K = P * (t + 1)
                s = n % 3
                dve.wait_ge(expd, 2 * (n + 1))
                st.add(V.reciprocal(sm[:, s, 6:8], sm[:, s, 4:6]))
                st.add(V.tensor_tensor(sm[:, s, 8:10], sm[:, s, 6:8], gates[:, t, NH + hd:2 * NH + hd + 1:NH], ALU.mult))
                for br in range(2):
                    V.tensor_scalar(PP[:, s, br, 0:K], PP[:, s, br, 0:K], sm[:, s, 8 + br:9 + br], None, ALU.mult)\
                        .then_inc(weighted, 1)

            def copy_out(n):
                t, hd = units[n]
                if hd % 2:
                    dve.wait_ge(summed, n + 1)
                    V.tensor_copy(OT[:, hd // 2, t * P:(t + 1) * P], ps[5 + (n // 2) % 2][:, 0:P]).then_inc(out, 1)

            compressed(0)
            before(0)
            for n in range(NU + 2):
                if n + 1 < NU:
                    before(n + 1)
                if n < NU:
                    after(n)
                if n >= 2:
                    copy_out(n - 2)
                if n == NH:
                    compressed(1)


def output_projection(nc, M):
    H, OT, ps, WO = M["H"], M["XT"], M["ps"], view(M, Map.WO, KD, D)
    with ExitStack() as ctx:
        sem = lambda n: ctx.enter_context(nc.semaphore("out_" + n))
        product, added = sem("product_ready"), sem("added")
        block = ctx.enter_context(nc.Block())
        parts = [(i, rows, half) for i, rows in enumerate(TILE_ROWS) for half in range(2)]

        @block.tensor
        def _(pe):
            pe.wait_ge(M["wo_in"], 16)
            for n, (i, rows, half) in enumerate(parts):
                for k in range(KD):
                    last = pe.matmul(ps[n][0:rows, :], OT[:, k, i * P:i * P + rows], WO[:, k, half * 512:(half + 1) * 512],
                                     start=(k == 0), stop=(k == KD - 1))
                last.then_inc(product, 1)

        @block.vector
        def _(dve):
            for n, (i, rows, half) in enumerate(parts):
                dve.wait_ge(product, n + 1)
                hv = H[0:rows, i, half * 512:(half + 1) * 512]
                nc.vector.tensor_tensor(hv, ps[n][0:rows, :], hv, ALU.add).then_inc(added, 1)


def constant_table():
    import numpy as np
    t = np.zeros((P, NCONST), np.float32)

    def put(name, a):
        a = np.asarray(a, np.float32)
        a = a.reshape(a.shape[0], -1)
        at, w = CONST[name]
        assert a.shape[1] == w
        t[:a.shape[0], at:at + w] = a

    p = np.arange(P)
    put("ident", np.eye(P))
    put("blockones", (p[:, None] // HD == p[None] // HD))
    grp, step = p // (HPG * STEPS), p % STEPS
    put("headsum", (grp[:, None] == grp[None]) & (step[:, None] == step[None]))
    q = np.arange(SEQ).reshape(2, P).T
    put("causal", np.where(np.arange(SEQ)[None, None] <= q[:, :, None], 0.0, NEG))
    ok = (np.arange(NCP) * CHUNK + 2 * CHUNK - 1)[None, None] <= q[:, :, None]
    put("cmpadd", np.where(ok, 0.0, NEG))
    put("cmpmul", ok)
    b, col = np.arange(NSEQ), np.arange(NEWTOK)
    mine = (col[None, None] // STEPS == b[None, :, None]) & (col[None, None] % STEPS <= step[:, None, None])
    put("newmask", np.where(mine, 0.0, NEG))
    put("winmask", np.where(np.arange(STEPS)[None] > step[:, None], 0.0, NEG))
    put("iota", np.tile(np.arange(1, NSB - 2), (P, 1)))
    r = np.arange(NEWTOK)
    put("stepsel", (r[:, None] % STEPS) == np.arange(STEPS)[None])
    put("seqsel", (r[:, None] // STEPS) == np.arange(NSEQ)[None])
    put("first", np.tile(np.arange(NG, 0, -1), (P, 1)))
    half = HD // 2
    inv = np.float32(1.0) / (np.float32(10000.0) ** (np.arange(half, dtype=np.float32) * np.float32(2.0 / HD)))
    pos = np.zeros((P, NT), np.float32)
    pos[:, 0], pos[:, 1] = p, p + P
    pos[:NEWTOK, 2] = PAST + r % STEPS
    ang = (pos[:, :, None] * inv[None, None]).astype(np.float32)
    put("cos", np.cos(ang))
    put("sin", np.sin(ang))
    return t


def pooling_matrices():
    import numpy as np
    m = np.zeros((P, NPOOL, NPM), np.float32)
    for g, w in enumerate(POOL_WINDOWS):
        for t in range(SEQ):
            lo = max(t + 1 - w, 0)
            for s in range(lo, t + 1):
                m[s % P, g, (s // P) * SEQ + t] += np.float32(1.0 / (t + 1 - lo))
            m[t % P, g, (t // P) * SEQ + t] -= 1.0
        for b in range(NSEQ):
            for t in range(STEPS):
                for s in range(STATE + t + 1 - w, STATE + t + 1):
                    if s < STATE:
                        m[b * STATE + s, g, 2 * SEQ + b * STEPS + t] += 1.0 / w
                    else:
                        m[b * STEPS + s - STATE, g, 2 * SEQ + NEWTOK + b * STEPS + t] += 1.0 / w
                m[b * STEPS + t, g, 2 * SEQ + NEWTOK + b * STEPS + t] -= 1.0
    return m


_PLAIN = ["x_prompt", "x_sample", "state_pool", "state_win", "norm_mix", "pool_w", "pool_scale", "w_kv", "cmp_w1",
          "cmp_b1", "cmp_w2", "w_qg", "w_o", "router_group", "router_expert", "w_gate_up", "w_down", "k_norm", "q_norm"]
_OUTS = [("y_prompt", (1, SEQ, D)), ("y_sample", (NSEQ, STEPS, D)), ("new_pool_prompt", (1, 1, STATE, D)),
         ("new_pool_sample", (1, NSEQ, STATE, D)), ("new_kv_prompt", (1, SEQ, 4, NKV, HD)),
         ("new_kv_sample", (NSEQ, STEPS, 4, NKV, HD)), ("new_win_prompt", (1, SEQ, 2, NKV, HD)),
         ("new_win_sample", (NSEQ, WIN, 2, NKV, HD))]


def kernel(**inputs):
    import numpy as np
    import concourse.bacc as bacc
    from concourse.bass_utils import run_bass_kernel_spmd

    x = {k: np.asarray(v) for k, v in inputs.items()}
    arrays = {n: x[n] for n in _PLAIN}
    arrays["consts"] = constant_table()
    arrays["pool_mats"] = pooling_matrices()
    gains = [x["norm_mix"][0], x["norm_ffn"][0], x["norm_mix"][1], x["kv_norm"], x["norm_ffn"][1]]
    arrays["gainsT"] = np.stack([g.reshape(KD, P).T for g in gains], axis=1)
    arrays["page_ids"] = x["page_table"].reshape(1, -1)
    pages = x["cache_kv"]
    n = pages.shape[0]
    raw = pages[:, :, 0:2].reshape(n, PAGE // CHUNK, CHUNK // 2, 2, 2, NKV, HD)
    arrays["pages_raw"] = raw.transpose(0, 3, 6, 4, 2, 5, 1).reshape(n, P, -1)
    ksel = pages[:, :, 2].reshape(n, PAGE, 2, P).transpose(0, 3, 2, 1).reshape(n, P, 2 * PAGE)
    arrays["pages_sel"] = np.concatenate([ksel, pages[:, :, 3].reshape(n, PAGE, NKV * HD)], axis=2)
    arrays["win_keysT"] = x["state_win"][:, :, 0].reshape(NSEQ, WIN, 2, P).transpose(0, 3, 2, 1).reshape(NSEQ, P, 2 * WIN)
    arrays["cmp_pe"] = x["cmp_pe"].reshape(2, 2, CHUNK // 2, P).transpose(3, 0, 1, 2)
    arrays["k_gainT"] = np.concatenate([x["k_norm"][0], x["k_norm"][0]]).reshape(P, 1)

    nc = bacc.Bacc("TRN2", target_bir_lowering=False, num_devices=1)
    feed, I, O = {}, {}, {}
    for name, a in arrays.items():
        a = np.ascontiguousarray(a)
        feed[f"in_{name}"] = a
        I[name] = nc.dram_tensor(f"in_{name}", a.shape, mybir.dt.from_np(a.dtype), kind="ExternalInput").ap()
    for name, shape in _OUTS:
        O[name] = nc.dram_tensor(f"out_{name}", shape, F32, kind="ExternalOutput").ap()
    build(nc, I, O)
    r = run_bass_kernel_spmd(nc, [feed], core_ids=[0])
    return tuple(r.results[0][f"out_{name}"] for name, _ in _OUTS)
```

```python
from contextlib import ExitStack, contextmanager

import concourse.bass as bass
from concourse import mybir

F32 = mybir.dt.float32
F32R = mybir.dt.float32r
I32 = mybir.dt.int32
ALU = mybir.AluOpType
ACT = mybir.ActivationFunctionType
AX = mybir.AxisListType

P = 128
D = 1024
KD = D // P
SEQ, NSEQ, STEPS = 256, 8, 8
NEWTOK = NSEQ * STEPS
TOK = SEQ + NEWTOK
TILE_ROWS = (P, P, NEWTOK)
NT = len(TILE_ROWS)
PAST, PAGE = 1024, 128
NPAGE = PAST // PAGE
WIN = 512
POOL_WINDOWS = (2, 4, 8, 16)
NPOOL = len(POOL_WINDOWS)
STATE = max(POOL_WINDOWS) - 1
GD = D // NPOOL
HD, NH, NKV = 64, 16, 4
HPG = NH // NKV
CHUNK = 16
HID = 2 * HD
NCP = SEQ // CHUNK - 1
NCS = PAST // CHUNK - 1
SELB = 64
NSB = PAST // SELB + 1
NE, NG, EPG, FE = 16, 4, 4, 512
CAP = 64
SCALE = HD ** -0.5
EPS = 1e-6
NEG = -1e30

CONST = {}
NCONST = {"C": 0, "CA": 0}
for _table, _name, _w in (("C", "ident", P), ("C", "first", NG), ("C", "before", P), ("C", "ones", P),
                          ("C", "slots", CAP), ("C", "experts", NE),
                          ("CA", "blockones", P), ("CA", "headsum", P), ("CA", "causal", 2 * SEQ),
                          ("CA", "cmpadd", 2 * NCP), ("CA", "cmpmul", 2 * NCP), ("CA", "newmask", NSEQ * NEWTOK),
                          ("CA", "winmask", STEPS), ("CA", "iota", NSB - 3), ("CA", "stepsel", STEPS),
                          ("CA", "seqsel", NSEQ), ("CA", "cos", NT * HD // 2), ("CA", "sin", NT * HD // 2)):
    CONST[_name] = (_table, NCONST[_table], _w)
    NCONST[_table] += _w
NPM = SEQ * 2 + NEWTOK * 2


ARENA = 44288


class Map:
    WKV, WQG = 0, 12288
    HEADS = 20864
    KVROWS = HEADS + NT * 24 * HD
    WINROWS = KVROWS + NT * 4 * NKV * HD
    QROPE = 31248
    XT2 = 35344
    GAIN24 = XT2 + KD * TOK
    SQ = GAIN24 + 24 * HD
    ROT = SQ + 24 * HD
    QNT, QRT = 0, 2048
    QSN, QSR = 4096, 4608
    QB = 5120
    KTP = 8192
    KTN = KTP + 2 * 2 * SEQ
    VP = KTN + 2 * 2 * NEWTOK
    GS = VP + 2 * 2 * NKV * 3 * HD
    CKP = GS + 3 * NSEQ
    CVP = CKP + 2 * CHUNK
    W1 = 13600
    W2 = W1 + 2 * 2 * 8 * HID
    BIAS = W2 + 2 * 3 * HD
    PE = BIAS + 2 * HID
    ONES = PE + 32
    VNEW = 18700
    CVB = VNEW + NKV * HD
    SMALL = CVB + 2 * NKV * HD
    GATEL = SMALL + 256
    CV = HEADS
    PC = CV + NSEQ * NKV * HD
    BM = PC + NSEQ * HD
    RP = BM + NSEQ * 16
    CHUNKS = 33664
    PAGES = 33664
    HIDB = 30080
    CKB = HIDB + 4 * 256
    WINB = W1
    PT0, PT1 = 30080, 30080 + 14 * P
    PROW0, PROW1 = 5632, PAGES + 8192
    WO = 33664
    PTC = HEADS
    PTP = PTC + 16 * P
    PP = 30080


class Steps:

    def __init__(self, eng, sem, base=0):
        self.eng, self.sem, self.n, self.base = eng, sem, 0, base

    def add(self, ins):
        ins.then_inc(self.sem, 1)
        self.n += 1
        self.eng.wait_ge(self.sem, self.base + self.n)


def build(nc, I, O):
    with ExitStack() as ctx:
        def sb(name, shape, dtype=F32):
            return ctx.enter_context(nc.sbuf_tensor(name, shape, dtype))

        M = {}
        M["H"] = sb("residual", [P, NT, D])
        M["C"] = sb("constants", [P, NCONST["C"]])
        M["gT"] = sb("gainsT", [P, 5, KD])
        M["stat"] = sb("row_stats", [P, 64])
        M["gates"] = sb("gates", [P, NT, 3 * NH])
        M["pages"] = sb("page_ids", [1, NSEQ * NPAGE], I32)
        M["kgain"] = sb("compressed_key_gain", [P, 1])
        M["sems"] = []
        M["ps"] = [ctx.enter_context(nc.psum_tensor(f"bank{i}", [P, 512], F32)) for i in range(8)]
        M["spill"] = nc.dram_tensor("ffn_input_T", [P, KD * TOK], F32, kind="Internal").ap()

        load_constants(nc, I, M)
        with region(nc, M, "a", 16384):
            pool_mixer(nc, I, O, M)
        ffn(nc, I, M, 0)
        clear_sems(nc, M)
        with region(nc, M, "b", ARENA), nc.sbuf_tensor("attention_constants", [P, NCONST["CA"]], F32) as CA:
            M["CA"] = CA
            M["wo_in"] = new_sem(nc, M, "w_o_landed")
            stage_attention(nc, I, O, M)
        clear_sems(nc, M)
        ffn(nc, I, M, 1)
        store_result(nc, O, M)


@contextmanager
def region(nc, M, tag, words):
    with nc.sbuf_tensor("modelT_" + tag, [P, KD, TOK], F32) as XT, \
            nc.sbuf_tensor("arena_" + tag, [P, words], F32) as A:
        M["XT"], M["A"] = XT, A
        yield
        del M["XT"], M["A"]


def new_sem(nc, M, name):
    M["sems"].append(nc.alloc_semaphore(name))
    return M["sems"][-1]


def clear_sems(nc, M):
    nc.clear_and_free_semaphores(M["sems"])
    M["sems"] = []
    nc.all_engine_barrier()


def const(M, name, rows=P):
    table, at, w = CONST[name]
    return M[table][0:rows, at:at + w]


def load_constants(nc, I, M):
    with ExitStack() as ctx:
        landed = new_sem(nc, M, "constants_landed")
        block = ctx.enter_context(nc.Block())

        @block.sync
        def _(sp):
            sp.dma_start(M["C"][:, :], I["consts"]).then_inc(landed, 16)
            sp.dma_start(M["gT"][:, :, :], I["gainsT"]).then_inc(landed, 16)
            sp.dma_start(M["pages"][:, :], I["page_ids"]).then_inc(landed, 16)
            for i, rows in enumerate(TILE_ROWS):
                src = I["x_prompt"][0, i * P:(i + 1) * P, :] if i < 2 else \
                    I["x_sample"].rearrange("b t d -> (b t) d")
                sp.dma_start(M["H"][0:rows, i, :], src).then_inc(landed, 16)
            sp.wait_ge(landed, 16 * 6)

        @block.vector
        def _(dve):
            nc.vector.memset(M["gates"][:, :, :], 0.0)
            nc.vector.memset(M["stat"][:, :], 1.0)


def row_sums(act, scratch, stat, src, summed, rooted, scaled):
    for i, rows in enumerate(TILE_ROWS):
        act.activation(scratch[0:rows, :], src[0:rows, i, :], ACT.Square,
                       accum_out=stat[0:rows, i:i + 1]).then_inc(summed, 1)
        act.wait_ge(summed, i + 1)
    act.wait_ge(scaled, 1)
    act.activation(stat[:, 8:8 + NT], stat[:, 4:4 + NT], ACT.Sqrt).then_inc(rooted, 1)


def pool_mixer(nc, I, O, M):
    A, H, XT, ps = M["A"], M["H"], M["XT"], M["ps"]
    gain = A[:, 0:D]
    pscale = A[:, D:2 * D]
    XN = A[:, 2 * D:5 * D].rearrange("p (i n) -> p i n", i=NT)
    SP = A[:, 5 * D:6 * D]
    PM = A[:, 6 * D:6 * D + NPOOL * NPM].rearrange("p (g n) -> p g n", g=NPOOL)
    at = 6 * D + NPOOL * NPM
    PW = A[:, at:at + NPOOL * 2 * GD].rearrange("p (g k n) -> p g k n", g=NPOOL, k=2)
    at += NPOOL * 2 * GD
    scratch = A[:, at:at + D]
    prod = A[:, at + D:at + 2 * D]
    stat = M["stat"]
    S = STATE * NSEQ
    with ExitStack() as ctx:
        sem = lambda n: new_sem(nc, M, n)
        rows_in, mats_in = sem("pool_rows_landed"), sem("pool_mats_landed")
        summed, scaled, rooted = sem("pool_summed"), sem("pool_scaled"), sem("pool_rooted")
        chain, xn_ready = sem("pool_chain"), sem("pool_xn_ready")
        mixed, mix_copied = sem("pool_mixed"), sem("pool_mix_copied")
        projected, added, stored = sem("pool_projected"), sem("pool_added"), sem("pool_stored")
        block = ctx.enter_context(nc.Block())

        @block.sync
        def _(sp):
            sp.dma_start(gain, I["norm_mix"][0:1, :].broadcast_to([P, D])).then_inc(rows_in, 16)
            sp.dma_start(pscale, I["pool_scale"][0:1, :].broadcast_to([P, D])).then_inc(rows_in, 16)
            sp.dma_start(SP[0:S, :], I["state_pool"][0].rearrange("b r d -> (b r) d")).then_inc(mats_in, 16)
            sp.dma_start(PM, I["pool_mats"]).then_inc(mats_in, 16)
            sp.dma_start(PW, I["pool_w"][0].rearrange("g (k p) n -> p g k n", p=P)).then_inc(mats_in, 16)
            sp.dma_start(O["new_pool_sample"][0, :, 0:STATE - STEPS, :],
                         I["state_pool"][0, :, STEPS:STATE, :]).then_inc(stored, 16)
            sp.wait_ge(xn_ready, NT)
            sp.dma_start(O["new_pool_prompt"][0, 0], XN[P - STATE:P, 1, :]).then_inc(stored, 16)
            for b in range(NSEQ):
                sp.dma_start(O["new_pool_sample"][0, b, STATE - STEPS:STATE, :],
                             XN[b * STEPS:(b + 1) * STEPS, 2, :]).then_inc(stored, 16)
            sp.wait_ge(stored, 16 * (2 + NSEQ))

        @block.scalar
        def _(act):
            row_sums(act, scratch, stat, H, summed, rooted, scaled)
            for c in range(KD):
                act.wait_ge(mixed, c + 1)
                nc.scalar.copy(XT[:, c, :], ps[c % 2][:, 0:TOK]).then_inc(mix_copied, 1)

        @block.vector
        def _(dve):
            st = Steps(dve, chain)
            row_rstd(nc, dve, st, stat, summed, scaled, rooted, D)
            dve.wait_ge(rows_in, 32)
            for i, rows in enumerate(TILE_ROWS):
                nc.vector.scalar_tensor_tensor(XN[0:rows, i, :], H[0:rows, i, :], stat[0:rows, 12 + i:13 + i],
                                               gain[0:rows, :], ALU.mult, ALU.mult).then_inc(xn_ready, 1)
            for i, rows in enumerate(TILE_ROWS):
                for half in range(2):
                    dve.wait_ge(projected, 2 * i + half + 1)
                    cols = slice(half * 512, half * 512 + 512)
                    st.add(nc.vector.tensor_tensor(prod[0:rows, cols], ps[2 + (2 * i + half) % 4][0:rows, :],
                                                   pscale[0:rows, cols], ALU.mult))
                    nc.vector.tensor_tensor(H[0:rows, i, cols], H[0:rows, i, cols], prod[0:rows, cols],
                                            ALU.add).then_inc(added, 1)
            dve.wait_ge(added, 2 * NT)

        @block.tensor
        def _(pe):
            pe.wait_ge(mats_in, 48)
            pe.wait_ge(xn_ready, NT)
            for c in range(KD):
                if c >= 2:
                    pe.wait_ge(mix_copied, c - 1)
                cs, g, bank = slice(c * P, c * P + P), c * P // GD, ps[c % 2]
                pe.matmul(bank[:, 0:SEQ], XN[:, 0, cs], PM[:, g, 0:SEQ], start=True, stop=False)
                pe.matmul(bank[:, 0:SEQ], XN[:, 1, cs], PM[:, g, SEQ:2 * SEQ], start=False, stop=True)
                pe.matmul(bank[:, SEQ:TOK], SP[0:S, cs], PM[0:S, g, 2 * SEQ:2 * SEQ + NEWTOK],
                          start=True, stop=False)
                pe.matmul(bank[:, SEQ:TOK], XN[0:NEWTOK, 2, cs], PM[0:NEWTOK, g, 2 * SEQ + NEWTOK:NPM],
                          start=False, stop=True).then_inc(mixed, 1)
            pe.wait_ge(mix_copied, KD)
            for i, rows in enumerate(TILE_ROWS):
                for half in range(2):
                    n = 2 * i + half
                    if n >= 4:
                        pe.wait_ge(added, n - 3)
                    for g in (2 * half, 2 * half + 1):
                        for k in range(2):
                            last = pe.matmul(ps[2 + n % 4][0:rows, (g % 2) * GD:(g % 2 + 1) * GD],
                                             XT[:, 2 * g + k, i * P:i * P + rows], PW[:, g, k, :],
                                             start=(k == 0), stop=(k == 1))
                    last.then_inc(projected, 1)


def row_rstd(nc, dve, st, stat, summed, scaled, rooted, width):
    dve.wait_ge(summed, NT)
    nc.vector.tensor_scalar(stat[:, 4:4 + NT], stat[:, 0:NT], 1.0 / width, EPS, ALU.mult, ALU.add)\
        .then_inc(scaled, 1)
    dve.wait_ge(rooted, 1)
    st.add(nc.vector.reciprocal(stat[:, 12:12 + NT], stat[:, 8:8 + NT]))


def norm_transpose(nc, I, M, tag, targets):
    H, ps, stat, gT = M["H"], M["ps"], M["stat"], M["gT"]
    Z = M["A"][:, 31248:31248 + NT * D].rearrange("p (i n) -> p i n", i=NT)
    scratch = M["A"][:, 31248 + NT * D:31248 + (NT + 1) * D]
    ident = const(M, "ident")
    with ExitStack() as ctx:
        sem = lambda n: new_sem(nc, M, tag + n)
        summed, scaled, rooted, chain = sem("_summed"), sem("_scaled"), sem("_rooted"), sem("_chain")
        z_ready, turned, copied = sem("_z_ready"), sem("_turned"), sem("_copied")
        consts_in = sem("_constants_landed")
        block = ctx.enter_context(nc.Block())

        @block.sync
        def _(sp):
            sp.dma_start(M["CA"][:, :], I["attention_consts"]).then_inc(consts_in, 16)
            sp.wait_ge(consts_in, 16)

        @block.scalar
        def _(act):
            row_sums(act, scratch, stat, H, summed, rooted, scaled)

        @block.vector
        def _(dve):
            st = Steps(dve, chain)
            row_rstd(nc, dve, st, stat, summed, scaled, rooted, D)
            for i, rows in enumerate(TILE_ROWS):
                nc.vector.tensor_scalar(Z[0:rows, i, :], H[0:rows, i, :], stat[0:rows, 12 + i:13 + i], None,
                                        ALU.mult).then_inc(z_ready, 1)
            n = 0
            for i, rows in enumerate(TILE_ROWS):
                for half in range(2):
                    dve.wait_ge(turned, n + 1)
                    for gi, T in targets:
                        last = nc.vector.tensor_tensor(
                            T[:, 4 * half:4 * half + 4, i * P:i * P + rows],
                            ps[n % 4][:, 0:4 * rows].rearrange("p (k t) -> p k t", k=4),
                            gT[:, gi, 4 * half:4 * half + 4].unsqueeze(2).broadcast_to([P, 4, rows]), ALU.mult)
                    last.then_inc(copied, 1)
                    n += 1
            dve.wait_ge(copied, n)

        @block.tensor
        def _(pe):
            n = 0
            for i, rows in enumerate(TILE_ROWS):
                pe.wait_ge(z_ready, i + 1)
                for half in range(2):
                    if n >= 4:
                        pe.wait_ge(copied, n - 3)
                    for k in range(4):
                        c = 4 * half + k
                        last = pe.transpose(ps[n % 4][:, k * rows:(k + 1) * rows],
                                            Z[0:rows, i, c * P:(c + 1) * P], ident[0:rows, 0:rows])
                    last.then_inc(turned, 1)
                    n += 1


def route(nc, I, M, R, layer):
    XT, A, ps, comb = M["XT"], M["A"], M["ps"], R["comb"]
    at = [0]

    def take(n, k=1):
        v = A[:, at[0]:at[0] + NT * n * k]
        at[0] += NT * n * k
        return v.rearrange("p (i n) -> p i n", i=NT)

    WR = A[:, 4096:4096 + KD * 20].rearrange("p (k n) -> p k n", k=KD)
    L = take(NG + NE)
    gbest, ghot, gkey, gkmax, gexp, gsum, gval = (take(1), take(NG), take(NG), take(1), take(NG), take(1), take(1))
    le, prod = take(EPG), take(NE)
    m1, m2, hot1, hot2, key, kmax, le2 = take(1), take(1), take(EPG), take(EPG), take(EPG), take(1), take(EPG)
    diff, ratio, den, w1, w2, share = take(1), take(1), take(1), take(1), take(1), take(EPG)
    hot2w = take(EPG)
    first = const(M, "first")

    def wide(x, n):
        return x.broadcast_to([P, NT, n])

    with ExitStack() as ctx:
        sem = lambda n: new_sem(nc, M, f"route{layer}_{n}")
        w_in, logits, chain = sem("weights_landed"), sem("logits_ready"), sem("chain")
        exp_in, exp_out = sem("exp_asked"), sem("exp_done")
        member_in, ranks, spilled = sem("members_ready"), sem("ranks_ready"), sem("spilled")
        block = ctx.enter_context(nc.Block())

        @block.sync
        def _(sp):
            sp.dma_start(WR[:, :, 0:NG], I["router_group"][layer].rearrange("(k p) n -> p k n", p=P)).then_inc(w_in, 16)
            sp.dma_start(WR[:, :, NG:], I["router_expert"][layer].rearrange("(k p) n -> p k n", p=P)).then_inc(w_in, 16)
            sp.dma_start(M["spill"], XT[:, :, :].rearrange("p k t -> p (k t)")).then_inc(spilled, 16)
            sp.wait_ge(spilled, 16)

        @block.tensor
        def _(pe):
            pe.wait_ge(w_in, 32)
            for i, rows in enumerate(TILE_ROWS):
                for k in range(KD):
                    last = pe.matmul(ps[0][0:rows, 32 * i:32 * i + NG + NE], XT[:, k, i * P:i * P + rows], WR[:, k, :],
                                     start=(k == 0), stop=(k == KD - 1))
            last.then_inc(logits, 1)
            pe.wait_ge(member_in, 1)
            for i in range(NT + 1):
                out = ps[1][:, i * NE:(i + 1) * NE]
                for j in range(min(i, NT - 1) + 1):
                    own = i == j
                    last = pe.matmul(out, const(M, "before" if own and i < NT else "ones"), R["member"][:, j, :],
                                     start=(j == 0), stop=(j == min(i, NT - 1)))
            last.then_inc(ranks, 1)

        @block.scalar
        def _(act):
            act.wait_ge(exp_in, 1)
            act.activation(gexp, gkey, ACT.Exp).then_inc(exp_out, 1)
            act.wait_ge(exp_in, 2)
            act.activation(ratio, diff, ACT.Exp).then_inc(exp_out, 1)

        @block.vector
        def _(dve):
            st = Steps(dve, chain)
            V = nc.vector
            st.add(V.memset(L, 0.0))
            dve.wait_ge(logits, 1)
            for i, rows in enumerate(TILE_ROWS):
                st.add(V.tensor_copy(L[0:rows, i, :], ps[0][0:rows, 32 * i:32 * i + NG + NE]))
            lg = L[:, :, 0:NG]

            def hot_of(out, src, best, keyt, kmaxt, n):
                st.add(V.tensor_reduce(best, src, AX.X, ALU.max))
                st.add(V.tensor_tensor(keyt, src, wide(best, n), ALU.is_equal))
                st.add(V.tensor_tensor(keyt, keyt, first.unsqueeze(1).broadcast_to([P, NT, n]), ALU.mult))
                st.add(V.tensor_reduce(kmaxt, keyt, AX.X, ALU.max))
                st.add(V.tensor_tensor(out, wide(kmaxt, n), first.unsqueeze(1).broadcast_to([P, NT, n]), ALU.is_equal))

            hot_of(ghot, lg, gbest, gkey, gkmax, NG)
            V.tensor_tensor(gkey, lg, wide(gbest, NG), ALU.subtract).then_inc(exp_in, 1)
            dve.wait_ge(exp_out, 1)
            st.add(V.tensor_reduce(gsum, gexp, AX.X, ALU.add))
            st.add(V.reciprocal(gval, gsum))
            st.add(V.tensor_tensor(prod.rearrange("p i (g e) -> p i g e", g=NG),
                                   L[:, :, NG:].rearrange("p i (g e) -> p i g e", g=NG),
                                   ghot.unsqueeze(3).broadcast_to([P, NT, NG, EPG]), ALU.mult))
            st.add(V.tensor_reduce(le, prod.rearrange("p i (g e) -> p i e g", g=NG), AX.X, ALU.add))
            hot_of(hot1, le, m1, key, kmax, EPG)
            st.add(V.tensor_scalar(le2, hot1, NEG, None, ALU.mult))
            st.add(V.tensor_tensor(le2, le2, le, ALU.add))
            hot_of(hot2, le2, m2, key, kmax, EPG)
            V.tensor_tensor(diff, m2, m1, ALU.subtract).then_inc(exp_in, 1)
            dve.wait_ge(exp_out, 2)
            st.add(V.tensor_scalar(den, ratio, 1.0, None, ALU.add))
            st.add(V.reciprocal(den, den))
            st.add(V.tensor_tensor(w1, den, gval, ALU.mult))
            st.add(V.tensor_tensor(w2, w1, ratio, ALU.mult))
            st.add(V.tensor_tensor(share, hot1, wide(w1, EPG), ALU.mult))
            st.add(V.tensor_tensor(hot2w, hot2, wide(w2, EPG), ALU.mult))
            st.add(V.tensor_tensor(share, share, hot2w, ALU.add))
            st.add(V.tensor_tensor(comb[:, :, :].rearrange("p i (g e) -> p i g e", g=NG),
                                   ghot.unsqueeze(3).broadcast_to([P, NT, NG, EPG]),
                                   share.unsqueeze(2).broadcast_to([P, NT, NG, EPG]), ALU.mult))
            member, rank, over = R["member"], R["rank"], R["comb_over"]
            st.add(V.tensor_tensor(le2, hot1, hot2, ALU.add))
            st.add(V.tensor_tensor(member[:, :, :].rearrange("p i (g e) -> p i g e", g=NG),
                                   ghot.unsqueeze(3).broadcast_to([P, NT, NG, EPG]),
                                   le2.unsqueeze(2).broadcast_to([P, NT, NG, EPG]), ALU.mult))
            V.memset(member[NEWTOK:P, NT - 1, :], 0.0).then_inc(member_in, 1)
            st.add(V.tensor_copy(R["combp"][:, :, :, 0], comb[:, :, :]))
            st.add(V.tensor_tensor(R["combp"][:, :, :, 1], comb[:, :, :], R["combp"][:, :, :, 0].bitcast(F32), ALU.subtract))
            dve.wait_ge(ranks, 1)
            pos = ps[1][:, 0:NT * NE].rearrange("p (i e) -> p i e", i=NT)
            st.add(V.tensor_scalar(rank[:, :, :], pos, 1.0, None, ALU.add))
            st.add(V.tensor_tensor(rank[:, :, :], rank[:, :, :], member[:, :, :], ALU.mult))
            st.add(V.tensor_scalar(rank[:, :, :], rank[:, :, :], -1.0, None, ALU.add))
            st.add(V.tensor_scalar(over[:, :, :], rank[:, :, :], float(CAP), None, ALU.is_ge))
            st.add(V.tensor_tensor(over[:, :, :], over[:, :, :], comb[:, :, :], ALU.mult))
            flag, count, hit = R["list"][0:1, 0:NE], R["list"][0:1, NE:2 * NE], A[0:1, 4400:4400 + MAXOVER * NE]
            st.add(V.tensor_scalar(flag, ps[1][0:1, NT * NE:(NT + 1) * NE], float(CAP), None, ALU.is_gt))
            st.add(V.tensor_copy(count, flag))
            step = 1
            while step < NE:
                tmp = A[0:1, 4380:4380 + NE]
                st.add(V.tensor_copy(tmp, count))
                st.add(V.tensor_tensor(count[:, step:], tmp[:, step:], tmp[:, 0:NE - step], ALU.add))
                step *= 2
            hitv = hit.rearrange("p (k e) -> p k e", k=MAXOVER)
            ranked = const(M, "experts", 1)[:, 0:MAXOVER].unsqueeze(2).broadcast_to([1, MAXOVER, NE])
            st.add(V.tensor_tensor(hitv, count.unsqueeze(1).broadcast_to([1, MAXOVER, NE]), ranked, ALU.subtract))
            st.add(V.tensor_scalar(hit, hit, 1.0, None, ALU.is_equal))
            st.add(V.tensor_tensor(hitv, hitv, flag.unsqueeze(1).broadcast_to([1, MAXOVER, NE]), ALU.mult))
            st.add(V.tensor_tensor(hitv, hitv, const(M, "experts", 1).unsqueeze(1).broadcast_to([1, MAXOVER, NE]), ALU.mult))
            ids = R["list"][0:1, 2 * NE:2 * NE + MAXOVER]
            st.add(V.tensor_reduce(ids, hitv, AX.X, ALU.add))
            st.add(V.tensor_copy(R["over"][0:1, 0:MAXOVER], ids))
            st.add(V.tensor_copy(R["over"][0:1, MAXOVER:MAXOVER + 1], count[:, NE - 1:NE]))


MAXOVER = min(NE, 2 * TOK // (CAP + 1))
NF = FE // P
PIECES = KD + NF
STAGES = 6


def ffn(nc, I, M, layer):
    with ExitStack() as ctx:
        def sb(name, shape, dtype=F32):
            return ctx.enter_context(nc.sbuf_tensor(f"ffn{layer}_{name}", shape, dtype))

        R = {
            "comb": sb("weights", [P, NT, NE]), "comb_over": sb("weights_over", [P, NT, NE]),
            "combp": sb("weight_parts", [P, NT, NE, 2], F32R), "member": sb("member", [P, NT, NE]),
            "rank": sb("rank", [P, NT, NE]), "list": sb("over_list", [1, 3 * NE]),
            "over": sb("over_ids", [1, MAXOVER + 1], I32),
            "xp": sb("x_parts", [P, 2, NT, D], F32R),
            "stage": sb("landing", [P, STAGES, D]),
        }
        landed = [new_sem(nc, M, f"ffn{layer}_piece_landed{n}") for n in range(STAGES)]
        with region(nc, M, f"f{layer}", 8192):
            ffn_input(nc, I, M, R, layer, landed)
            route(nc, I, M, R, layer)
        moe(nc, I, M, R, layer, landed)
        moe_over(nc, I, M, R, layer)


def load_piece(sp, I, R, layer, landed, e, p):
    if p < KD:
        src = I["w_gate_up"][layer][bass.ds(e, 1), p * P:(p + 1) * P, :]
    else:
        src = I["w_down"][layer][bass.ds(e, 1), (p - KD) * P:(p - KD + 1) * P, :]
    sp.dma_start(R["stage"][:, p % STAGES, :], src.rearrange("a p n -> p (a n)")).then_inc(landed[p % STAGES], 16)


def ffn_input(nc, I, M, R, layer, landed):
    H, XT, ps, stat, XP = M["H"], M["XT"], M["ps"], M["stat"], R["xp"]
    XN = M["A"][:, 0:NT * D].rearrange("p (i n) -> p i n", i=NT)
    scratch, gain = M["A"][:, 3 * D:4 * D], M["A"][:, 4 * D:5 * D]
    ident = const(M, "ident")
    with ExitStack() as ctx:
        sem = lambda n: new_sem(nc, M, f"ffnin{layer}_" + n)
        gain_in, summed, scaled, rooted, chain = (sem("gain_landed"), sem("summed"), sem("scaled"), sem("rooted"),
                                                  sem("chain"))
        xn_ready, high, turned, by_dve, by_act = (sem("xn_ready"), sem("high_ready"), sem("turned"),
                                                  sem("copied_by_dve"), sem("copied_by_act"))
        block = ctx.enter_context(nc.Block())

        @block.sync
        def _(sp):
            sp.dma_start(gain, I["norm_ffn"][layer:layer + 1, :].broadcast_to([P, D])).then_inc(gain_in, 16)
            for p in range(STAGES):
                load_piece(sp, I, R, layer, landed, 0, p)

        @block.scalar
        def _(act):
            row_sums(act, scratch, stat, H, summed, rooted, scaled)
            for i, rows in enumerate(TILE_ROWS):
                act.wait_ge(xn_ready, i + 1)
                nc.scalar.copy(XP[0:rows, 0, i, :], XN[0:rows, i, :]).then_inc(high, 1)
                act.wait_ge(turned, 2 * i + 2)
                nc.scalar.copy(XT[:, 4:8, i * P:i * P + rows],
                               ps[(2 * i + 1) % 4][:, 0:4 * rows].rearrange("p (k t) -> p k t", k=4)).then_inc(by_act, 1)

        @block.vector
        def _(dve):
            st = Steps(dve, chain)
            row_rstd(nc, dve, st, stat, summed, scaled, rooted, D)
            dve.wait_ge(gain_in, 16)
            for i, rows in enumerate(TILE_ROWS):
                nc.vector.scalar_tensor_tensor(XN[0:rows, i, :], H[0:rows, i, :], stat[0:rows, 12 + i:13 + i],
                                               gain[0:rows, :], ALU.mult, ALU.mult).then_inc(xn_ready, 1)
            for i, rows in enumerate(TILE_ROWS):
                dve.wait_ge(turned, 2 * i + 1)
                nc.vector.tensor_copy(XT[:, 0:4, i * P:i * P + rows],
                                      ps[(2 * i) % 4][:, 0:4 * rows].rearrange("p (k t) -> p k t", k=4)).then_inc(by_dve, 1)
                dve.wait_ge(high, i + 1)
                nc.vector.tensor_tensor(XP[0:rows, 1, i, :], XN[0:rows, i, :], XP[0:rows, 0, i, :].bitcast(F32),
                                        ALU.subtract)

        @block.tensor
        def _(pe):
            n = 0
            for i, rows in enumerate(TILE_ROWS):
                pe.wait_ge(xn_ready, i + 1)
                for half in range(2):
                    if n >= 4:
                        pe.wait_ge((by_dve, by_act)[half], i - 1)
                    for k in range(4):
                        c = 4 * half + k
                        last = pe.transpose(ps[n % 4][:, k * rows:(k + 1) * rows],
                                            XN[0:rows, i, c * P:(c + 1) * P], ident[0:rows, 0:rows])
                    last.then_inc(turned, 1)
                    n += 1


def reach(eng, sem, value):
    if not isinstance(value, int) or value > 0:
        eng.wait_ge(sem, value)


def over_experts(eng, body):
    for e in (0, 1):
        body(e, e % 2)
    with eng.Fori(1, NE // 2 - 1) as i:
        for s in range(2):
            body(i * 2 + s, s)
    for e in (NE - 2, NE - 1):
        body(e, e % 2)


def moe(nc, I, M, R, layer, landed):
    H, ps, XP, STG = M["H"], M["ps"], R["xp"], R["stage"]
    ident, slots = const(M, "ident"), const(M, "slots")
    is_last = lambda e: isinstance(e, int) and e == NE - 1
    with ExitStack() as ctx:
        def sb(name, shape, dtype=F32):
            return ctx.enter_context(nc.sbuf_tensor(f"moe{layer}_{name}", shape, dtype))

        W = sb("weight_parts", [P, PIECES, 2, D], F32R)
        SG = sb("gather", [P, 2, NT, 4 * CAP], F32R)
        XE = sb("gathered_rows", [P, D])
        XS = sb("gatheredT", [P, KD, P], F32R)
        GE = sb("gate_up_rows", [P, D])
        GT = sb("gate_upT", [P, 2, NF * CAP])
        SIL, HR = sb("silu", [P, NF * CAP]), sb("hidden", [P, NF * CAP])
        HT = sb("hidden_parts", [P, NF, P], F32R)
        ST = sb("scatter", [P, 2, TOK], F32R)
        YP = sb("down_parts", [P, 2, 2, D], F32R)
        WS = sb("slot_weight", [P, 2])
        sem = lambda n: new_sem(nc, M, f"moe{layer}_{n}")
        high, low, used = sem("high_part_ready"), sem("low_part_ready"), sem("piece_used")
        sg, gathered, xe, xturned = sem("gather_ready"), sem("rows_gathered"), sem("rows_copied"), sem("rows_turned")
        xs_act, xs_dve = sem("gatheredT_by_act"), sem("gatheredT_by_dve")
        ge, gturned, gate, up, silu, hidden = (sem("gate_up_copied"), sem("gate_up_turned"), sem("gate_summed"),
                                               sem("up_summed"), sem("silu_ready"), sem("hidden_ready"))
        hh, hl, sturned, st_ready, wsum, ws = (sem("hidden_high"), sem("hidden_low"), sem("scatter_turned"),
                                               sem("scatter_ready"), sem("slot_weight_summed"), sem("slot_weight_ready"))
        yh, yl, scattered, added = sem("down_high"), sem("down_low"), sem("scattered"), sem("added")
        NY = 2 * NT
        block = ctx.enter_context(nc.Block())

        @block.sync
        def _(sp):
            def expert(e, s):
                for p in range(PIECES):
                    if isinstance(e, int) and e == 0 and p < STAGES:
                        continue
                    reach(sp, low, e * PIECES + (p - STAGES + 1))
                    load_piece(sp, I, R, layer, landed, e, p)
            over_experts(sp, expert)

        @block.tensor
        def _(pe):
            def gather(e, s):
                pe.wait_ge(sg, e + 1)
                reach(pe, xe, e * 2)
                for half in range(2):
                    for part in range(2):
                        for i, rows in enumerate(TILE_ROWS):
                            lo = P if part == 0 else 0
                            last = pe.matmul(ps[2 + half][:, :], SG[0:rows, s, i, lo:lo + P],
                                             XP[0:rows, part, i, half * 512:(half + 1) * 512],
                                             start=(part == 0 and i == 0), stop=(part == 1 and i == NT - 1))
                last.then_inc(gathered, 1)

            def turn_gathered(e, s):
                for half in range(2):
                    pe.wait_ge(xe, e * 2 + half + 1)
                    reach(pe, (gate, up)[half], e)
                    for k in range(4):
                        c = 4 * half + k
                        last = pe.transpose(ps[4 + half][:, k * P:(k + 1) * P], XE[:, c * P:(c + 1) * P], ident)
                    last.then_inc(xturned, 1)

            def gate_up(e, s):
                pe.wait_ge(xs_act, e + 1)
                pe.wait_ge(xs_dve, e + 1)
                reach(pe, ge, e * 2)
                for k in range(KD):
                    pe.wait_ge(low, e * PIECES + (k + 1))
                    for part in range(2):
                        for half in range(2):
                            last = pe.matmul(ps[half][:, :], XS[:, k, :], W[:, k, part, half * 512:(half + 1) * 512],
                                             start=(k == 0 and part == 0), stop=(k == KD - 1 and part == 1))
                    last.then_inc(used, 1)

            def scatter(e):
                pe.wait_ge(yl, e * 2)
                for t, rows in enumerate(TILE_ROWS):
                    for half in range(2):
                        m = 2 * t + half
                        if m >= 2:
                            pe.wait_ge(added, e * NT + (m - 1 - NY))
                        for x in range(2):
                            for part in range(2):
                                last = pe.matmul(ps[2 + half][0:rows, :], ST[:, x, t * P:t * P + rows],
                                                 YP[:, x, part, half * 512:(half + 1) * 512],
                                                 start=(x + part == 0), stop=(x + part == 2))
                        last.then_inc(scattered, 1)

            def turn_gate_up(e):
                for half in range(2):
                    pe.wait_ge(ge, e * 2 + half + 1)
                    pe.wait_ge((xs_act, xs_dve)[half], e + 1)
                    for f in range(NF):
                        last = pe.transpose(ps[4 + half][:, f * P:(f + 1) * P],
                                            GE[:, half * 512 + f * P:half * 512 + (f + 1) * P], ident)
                    last.then_inc(gturned, 1)

            def turn_scatter(e, s):
                reach(pe, yl, e * 2)
                for i, rows in enumerate(TILE_ROWS):
                    last = pe.transpose(ps[6][:, i * P:i * P + rows], SG[0:rows, s, i, CAP:3 * CAP].bitcast(F32),
                                        ident[0:rows, 0:rows])
                last.then_inc(sturned, 1)
                for i, rows in enumerate(TILE_ROWS):
                    rhs = R["combp"][0:rows, i, bass.ds(e, 1), :].rearrange("p a b -> p (a b)")
                    last = pe.matmul(ps[7][:, 0:2], SG[0:rows, s, i, CAP:3 * CAP], rhs, start=(i == 0), stop=(i == NT - 1))
                last.then_inc(wsum, 1)

            def down(e):
                pe.wait_ge(hh, e + 1)
                pe.wait_ge(hl, e + 1)
                pe.wait_ge(st_ready, e + 1)
                pe.wait_ge(ws, e + 1)
                for f in range(NF):
                    pe.wait_ge(low, e * PIECES + (KD + f + 1))
                    for part in range(2):
                        for half in range(2):
                            last = pe.matmul(ps[6 + half][:, :], HT[:, f, :],
                                             W[:, KD + f, part, half * 512:(half + 1) * 512],
                                             start=(f == 0 and part == 0), stop=(f == NF - 1 and part == 1))
                    last.then_inc(used, 1)

            def expert(e, s):
                gate_up(e, s)
                if s == 0 and not (isinstance(e, int) and e == 0):
                    scatter(e)
                if not is_last(e):
                    reach(pe, added, after_scatter(e, s))
                    gather(e + 1, 1 - s)
                turn_gate_up(e)
                turn_scatter(e, s)
                if not is_last(e):
                    turn_gathered(e + 1, 1 - s)
                down(e)

            def after_scatter(e, s):
                return (e - s) * NT

            gather(0, 0)
            turn_gathered(0, 0)
            over_experts(pe, expert)
            scatter(NE)

        @block.scalar
        def _(act):
            A = nc.scalar

            def high_part(e, p):
                act.wait_ge(landed[p % STAGES], e * (16 * PIECES // STAGES) + (16 * (p // STAGES) + 16))
                reach(act, used, e * PIECES + (p + 1 - PIECES))
                A.copy(W[:, p, 0, :], STG[:, p % STAGES, :]).then_inc(high, 1)

            def copy_rows(e, s):
                for half in range(2):
                    act.wait_ge(gathered, e + 1)
                    reach(act, xturned, e * 2)
                    A.copy(XE[:, half * 512:(half + 1) * 512], ps[2 + half][:, :]).then_inc(xe, 1)

            def copy_turned_rows(e):
                act.wait_ge(xturned, e * 2 + 1)
                reach(act, used, (e - 1) * PIECES + KD if not isinstance(e, int) or e else 0)
                A.copy(XS[:, 0:4, :].rearrange("p k t -> p (k t)"), ps[4][:, :]).then_inc(xs_act, 1)

            def down_high(e, s):
                for half in range(2):
                    act.wait_ge(used, (e + 1) * PIECES)
                    if s == 0:
                        reach(act, scattered, e * NT)
                    A.activation(YP[:, s, 0, half * 512:(half + 1) * 512], ps[6 + half][:, :], ACT.Copy,
                                 scale=WS[:, s:s + 1]).then_inc(yh, 1)

            def expert(e, s):
                if not (isinstance(e, int) and e == 0):
                    down_high(e - 1, 1 - s)
                for p in range(KD, PIECES):
                    high_part(e, p)
                for half in range(2):
                    act.wait_ge(used, e * PIECES + KD)
                    reach(act, gturned, e * 2)
                    A.copy(GE[:, half * 512:(half + 1) * 512], ps[half][:, :]).then_inc(ge, 1)
                if not is_last(e):
                    copy_rows(e + 1, 1 - s)
                    high_part(e + 1, 0)
                    high_part(e + 1, 1)
                act.wait_ge(gate, e + 1)
                reach(act, hidden, e)
                act.activation(SIL[:, :], GT[:, 0, :], ACT.Silu).then_inc(silu, 1)
                act.wait_ge(hidden, e + 1)
                reach(act, used, e * PIECES)
                A.copy(HT[:, :, 0:CAP], HR[:, :].rearrange("p (f t) -> p f t", f=NF)).then_inc(hh, 1)
                if not is_last(e):
                    copy_turned_rows(e + 1)
                act.wait_ge(sturned, e + 1)
                reach(act, scattered, (e - s) * NT)
                A.copy(ST[:, s, :], ps[6][:, 0:TOK]).then_inc(st_ready, 1)
                if not is_last(e):
                    for p in range(2, KD):
                        high_part(e + 1, p)

            copy_rows(0, 0)
            copy_turned_rows(0)
            for p in range(KD):
                high_part(0, p)
            over_experts(act, expert)
            down_high(NE - 1, 1)

        @block.vector
        def _(dve):
            V = nc.vector

            def low_part(e, p):
                dve.wait_ge(high, e * PIECES + (p + 1))
                V.tensor_tensor(W[:, p, 1, :], STG[:, p % STAGES, :], W[:, p, 0, :].bitcast(F32), ALU.subtract)\
                    .then_inc(low, 1)

            def build_gather(e, s):
                reach(dve, sturned, e - 1)
                reach(dve, wsum, e - 1)
                V.tensor_tensor(SG[:, s, :, CAP:3 * CAP].rearrange("p i (r k) -> p i r k", r=2),
                                slots.unsqueeze(1).unsqueeze(1).broadcast_to([P, NT, 2, CAP]),
                                R["rank"][:, :, bass.ds(e, 1)].unsqueeze(2).broadcast_to([P, NT, 2, CAP]),
                                ALU.is_equal).then_inc(sg, 1)

            def down_low(e, s):
                for half in range(2):
                    dve.wait_ge(yh, e * 2 + half + 1)
                    cols = slice(half * 512, (half + 1) * 512)
                    V.scalar_tensor_tensor(YP[:, s, 1, cols], ps[6 + half][:, :], WS[:, s:s + 1],
                                           YP[:, s, 0, cols].bitcast(F32), ALU.mult, ALU.subtract).then_inc(yl, 1)

            def add_sums(e):
                for t, rows in enumerate(TILE_ROWS):
                    for half in range(2):
                        m = 2 * t + half
                        dve.wait_ge(scattered, e * NT + (m + 1 - NY))
                        hv = H[0:rows, t, half * 512:(half + 1) * 512]
                        V.tensor_tensor(hv, ps[2 + half][0:rows, :], hv, ALU.add).then_inc(added, 1)

            def expert(e, s):
                low_part(e, KD)
                low_part(e, KD + 1)
                if not (isinstance(e, int) and e == 0):
                    down_low(e - 1, 1 - s)
                low_part(e, KD + 2)
                low_part(e, KD + 3)
                if s == 0 and not (isinstance(e, int) and e == 0):
                    add_sums(e)
                for half in range(2):
                    dve.wait_ge(gturned, e * 2 + half + 1)
                    if half == 0:
                        reach(dve, hidden, e)
                    V.tensor_reduce(GT[:, half, :].rearrange("p (f t) -> p f t", f=NF),
                                    ps[4 + half][:, :].rearrange("p (f a t) -> p f t a", f=NF, a=2), AX.X, ALU.add)\
                        .then_inc((gate, up)[half], 1)
                if not is_last(e):
                    low_part(e + 1, 0)
                    low_part(e + 1, 1)
                dve.wait_ge(silu, e + 1)
                dve.wait_ge(up, e + 1)
                reach(dve, hl, e)
                reach(dve, hh, e)
                V.tensor_tensor(HR[:, :], SIL[:, :], GT[:, 1, :], ALU.mult).then_inc(hidden, 1)
                dve.wait_ge(hh, e + 1)
                V.tensor_tensor(HT[:, :, CAP:2 * CAP], HR[:, :].rearrange("p (f t) -> p f t", f=NF),
                                HT[:, :, 0:CAP].bitcast(F32), ALU.subtract).then_inc(hl, 1)
                dve.wait_ge(wsum, e + 1)
                reach(dve, yl, e * 2)
                V.tensor_reduce(WS[:, s:s + 1], ps[7][:, 0:2], AX.X, ALU.add).then_inc(ws, 1)
                if not is_last(e):
                    copy_turned(e + 1)
                    for p in range(2, KD):
                        low_part(e + 1, p)
                    if not (isinstance(e, int) and e >= NE - 2):
                        build_gather(e + 2, s)

            def copy_turned(e):
                dve.wait_ge(xturned, e * 2 + 2)
                V.tensor_copy(XS[:, 4:8, :].rearrange("p k t -> p (k t)"), ps[5][:, :]).then_inc(xs_dve, 1)

            zeroed = new_sem(nc, M, f"moe{layer}_zeroed")
            V.memset(SG[:, :, :, 0:CAP].bitcast(F32), 0.0).then_inc(zeroed, 1)
            V.memset(SG[:, :, :, 3 * CAP:].bitcast(F32), 0.0).then_inc(zeroed, 1)
            dve.wait_ge(zeroed, 2)
            build_gather(0, 0)
            build_gather(1, 1)
            copy_turned(0)
            for p in range(KD):
                low_part(0, p)
            over_experts(dve, expert)
            down_low(NE - 1, 1)
            add_sums(NE)
            dve.wait_ge(added, NE // 2 * NY)


def moe_over(nc, I, M, R, layer):
    H, ps, comb = M["H"], M["ps"], R["comb_over"]
    with ExitStack() as ctx:
        def sb(name, shape, dtype=F32):
            return ctx.enter_context(nc.sbuf_tensor(f"over{layer}_{name}", shape, dtype))

        XT, GU, DN = sb("xT", [P, KD, TOK]), sb("gate_up", [P, KD, 2 * FE]), sb("down", [P, NF, D])
        SIL, HDN = sb("silu", [P, NF, TOK]), sb("hidden", [P, NF, TOK])
        sem = lambda n: new_sem(nc, M, f"over{layer}_{n}")
        x_in, w_in, turn = sem("x_landed"), sem("weights_landed"), sem("expert_turn")
        pair, silu, hid, y_ready, y_added = (sem("gate_up_ready"), sem("silu_ready"), sem("hidden_ready"),
                                             sem("y_ready"), sem("y_added"))
        block = ctx.enter_context(nc.Block())

        def over_list(eng, body, before=None):
            n = eng.value_load(R["over"][0:1, MAXOVER:MAXOVER + 1], min_val=0, max_val=MAXOVER)
            with eng.If(n > 0):
                if before:
                    before()
                with eng.Fori(0, MAXOVER) as k:
                    with eng.If(n > k):
                        e = eng.value_load(R["over"][0:1, bass.ds(k, 1)], min_val=0, max_val=NE - 1)
                        body(k, e)

        @block.sync
        def _(sp):
            def load_x():
                sp.dma_start(XT[:, :, :].rearrange("p k t -> p (k t)"), M["spill"]).then_inc(x_in, 16)

            def load(k, e):
                sp.wait_ge(turn, k + 1)
                sp.dma_start(GU[:, :, :], I["w_gate_up"][layer][bass.ds(e, 1)].rearrange("a (k p) n -> p (a k) n", p=P))\
                    .then_inc(w_in, 16)
                sp.dma_start(DN[:, :, :], I["w_down"][layer][bass.ds(e, 1)].rearrange("a (k p) n -> p (a k) n", p=P))\
                    .then_inc(w_in, 16)
            over_list(sp, load, load_x)

        @block.tensor
        def _(pe):
            def expert(k, e):
                pe.wait_ge(turn, k + 1)
                pe.wait_ge(x_in, 16)
                pe.wait_ge(w_in, k * 32 + 32)
                for f in range(NF):
                    for u in range(2):
                        for c in range(KD):
                            last = pe.matmul(ps[2 * f + u][:, 0:TOK], GU[:, c, u * FE + f * P:u * FE + (f + 1) * P],
                                             XT[:, c, :], start=(c == 0), stop=(c == KD - 1))
                    last.then_inc(pair, 1)
                pe.wait_ge(hid, k * NF + NF)
                for t, rows in enumerate(TILE_ROWS):
                    for half in range(2):
                        for f in range(NF):
                            last = pe.matmul(ps[2 * t + half][0:rows, :], HDN[:, f, t * P:t * P + rows],
                                             DN[:, f, half * 512:(half + 1) * 512], start=(f == 0), stop=(f == NF - 1))
                        last.then_inc(y_ready, 1)
            over_list(pe, expert)

        @block.scalar
        def _(act):
            def expert(k, e):
                for f in range(NF):
                    act.wait_ge(pair, k * NF + (f + 1))
                    act.activation(SIL[:, f, :], ps[2 * f][:, 0:TOK], ACT.Silu).then_inc(silu, 1)
            over_list(act, expert)

        @block.vector
        def _(dve):
            def expert(k, e):
                for f in range(NF):
                    dve.wait_ge(silu, k * NF + (f + 1))
                    nc.vector.tensor_tensor(HDN[:, f, :], ps[2 * f + 1][:, 0:TOK], SIL[:, f, :], ALU.mult).then_inc(hid, 1)
                for t, rows in enumerate(TILE_ROWS):
                    for half in range(2):
                        dve.wait_ge(y_ready, k * (2 * NT) + (2 * t + half + 1))
                        hv = H[0:rows, t, half * 512:(half + 1) * 512]
                        c = comb[0:rows, t, bass.ds(e, 1)]
                        nc.vector.scalar_tensor_tensor(hv, ps[2 * t + half][0:rows, :], c, hv, ALU.mult, ALU.add)\
                            .then_inc(y_added, 1)
                dve.wait_ge(y_added, k * (2 * NT) + 2 * NT)
                nc.vector.memset(SIL[0:1, 0, 0:1], 0.0).then_inc(turn, 1)

            def first_turn():
                nc.vector.memset(SIL[0:1, 0, 0:1], 0.0).then_inc(turn, 1)
            over_list(dve, expert, first_turn)


def store_result(nc, O, M):
    with ExitStack() as ctx:
        stored = new_sem(nc, M, "y_stored")
        block = ctx.enter_context(nc.Block())

        @block.sync
        def _(sp):
            for i, rows in enumerate(TILE_ROWS):
                dst = O["y_prompt"][0, i * P:(i + 1) * P, :] if i < 2 else O["y_sample"].rearrange("b t d -> (b t) d")
                sp.dma_start(dst, M["H"][0:rows, i, :]).then_inc(stored, 16)
            sp.wait_ge(stored, 16 * NT)


def view(M, at, *dims):
    n = 1
    for d in dims:
        n *= d
    names = "abcd"[:len(dims)]
    v = M["A"][:, at:at + n]
    if len(dims) == 1:
        return v
    return v.rearrange(f"p ({' '.join(names)}) -> p {' '.join(names)}", **dict(zip(names, dims)))


def stage_attention(nc, I, O, M):
    norm_transpose(nc, I, M, "mix1", [(2, M["XT"]), (3, view(M, Map.XT2, KD, TOK))])
    project(nc, I, O, M)
    turn_heads(nc, I, M)
    compress_prompt(nc, I, O, M)
    compress_samples(nc, I, M)
    attend_samples(nc, I, M)
    attend_prompt(nc, I, M)
    output_projection(nc, M)


def project(nc, I, O, M):
    XT, XT2, ps, stat = M["XT"], view(M, Map.XT2, KD, TOK), M["ps"], M["stat"]
    WKV, WQG = view(M, Map.WKV, KD, 6 * NKV * HD), view(M, Map.WQG, KD, NH * HD + 3 * NH)
    HEADS = view(M, Map.HEADS, NT, 24, HD)
    KV, WN = view(M, Map.KVROWS, NT, 4 * NKV * HD), view(M, Map.WINROWS, NT, 2 * NKV * HD)
    QR = view(M, Map.QROPE, NT, NH, HD)
    GAIN, SQ = view(M, Map.GAIN24, 24, HD), view(M, Map.SQ, 24, HD)
    t1, t2 = view(M, Map.ROT, 24, HD // 2), view(M, Map.ROT + 24 * HD // 2, 24, HD // 2)
    gates = M["gates"]
    cos = const(M, "cos").rearrange("p (i d) -> p i d", i=NT)
    sin = const(M, "sin").rearrange("p (i d) -> p i d", i=NT)
    KW = NKV * HD
    chunks = [(XT2, WKV, 0, 512), (XT2, WKV, 512, 512), (XT2, WKV, 1024, 512),
              (XT, WQG, 0, 512), (XT, WQG, 512, 512), (XT, WQG, 1024, 3 * NH)]
    NC = len(chunks)
    with ExitStack() as ctx:
        sem = lambda n: new_sem(nc, M, "proj_" + n)
        kv_in, q_in, gains_in = sem("kv_weights_landed"), sem("q_weights_landed"), sem("gains_landed")
        product, copied, parts = sem("product_ready"), sem("product_copied"), sem("part_copied")
        squared, scaled, rooted = sem("squares_ready"), sem("mean_ready"), sem("root_ready")
        chain, roped, stored = sem("chain"), sem("rows_roped"), sem("rows_stored")
        block = ctx.enter_context(nc.Block())

        @block.sync
        def _(sp):
            for h in range(2):
                ks = slice(4 * h, 4 * h + 4)
                sp.dma_start(WKV[:, ks, :], I["w_kv"].rearrange("(k p) n -> p k n", p=P)[:, ks, :]).then_inc(kv_in, 16)
            sp.dma_start(WQG, I["w_qg"][0].rearrange("(k p) n -> p k n", p=P)).then_inc(q_in, 16)
            for lo, hi, src in ((0, 4, I["k_norm"][1:2, :]), (4, 8, I["k_norm"][2:3, :]), (8, 24, I["q_norm"][0:1, :])):
                sp.dma_start(GAIN[:, lo:hi, :], src.unsqueeze(1).broadcast_to([1, hi - lo, HD])
                             .broadcast_to([P, hi - lo, HD])).then_inc(gains_in, 16)
            sp.dma_start(O["new_win_sample"][:, 0:WIN - STEPS], I["state_win"][:, STEPS:WIN]).then_inc(stored, 16)
            for i in range(NT):
                sp.wait_ge(roped, i + 1)
                if i < 2:
                    sp.dma_start(O["new_kv_prompt"][0, i * P:(i + 1) * P].rearrange("t s g d -> t (s g d)"),
                                 KV[:, i, :]).then_inc(stored, 16)
                    sp.dma_start(O["new_win_prompt"][0, i * P:(i + 1) * P].rearrange("t s g d -> t (s g d)"),
                                 WN[:, i, :]).then_inc(stored, 16)
                else:
                    sp.dma_start(O["new_kv_sample"].rearrange("b t s g d -> (b t) (s g d)"),
                                 KV[0:NEWTOK, i, :]).then_inc(stored, 16)
                    for b in range(NSEQ):
                        sp.dma_start(O["new_win_sample"][b, WIN - STEPS:WIN].rearrange("t s g d -> t (s g d)"),
                                     WN[b * STEPS:(b + 1) * STEPS, i, :]).then_inc(stored, 16)
            sp.wait_ge(stored, 16 * (6 + NSEQ))

        @block.tensor
        def _(pe):
            n = 0
            for i, rows in enumerate(TILE_ROWS):
                for c, (T, W, at, w) in enumerate(chunks):
                    if i == 0 and c == 0:
                        pe.wait_ge(kv_in, 32)
                    if i == 0 and c == 3:
                        pe.wait_ge(q_in, 16)
                    if n >= 8:
                        pe.wait_ge(copied, n - 7)
                    for k in range(KD):
                        last = pe.matmul(ps[n % 8][0:rows, 0:w], T[:, k, i * P:i * P + rows], W[:, k, at:at + w],
                                         start=(k == 0), stop=(k == KD - 1))
                    last.then_inc(product, 1)
                    n += 1

        @block.scalar
        def _(act):
            for i, rows in enumerate(TILE_ROWS):
                flat = HEADS[0:rows, i].rearrange("p h d -> p (h d)")
                dests = [[(KV[0:rows, i, 0:512], 0)],
                         [(flat[:, 0:KW], 0), (KV[0:rows, i, 3 * KW:4 * KW], KW)],
                         [(flat[:, KW:2 * KW], 0), (WN[0:rows, i, KW:2 * KW], KW)],
                         [(HEADS[0:rows, i, 8:16].rearrange("p (h g) d -> p g h d", g=2), 0)],
                         [(HEADS[0:rows, i, 16:24].rearrange("p (h g) d -> p g h d", g=2), 0)],
                         [(gates[0:rows, i, :], 0)]]
                for c in range(NC):
                    n = i * NC + c
                    act.wait_ge(product, n + 1)
                    for m, (dst, at) in enumerate(dests[c]):
                        if len(dst.shape) == 4:
                            src = ps[n % 8][0:rows, :].rearrange("p (g h d) -> p g h d", g=2, h=HPG)
                        else:
                            src = ps[n % 8][0:rows, at:at + dst.shape[1]]
                        ins = nc.scalar.copy(dst, src)
                        ins.then_inc(copied if m == len(dests[c]) - 1 else parts, 1)
                act.wait_ge(copied, (i + 1) * NC)
                act.wait_ge(parts, 2 * (i + 1))
                if i:
                    act.wait_ge(scaled, i)
                act.activation(SQ[0:rows].rearrange("p h d -> p (h d)"), flat, ACT.Square).then_inc(squared, 1)
                act.wait_ge(scaled, i + 1)
                act.activation(stat[0:rows, 16:40], stat[0:rows, 40:64], ACT.Sqrt).then_inc(rooted, 1)
            act.activation(gates[:, :, :], gates[:, :, :], ACT.Sigmoid).then_inc(parts, 1)

        @block.vector
        def _(dve):
            V = nc.vector
            st = Steps(dve, chain)
            dve.wait_ge(gains_in, 48)
            for i, rows in enumerate(TILE_ROWS):
                r = slice(0, rows)
                dve.wait_ge(squared, i + 1)
                st.add(V.tensor_reduce(stat[r, 16:40], SQ[r], AX.X, ALU.add))
                V.tensor_scalar(stat[r, 40:64], stat[r, 16:40], 1.0 / HD, EPS, ALU.mult, ALU.add).then_inc(scaled, 1)
                dve.wait_ge(rooted, i + 1)
                st.add(V.reciprocal(stat[r, 40:64], stat[r, 16:40]))
                x = HEADS[r, i]
                st.add(V.tensor_tensor(x, x, stat[r, 40:64].unsqueeze(2).broadcast_to([rows, 24, HD]), ALU.mult))
                st.add(V.tensor_tensor(x, x, GAIN[r], ALU.mult))
                x1, x2 = x[:, :, 0:HD // 2], x[:, :, HD // 2:HD]
                c = cos[r, i].unsqueeze(1).broadcast_to([rows, 24, HD // 2])
                s = sin[r, i].unsqueeze(1).broadcast_to([rows, 24, HD // 2])
                dst = [(0, 4, KV[r, i, 2 * KW:3 * KW].rearrange("p (g d) -> p g d", g=NKV)),
                       (4, 8, WN[r, i, 0:KW].rearrange("p (g d) -> p g d", g=NKV)), (8, 24, QR[r, i])]
                for lo, first, second, op in ((0, x1, x2, ALU.subtract), (HD // 2, x2, x1, ALU.add)):
                    st.add(V.tensor_tensor(t1[r], first, c, ALU.mult))
                    st.add(V.tensor_tensor(t2[r], second, s, ALU.mult))
                    for m, (a, b, d) in enumerate(dst):
                        ins = V.tensor_tensor(d[:, :, lo:lo + HD // 2], t1[r, a:b], t2[r, a:b], op)
                        if lo and m == 2:
                            ins.then_inc(roped, 1)
                            dve.wait_ge(roped, i + 1)
                        else:
                            st.add(ins)


def turn_heads(nc, I, M):
    ps, gates = M["ps"], M["gates"]
    HEADS, QR = view(M, Map.HEADS, NT, 24, HD), view(M, Map.QROPE, NT, NH, HD)
    KV, WN = view(M, Map.KVROWS, NT, 4, NKV * HD), view(M, Map.WINROWS, NT, 2, NKV * HD)
    QT = [view(M, Map.QNT, 2, HPG, SEQ), view(M, Map.QRT, 2, HPG, SEQ)]
    QS = [view(M, Map.QSN, 2, HPG, NEWTOK), view(M, Map.QSR, 2, HPG, NEWTOK)]
    KTP, KTN = view(M, Map.KTP, 4, SEQ), view(M, Map.KTN, 4, NEWTOK)
    VP, VNEW = view(M, Map.VP, 2, 2, NKV, 3 * HD), view(M, Map.VNEW, NKV * HD)
    GS, GL = view(M, Map.GS, 3, NSEQ), view(M, Map.GATEL, 3, NH, STEPS)
    ident, stepsel, seqsel = const(M, "ident"), const(M, "stepsel", NEWTOK), const(M, "seqsel", NEWTOK)

    def query_pair(which, i, j, h):
        rows = TILE_ROWS[i]
        src, at = ((HEADS, 8), (QR, 0))[which]
        a = at + 2 * HPG * j + 2 * h
        return src[0:rows, i, a:a + 2, :].rearrange("p g d -> p (g d)")

    def key_pair(br, i, j):
        rows = TILE_ROWS[i]
        src = KV[0:rows, i, 2] if br == 0 else WN[0:rows, i, 0]
        return src[:, j * P:(j + 1) * P]

    batches = []
    for i in range(2):
        for which in range(2):
            for j in range(2):
                batches.append(([query_pair(which, i, j, h) for h in range(HPG)], P,
                                QT[which][:, j, :, i * P:(i + 1) * P]))
        batches.append(([key_pair(br, i, j) for br in range(2) for j in range(2)], P, KTP[:, :, i * P:(i + 1) * P]))
    for which in range(2):
        for j in range(2):
            batches.append(([query_pair(which, 2, j, h) for h in range(HPG)], NEWTOK, QS[which][:, j]))
    batches.append(([key_pair(br, 2, j) for br in range(2) for j in range(2)], NEWTOK, KTN))
    NB = len(batches)
    with ExitStack() as ctx:
        sem = lambda n: new_sem(nc, M, "turn_" + n)
        turned, by_dve, by_act = sem("batch_turned"), sem("copied_by_dve"), sem("copied_by_act")
        zeroed, gl, gsum = sem("zeroed"), sem("gate_rows_spread"), sem("gates_summed")
        block = ctx.enter_context(nc.Block())

        @block.tensor
        def _(pe):
            for n, (srcs, w, dst) in enumerate(batches):
                if n >= 6:
                    pe.wait_ge(by_act if n % 2 else by_dve, (n - 6) // 2 + 1)
                for m, src in enumerate(srcs):
                    last = pe.transpose(ps[n % 6][:, m * w:(m + 1) * w], src, ident[0:w, 0:w])
                last.then_inc(turned, 1)
            pe.wait_ge(gl, 3)
            for br in range(3):
                last = pe.matmul(ps[6][:, br * NSEQ:(br + 1) * NSEQ], GL[0:NEWTOK, br].rearrange("p h t -> p (h t)"),
                                 seqsel, start=True, stop=True)
            last.then_inc(gsum, 1)

        def copy(n, on_act):
            srcs, w, dst = batches[n]
            src = ps[n % 6][:, 0:4 * w].rearrange("p (m t) -> p m t", m=4)
            return nc.scalar.copy(dst, src) if on_act else nc.vector.tensor_copy(dst, src)

        @block.scalar
        def _(act):
            for n in range(1, NB, 2):
                act.wait_ge(turned, n + 1)
                copy(n, True).then_inc(by_act, 1)

        @block.vector
        def _(dve):
            for br in range(3):
                nc.vector.tensor_tensor(GL[0:NEWTOK, br], gates[0:NEWTOK, 2, br * NH:(br + 1) * NH].unsqueeze(2)
                                        .broadcast_to([NEWTOK, NH, STEPS]),
                                        stepsel.unsqueeze(1).broadcast_to([NEWTOK, NH, STEPS]), ALU.mult)\
                    .then_inc(gl, 1)
            for n in range(0, NB, 2):
                dve.wait_ge(turned, n + 1)
                copy(n, False).then_inc(by_dve, 1)
            dve.wait_ge(gsum, 1)
            nc.vector.tensor_copy(GS, ps[6][:, 0:3 * NSEQ].rearrange("p (a b) -> p a b", a=3))
            nc.vector.tensor_copy(VNEW[0:NEWTOK], KV[0:NEWTOK, 2, 3])
            nc.vector.tensor_copy(VNEW[NEWTOK:P], WN[0:NEWTOK, 2, 1])

        @block.gpsimd
        def _(pool):
            nc.gpsimd.memset(view(M, Map.QB, 512), 0.0)
            nc.gpsimd.memset(view(M, Map.W2, 2 * 3 * HD), 0.0)
            nc.gpsimd.memset(view(M, Map.ONES, 260), 1.0)
            nc.gpsimd.memset(view(M, Map.CVP, NKV * 3 * HD), 0.0)
            nc.gpsimd.memset(view(M, Map.VP, 2 * 2 * NKV * 3 * HD), 0.0).then_inc(zeroed, 1)
            pool.wait_ge(zeroed, 1)
            for i in range(2):
                nc.gpsimd.tensor_copy(VP[:, i, 0, :, HD:2 * HD], KV[:, i, 3].rearrange("p (g d) -> p g d", g=NKV))
                nc.gpsimd.tensor_copy(VP[:, i, 1, :, HD:2 * HD], WN[:, i, 1].rearrange("p (g d) -> p g d", g=NKV))


def compress_prompt(nc, I, O, M):
    ps, stat = M["ps"], M["stat"]
    W1, W2 = view(M, Map.W1, 2, 2, 8, HID), view(M, Map.W2, 2, 3 * HD)
    PEC, BIAS, ONES = view(M, Map.PE, 2, 2, 8), view(M, Map.BIAS, 2, HID), view(M, Map.ONES, 260)
    CR = view(M, Map.CHUNKS, 2, 8 * NKV, 2, HD)
    RP = view(M, Map.RP, 2, 8, NKV, CHUNK)
    HIDP = view(M, Map.HIDB, 2, NKV, NCP)
    CKP, CVP = view(M, Map.CKP, 2, CHUNK), view(M, Map.CVP, NKV, 3 * HD)
    SQ, RS = view(M, Map.CKB, 2, NCP), view(M, Map.CKB + 64, 2, NCP)
    B1 = view(M, Map.CKB + 128, 2, HID)
    KG = M["kgain"]
    ident, blockones = const(M, "ident"), const(M, "blockones")
    NCH = NCP + 1
    with ExitStack() as ctx:
        sem = lambda n: new_sem(nc, M, "cmpp_" + n)
        w_in, rows_in, small_in = sem("weights_landed"), sem("rows_landed"), sem("small_landed")
        turned, copied, biased = sem("rows_turned"), sem("rows_copied"), sem("bias_ready")
        product, gelu, ck, sq, ss = sem("hidden_ready"), sem("gelu_ready"), sem("ck_ready"), sem("ck_squared"), sem("ck_summed")
        cv, mean, root, chain, bias_mm = sem("cv_ready"), sem("mean_ready"), sem("root_ready"), sem("chain"), sem("bias_summed")
        block = ctx.enter_context(nc.Block())

        @block.sync
        def _(sp):
            src = O["new_kv_prompt"][0].rearrange("(c i r) k g d -> k r c i g d", r=2, i=CHUNK // 2)
            for kind in range(2):
                for r in range(2):
                    sp.dma_start(CR[0:NCH, kind, :, r, :].rearrange("c (i g) d -> c i g d", g=NKV), src[kind, r])\
                        .then_inc(rows_in, 16)
            for kind in range(2):
                sp.dma_start(W1[:, kind], I["cmp_w1"][kind].rearrange("(h i p) n -> p h i n", p=P, h=2)).then_inc(w_in, 16)
            sp.dma_start(W2[:, :, HD:2 * HD], I["cmp_w2"].rearrange("k p n -> p k n")).then_inc(small_in, 16)
            sp.dma_start(PEC, I["cmp_pe"]).then_inc(small_in, 16)
            sp.dma_start(B1[0:1], I["cmp_b1"].unsqueeze(0)).then_inc(small_in, 16)
            sp.dma_start(KG[:, :], I["k_gainT"]).then_inc(small_in, 16)

        @block.tensor
        def _(pe):
            pe.wait_ge(rows_in, 64)
            for kind in range(2):
                for i in range(8):
                    for g in range(NKV):
                        last = pe.transpose(ps[kind][:, (i * NKV + g) * NCH:(i * NKV + g + 1) * NCH],
                                            CR[0:NCH, kind, i * NKV + g].rearrange("c r d -> c (r d)"),
                                            ident[0:NCH, 0:NCH])
                last.then_inc(turned, 1)
            pe.wait_ge(w_in, 32)
            pe.wait_ge(small_in, 64)
            for kind in range(2):
                for half in range(2):
                    for i in range(8):
                        last = pe.matmul(ps[2][0:1, kind * HID:(kind + 1) * HID], PEC[:, kind, half, i:i + 1],
                                         W1[:, kind, half, i, :], start=(half + i == 0), stop=(half + i == 8))
            last.then_inc(bias_mm, 1)
            pe.wait_ge(biased, 1)
            pe.wait_ge(copied, 2)
            for kind in range(2):
                bank = ps[3 + kind][:, 0:NKV * NCP].rearrange("p (g c) -> p g c", g=NKV)
                pe.matmul(ps[3 + kind][:, 0:NKV * NCP], BIAS[0:1, kind, :], ONES[0:1, 0:NKV * NCP], start=True, stop=False)
                for half in range(2):
                    for i in range(8):
                        last = pe.matmul(bank, W1[:, kind, half, i, :], RP[:, kind, i, :, half:half + NCP],
                                         start=False, stop=(half + i == 8))
                last.then_inc(product, 1)
            pe.wait_ge(gelu, 2)
            for j in range(2):
                out = ps[5][:, j * NCP:(j + 1) * NCP]
                pe.matmul(out, W2[:, 0, HD:3 * HD], HIDP[:, 0, 2 * j, :], start=True, stop=False)
                last = pe.matmul(out, W2[:, 0, 0:2 * HD], HIDP[:, 0, 2 * j + 1, :], start=False, stop=True)
            last.then_inc(ck, 1)
            for g in range(NKV):
                last = pe.matmul(ps[6][0:NCP, g * HD:(g + 1) * HD], HIDP[:, 1, g, :], W2[:, 1, HD:2 * HD],
                                 start=True, stop=True)
            last.then_inc(cv, 1)
            pe.wait_ge(sq, 1)
            pe.matmul(ps[7][:, 0:2 * NCP], blockones, SQ.rearrange("p j c -> p (j c)"), start=True, stop=True).then_inc(ss, 1)

        @block.scalar
        def _(act):
            for kind in range(2):
                act.wait_ge(product, kind + 1)
                act.activation(HIDP[:, kind].rearrange("p g c -> p (g c)"), ps[3 + kind][:, 0:NKV * NCP],
                               ACT.Gelu_apprx_tanh).then_inc(gelu, 1)
            act.wait_ge(ck, 1)
            act.activation(SQ.rearrange("p j c -> p (j c)"), ps[5][:, 0:2 * NCP], ACT.Square).then_inc(sq, 1)
            act.wait_ge(mean, 1)
            act.activation(RS, RS, ACT.Sqrt).then_inc(root, 1)

        @block.vector
        def _(dve):
            V = nc.vector
            st = Steps(dve, chain)
            for kind in range(2):
                dve.wait_ge(turned, kind + 1)
                V.tensor_copy(RP[:, kind].rearrange("p i g c -> p (i g c)"), ps[kind][:, :]).then_inc(copied, 1)
            dve.wait_ge(bias_mm, 1)
            dve.wait_ge(small_in, 64)
            V.tensor_tensor(BIAS[0:1].rearrange("p k n -> p (k n)"), ps[2][0:1, 0:2 * HID],
                            B1[0:1].rearrange("p k n -> p (k n)"), ALU.add).then_inc(biased, 1)
            dve.wait_ge(cv, 1)
            st.add(V.tensor_copy(CVP[0:NCP, :, HD:2 * HD], ps[6][0:NCP, 0:NKV * HD].rearrange("p (g d) -> p g d", g=NKV)))
            dve.wait_ge(ss, 1)
            V.tensor_scalar(RS, ps[7][:, 0:2 * NCP].rearrange("p (j c) -> p j c", j=2), 1.0 / HD, EPS, ALU.mult, ALU.add)\
                .then_inc(mean, 1)
            dve.wait_ge(root, 1)
            st.add(V.reciprocal(RS, RS))
            st.add(V.scalar_tensor_tensor(CKP[:, :, 0:NCP], ps[5][:, 0:2 * NCP].rearrange("p (j c) -> p j c", j=2),
                                          KG[:, 0:1], RS, ALU.mult, ALU.mult))


def queries_of(nc, QS, QB, b, s, done):
    for par in range(2):
        half = slice(par * HD, (par + 1) * HD)
        for j in range(2):
            at = (2 * j + par) * HPG * STEPS
            dst = QB[half, s, j, at:at + HPG * STEPS].rearrange("p (h t) -> p h t", h=HPG)
            nc.gpsimd.tensor_copy(dst, QS[half, j, :, bass.ds(b * STEPS, STEPS)]).then_inc(done, 1)


def compress_samples(nc, I, M):
    ps, stat = M["ps"], M["stat"]
    W1, W2 = view(M, Map.W1, 2, 2, 8, HID), view(M, Map.W2, 2, 3 * HD)
    BIAS, ONES, KG = view(M, Map.BIAS, 2, HID), view(M, Map.ONES, 260), M["kgain"]
    RAW = view(M, Map.PAGES, 2, NPAGE, 2, 256)
    HIDB = view(M, Map.HIDB, 2, 2, 256)
    NB = NCS + 1
    SQ = view(M, Map.CKB, 2, NB)
    RS = view(M, Map.CKB + 128, 2, NB)
    CKT = view(M, Map.CKB + 256, 2, NB)
    PR = view(M, Map.CKB + 384, NB)
    SCORE, KEY = view(M, Map.CKB + 448, NSB - 3), view(M, Map.CKB + 464, NSB - 3)
    CV, PC, BM = view(M, Map.CV, NSEQ, NKV * HD), view(M, Map.PC, NSEQ, NB), view(M, Map.BM, NSEQ, 16)
    GS = view(M, Map.GS, 3, NSEQ)
    QS, QB = view(M, Map.QSN, 2, HPG, NEWTOK), view(M, Map.QB, 2, 2, P)
    sm = view(M, Map.SMALL, 16)
    blockones, headsum, iota = const(M, "blockones"), const(M, "headsum"), const(M, "iota")
    NBLK = NPAGE * (PAGE // CHUNK) * NKV
    with ExitStack() as ctx:
        sem = lambda n: new_sem(nc, M, "cmps_" + n)
        raw_in = [sem(f"pages_landed{s}") for s in range(2)]
        hidden, gelu, ck, cv = sem("hidden_ready"), sem("gelu_ready"), sem("ck_ready"), sem("cv_ready")
        squared, ss, mean, root, ckt = sem("ck_squared"), sem("ck_summed"), sem("mean_ready"), sem("root_ready"), sem("ckT_ready")
        cv_out, qb, score, negmax = sem("cv_copied"), sem("queries_ready"), sem("scores_ready"), sem("negmax_ready")
        expd, prob, pooled, chain = sem("exp_ready"), sem("probs_ready"), sem("group_sums_ready"), sem("chain")
        chosen = sem("blocks_chosen")
        block = ctx.enter_context(nc.Block())
        DCH = 11

        def over_sequences(eng, body):
            for s in range(2):
                body(s, s, True, False)
            with eng.Fori(1, NSEQ // 2 - 1) as i:
                for s in range(2):
                    body(i * 2 + s, s, False, False)
            for s in range(2):
                body(NSEQ - 2 + s, s, False, s == 1)

        @block.sync
        def _(sp):
            def load(b, s, first, last):
                if not first:
                    sp.wait_ge(hidden, b * 2 - 2)
                for pg in range(NPAGE):
                    with_id = sp.value_load(M["pages"][0:1, bass.ds(b * NPAGE + pg, 1)], min_val=0,
                                            max_val=I["pages_raw"].shape[0] - 1)
                    sp.dma_start(RAW[:, s, pg].rearrange("p k n -> p (k n)"),
                                 I["pages_raw"][bass.ds(with_id, 1)].rearrange("a p n -> p (a n)")).then_inc(raw_in[s], 16)
            over_sequences(sp, load)

        @block.gpsimd
        def _(pool):
            def queries(b, s, first, last):
                if not first:
                    pool.wait_ge(score, b - 1)
                queries_of(nc, QS, QB, b, s, qb)
            over_sequences(pool, queries)

        @block.tensor
        def _(pe):
            def hide(b, s, kind, half):
                bank = ps[2 * s + kind]
                out = bank[:, 1 - half:1 - half + NBLK].rearrange("p (g n c) -> p g n c", g=NKV, n=NPAGE)
                for i in range(8):
                    rhs = RAW[:, s, :, kind, i * 32:(i + 1) * 32].rearrange("p n (g c) -> p g n c", g=NKV)
                    pe.matmul(out, W1[:, kind, half, i, :], rhs, start=(half + i == 0), stop=False,
                              skip_group_check=True)
                if half == 1:
                    pe.matmul(bank[:, 1:1 + NBLK], BIAS[0:1, kind, :], ONES[0:1, 0:NBLK], start=False, stop=True,
                              skip_group_check=True).then_inc(hidden, 1)

            def hide_after(b, s, kind, half, first):
                if kind == 0 and half == 0:
                    pe.wait_ge(raw_in[s], landed_pages(b, s))
                if half == 0 and not first:
                    pe.wait_ge(gelu, b * 2 + (kind - 3))
                hide(b, s, kind, half)

            def landed_pages(b, s):
                return (b - s) * (16 * NPAGE // 2) + 16 * NPAGE

            def seq(b, s, first, last):
                nxt = lambda kind, half: None if last else hide_after(b + 1, 1 - s, kind, half, first and s == 0)
                nxt(0, 0)
                pe.wait_ge(gelu, b * 2 + 2)
                if not (first and s == 0):
                    pe.wait_ge(ckt, b)
                    pe.wait_ge(cv_out, b)
                for j in range(2):
                    out = ps[4][:, j * NB:(j + 1) * NB]
                    pe.matmul(out, W2[:, 0, HD:3 * HD], HIDB[:, s, 0, 2 * j * NB:(2 * j + 1) * NB], start=True, stop=False)
                    last_mm = pe.matmul(out, W2[:, 0, 0:2 * HD], HIDB[:, s, 0, (2 * j + 1) * NB:(2 * j + 2) * NB],
                                        start=False, stop=True)
                last_mm.then_inc(ck, 1)
                for g in range(NKV):
                    last_mm = pe.matmul(ps[5][0:NB, g * HD:(g + 1) * HD], HIDB[:, s, 1, g * NB:(g + 1) * NB],
                                        W2[:, 1, HD:2 * HD], start=True, stop=True)
                last_mm.then_inc(cv, 1)
                nxt(0, 1)
                pe.wait_ge(squared, b + 1)
                pe.matmul(ps[4][:, 2 * NB:4 * NB], blockones, SQ.rearrange("p j c -> p (j c)"), start=True, stop=True)\
                    .then_inc(ss, 1)
                nxt(1, 0)
                pe.wait_ge(ckt, b + 1)
                pe.wait_ge(qb, b * 4 + 4)
                if not (first and s == 0):
                    pe.wait_ge(chosen, b)
                for j in range(2):
                    last_mm = pe.matmul(ps[6][:, 0:NB], QB[:, s, j, :], CKT[:, j, :], start=(j == 0), stop=(j == 1))
                last_mm.then_inc(score, 1)
                nxt(1, 1)
                pe.wait_ge(prob, b + 1)
                pe.matmul(ps[6][:, NB:2 * NB], headsum, PR, start=True, stop=True).then_inc(pooled, 1)

            for kind in range(2):
                for half in range(2):
                    hide_after(0, 0, kind, half, True)
            over_sequences(pe, seq)

        @block.scalar
        def _(act):
            def take_gelu(b, s, first):
                for kind in range(2):
                    act.wait_ge(hidden, b * 2 + (kind + 1))
                    if not first:
                        act.wait_ge(cv, b - 1)
                    act.activation(HIDB[:, s, kind, :], ps[2 * s + kind][:, 1:NBLK + 1], ACT.Gelu_apprx_tanh)\
                        .then_inc(gelu, 1)

            def seq(b, s, first, last):
                act.wait_ge(ck, b + 1)
                if not (first and s == 0):
                    act.wait_ge(ss, b)
                act.activation(SQ.rearrange("p j c -> p (j c)"), ps[4][:, 0:2 * NB], ACT.Square).then_inc(squared, 1)
                act.wait_ge(mean, b + 1)
                act.activation(RS, RS, ACT.Sqrt).then_inc(root, 1)
                act.wait_ge(negmax, b + 1)
                act.activation(PR, ps[6][:, 0:NB], ACT.Exp, bias=sm[:, 0:1], scale=SCALE,).then_inc(expd, 1)
                if not last:
                    take_gelu(b + 1, 1 - s, first and s == 0)
            take_gelu(0, 0, True)
            over_sequences(act, seq)

        @block.vector
        def _(dve):
            V = nc.vector

            def seq(b, s, first, last):
                st = Steps(dve, chain, b * DCH)
                dve.wait_ge(cv, b + 1)
                V.tensor_copy(CV[0:NB, bass.ds(b, 1), :], ps[5][0:NB, 0:NKV * HD].unsqueeze(1)).then_inc(cv_out, 1)
                dve.wait_ge(ss, b + 1)
                V.tensor_scalar(RS, ps[4][:, 2 * NB:4 * NB].rearrange("p (j c) -> p j c", j=2), 1.0 / HD, EPS,
                                ALU.mult, ALU.add).then_inc(mean, 1)
                dve.wait_ge(root, b + 1)
                st.add(V.reciprocal(RS, RS))
                if not (first and s == 0):
                    dve.wait_ge(score, b)
                V.scalar_tensor_tensor(CKT, ps[4][:, 0:2 * NB].rearrange("p (j c) -> p j c", j=2), KG[:, 0:1], RS,
                                       ALU.mult, ALU.mult).then_inc(ckt, 1)
                dve.wait_ge(score, b + 1)
                st.add(V.tensor_reduce(sm[:, 1:2], ps[6][:, 0:NCS], AX.X, ALU.max))
                V.tensor_scalar(sm[:, 0:1], sm[:, 1:2], -SCALE, None, ALU.mult).then_inc(negmax, 1)
                dve.wait_ge(expd, b + 1)
                st.add(V.tensor_reduce(sm[:, 2:3], PR[:, 0:NCS], AX.X, ALU.add))
                st.add(V.reciprocal(sm[:, 3:4], sm[:, 2:3]))
                V.tensor_scalar(PR, PR, sm[:, 3:4], None, ALU.mult).then_inc(prob, 1)
                dve.wait_ge(prob, b + 1)
                V.tensor_scalar(PC[:, bass.ds(b, 1), :], PR.unsqueeze(1), GS[:, 0, bass.ds(b, 1)], None, ALU.mult)
                dve.wait_ge(pooled, b + 1)
                pg = ps[6][:, NB + 4:NB + 4 * (NSB - 2)].rearrange("p (j o) -> p j o", o=4)
                prev = ps[6][:, NB + 3:NB + 3 + 4 * (NSB - 3)].rearrange("p (j o) -> p j o", o=4)[:, :, 0]
                st.add(V.tensor_reduce(SCORE, pg, AX.X, ALU.add))
                st.add(V.tensor_tensor(SCORE, SCORE, prev, ALU.add))
                st.add(V.tensor_reduce(sm[:, 4:5], SCORE, AX.X, ALU.min))
                st.add(V.scalar_tensor_tensor(KEY, SCORE, sm[:, 4:5], iota, ALU.is_equal, ALU.mult))
                st.add(V.tensor_reduce(sm[:, 5:6], KEY, AX.X, ALU.max))
                st.add(V.tensor_scalar(KEY, iota, sm[:, 5:6], NEG, ALU.is_equal, ALU.mult))
                V.tensor_copy(BM[:, bass.ds(b, 1), 1:NSB - 2], KEY.unsqueeze(1)).then_inc(chosen, 1)
                st.add(V.memset(sm[:, 6:7], 0.0))
                assert st.n == DCH - 1 + 0 or True
                DCHN[0] = st.n

            DCHN = [0]
            over_sequences(dve, seq)
            assert DCHN[0] == DCH, DCHN

    with ExitStack() as ctx:
        block = ctx.enter_context(nc.Block())

        @block.vector
        def _(dve):
            nc.vector.memset(BM[:, :, 0:1], 0.0)
            nc.vector.memset(BM[:, :, NSB - 2:16], 0.0)


def attend_samples(nc, I, M):
    ps, OT = M["ps"], M["XT"]
    SEL = view(M, Map.PAGES, 2, NPAGE, 512)
    WB = view(M, Map.WINB, 2, 2048)
    QS, QB = view(M, Map.QSR, 2, HPG, NEWTOK), view(M, Map.QB, 2, 2, P)
    KTN = view(M, Map.KTN, 2, 2, NEWTOK)
    VNEW, CVB = view(M, Map.VNEW, NKV * HD), view(M, Map.CVB, 2, NKV * HD)
    CV, PC, BM = view(M, Map.CV, NSEQ, NKV * HD), view(M, Map.PC, NSEQ, NCS + 1), view(M, Map.BM, NSEQ, 16)
    GS = view(M, Map.GS, 3, NSEQ)
    NEW = PAST
    WCOL = PAST + 2 * NEWTOK
    CCOL = WCOL + WIN
    NCOL = CCOL + NCS + 1
    NTILE = 14
    PR = [view(M, Map.PROW0, NCOL), view(M, Map.PROW1, NCOL)]
    PT = [view(M, Map.PT0, NTILE, P), view(M, Map.PT1, NTILE, P)]
    sm = view(M, Map.SMALL, 2, 32)
    newmask = const(M, "newmask").rearrange("p (b t) -> p b t", b=NSEQ)
    winmask, ident = const(M, "winmask"), const(M, "ident")
    tiles = [(i * P, P) for i in range(NPAGE + 1)] + [(WCOL + i * P, P) for i in range(WIN // P)] + [(CCOL, NCS)]
    with ExitStack() as ctx:
        sem = lambda n: new_sem(nc, M, "atts_" + n)
        sel_in = [sem(f"pages_landed{s}") for s in range(2)]
        win_in = [sem(f"window_landed{s}") for s in range(2)]
        qb, cvb, bmb = sem("queries_ready"), sem("cvalues_ready"), sem("blockmask_ready")
        score, masked, negmax, expd = sem("scores_ready"), sem("scores_read"), sem("negmax_ready"), sem("exp_ready")
        weighted, turned, by_dve, by_act = sem("probs_ready"), sem("probs_turned"), sem("turned_by_dve"), sem("turned_by_act")
        summed, out, chain, wread = sem("values_summed"), sem("out_copied"), sem("chain"), sem("window_masked")
        block = ctx.enter_context(nc.Block())
        DCH = 10

        def over_sequences(eng, body):
            for s in range(2):
                body(s, s, True, False)
            with eng.Fori(1, NSEQ // 2 - 1) as i:
                for s in range(2):
                    body(i * 2 + s, s, False, False)
            for s in range(2):
                body(NSEQ - 2 + s, s, False, s == 1)

        @block.sync
        def _(sp):
            def load(b, s, first, last):
                if not first:
                    sp.wait_ge(summed, b - 1)
                for pg in range(NPAGE):
                    pid = sp.value_load(M["pages"][0:1, bass.ds(b * NPAGE + pg, 1)], min_val=0,
                                        max_val=I["pages_sel"].shape[0] - 1)
                    sp.dma_start(SEL[:, s, pg], I["pages_sel"][bass.ds(pid, 1)].rearrange("a p n -> p (a n)"))\
                        .then_inc(sel_in[s], 16)
                sp.dma_start(WB[:, s, 0:2 * WIN], I["win_keysT"][bass.ds(b, 1)].rearrange("a p n -> p (a n)"))\
                    .then_inc(win_in[s], 16)
                sp.dma_start(WB[:, s, 2 * WIN:].rearrange("p (k n) -> p k n", k=WIN // P),
                             I["state_win"][bass.ds(b, 1), :, 1].rearrange("a (k p) g d -> p (a k) (g d)", p=P))\
                    .then_inc(win_in[s], 16)
            over_sequences(sp, load)

        @block.gpsimd
        def _(pool):
            def prepare(b, s, first, last):
                if not first:
                    pool.wait_ge(score, b - 1)
                queries_of(nc, QS, QB, b, s, qb)
                pool.wait_ge(qb, b * 4 + 4)
                if not first:
                    pool.wait_ge(masked, b * 4 - 4)
                nc.gpsimd.tensor_copy(sm[:, s, 16:32].unsqueeze(1), BM[:, bass.ds(b, 1), :]).then_inc(bmb, 1)
                pool.wait_ge(bmb, b + 1)
                if not first:
                    pool.wait_ge(summed, b - 1)
                nc.gpsimd.tensor_copy(CVB[0:NCS + 1, s].unsqueeze(1), CV[0:NCS + 1, bass.ds(b, 1), :]).then_inc(cvb, 1)
            over_sequences(pool, prepare)

        @block.tensor
        def _(pe):
            def scores(b, s, first):
                pe.wait_ge(qb, b * 4 + 4)
                pe.wait_ge(sel_in[s], (b - s) * (16 * NPAGE // 2) + 16 * NPAGE)
                if not first:
                    pe.wait_ge(masked, b * 4)
                    pe.wait_ge(expd, b * 4)
                for bank in range(2):
                    for j in range(2):
                        pe.matmul(ps[bank][:, :], QB[:, s, j, :],
                                  SEL[:, s, 4 * bank:4 * bank + 4, j * PAGE:(j + 1) * PAGE], start=(j == 0), stop=(j == 1))
                for br in range(2):
                    for j in range(2):
                        pe.matmul(ps[3][:, br * NEWTOK:(br + 1) * NEWTOK], QB[:, s, j, :], KTN[:, br, j, :],
                                  start=(j == 0), stop=(j == 1))
                pe.wait_ge(win_in[s], (b - s) * 16 + 32)
                for j in range(2):
                    last = pe.matmul(ps[2][:, :], QB[:, s, j, :], WB[:, s, j * WIN:(j + 1) * WIN],
                                     start=(j == 0), stop=(j == 1))
                last.then_inc(score, 1)

            def turn(b, s):
                pe.wait_ge(weighted, b * 3 + 3)
                for q in range(4):
                    if q >= 2:
                        pe.wait_ge((by_dve, by_act)[q % 2], b * 2 + 1)
                    elif True:
                        wait_prev(b, s, q)
                    for m, (at, w) in enumerate(tiles[4 * q:4 * q + 4]):
                        last = pe.transpose(ps[4 + q % 2][0:w, m * P:(m + 1) * P], PR[s][:, at:at + w], ident)
                    last.then_inc(turned, 1)

            def wait_prev(b, s, q):
                if not first_turn[0]:
                    pe.wait_ge((by_dve, by_act)[q % 2], b * 2)

            def values(b, s, first):
                pe.wait_ge(by_dve, b * 2 + 2)
                pe.wait_ge(by_act, b * 2 + 2)
                pe.wait_ge(cvb, b + 1)
                if not first:
                    pe.wait_ge(out, b * 2 - 2)
                for g in range(NKV):
                    gd = slice(g * HD, (g + 1) * HD)
                    for t in range(NTILE):
                        if t < NPAGE:
                            v = SEL[:, s, t, 2 * PAGE + g * HD:2 * PAGE + (g + 1) * HD]
                        elif t == NPAGE:
                            v = VNEW[:, gd]
                        elif t < NTILE - 1:
                            at = 2 * WIN + (t - NPAGE - 1) * NKV * HD + g * HD
                            v = WB[:, s, at:at + HD]
                        else:
                            v = CVB[0:NCS, s, gd]
                        k = NCS if t == NTILE - 1 else P
                        q = g * HPG * STEPS
                        last = pe.matmul(ps[6 + s][0:HD, q:q + HPG * STEPS], v, PT[s][0:k, t, q:q + HPG * STEPS],
                                         start=(t == 0), stop=(t == NTILE - 1))
                last.then_inc(summed, 1)

            first_turn = [True]

            def seq(b, s, first, last):
                if not last:
                    scores(b + 1, 1 - s, False)
                first_turn[0] = first and s == 0
                turn(b, s)
                values(b, s, first)
            scores(0, 0, True)
            over_sequences(pe, seq)

        def copy_turned(eng, copy, b, s, half, first, done, other):
            for q in (half, half + 2):
                eng.wait_ge(turned, b * 4 + (q + 1))
                if q == half and not first:
                    eng.wait_ge(summed, b - 1)
                if q == 3:
                    copy(PT[s][:, 12, :], ps[4 + q % 2][:, 0:P]).then_inc(other, 1)
                    copy(PT[s][0:NCS, 13, :], ps[4 + q % 2][0:NCS, P:2 * P]).then_inc(done, 1)
                else:
                    copy(PT[s][:, 4 * q:4 * q + 4, :].rearrange("p m t -> p (m t)"), ps[4 + q % 2][:, :]).then_inc(done, 1)

        tail = new_sem(nc, M, "atts_tail_copied")

        @block.scalar
        def _(act):
            def softmax(b, s, first):
                act.wait_ge(negmax, b + 1)
                if not first:
                    act.wait_ge(turned, b * 4 - 4)
                for n, (dst, src, br) in enumerate(((slice(0, PAST), PR[s][:, 0:PAST], 0),
                                                    (slice(NEW, NEW + NEWTOK), PR[s][:, NEW:NEW + NEWTOK], 0),
                                                    (slice(NEW + NEWTOK, WCOL), PR[s][:, NEW + NEWTOK:WCOL], 1),
                                                    (slice(WCOL, CCOL), ps[2][:, :], 1))):
                    act.activation(PR[s][:, dst], src, ACT.Exp, bias=sm[:, s, br:br + 1], scale=SCALE,
                                   accum_out=sm[:, s, 4 + n:5 + n]).then_inc(expd, 1)

            def seq(b, s, first, last):
                if not last:
                    softmax(b + 1, 1 - s, first and s == 0)
                copy_turned(act, nc.scalar.copy, b, s, 1, first, by_act, tail)
            softmax(0, 0, True)
            over_sequences(act, seq)

        @block.vector
        def _(dve):
            V = nc.vector

            def softmax(b, s, first):
                st = Steps(dve, chain, b * DCH)
                dve.wait_ge(score, b + 1)
                dve.wait_ge(bmb, b + 1)
                if not first:
                    dve.wait_ge(turned, b * 4 - 4)
                V.tensor_tensor(PR[s][:, NEW:WCOL].rearrange("p (r t) -> p r t", r=2),
                                ps[3][:, 0:2 * NEWTOK].rearrange("p (r t) -> p r t", r=2),
                                newmask[:, bass.ds(b, 1), :].broadcast_to([P, 2, NEWTOK]), ALU.add).then_inc(masked, 1)
                for bank in range(2):
                    V.tensor_tensor_reduce(
                        PR[s][:, bank * 512:(bank + 1) * 512].rearrange("p (k c) -> p k c", c=SELB),
                        ps[bank][:, :].rearrange("p (k c) -> p k c", c=SELB),
                        sm[:, s, 16 + 8 * bank:24 + 8 * bank].unsqueeze(2).broadcast_to([P, 8, SELB]),
                        1.0, -3e38, ALU.add, ALU.max, sm[:, s, 8 + bank:9 + bank]).then_inc(masked, 1)
                V.tensor_tensor(ps[2][:, 0:STEPS], ps[2][:, 0:STEPS], winmask, ALU.add).then_inc(masked, 1)
                dve.wait_ge(masked, b * 4 + 4)
                st.add(V.tensor_reduce(sm[:, s, 10:12], PR[s][:, NEW:WCOL].rearrange("p (r t) -> p r t", r=2), AX.X, ALU.max))
                st.add(V.tensor_reduce(sm[:, s, 12:13], ps[2][:, :], AX.X, ALU.max))
                st.add(V.tensor_tensor(sm[:, s, 13:14], sm[:, s, 8:9], sm[:, s, 9:10], ALU.max))
                st.add(V.tensor_tensor(sm[:, s, 14:15], sm[:, s, 10:11], sm[:, s, 13:14], ALU.max))
                st.add(V.tensor_tensor(sm[:, s, 15:16], sm[:, s, 11:12], sm[:, s, 12:13], ALU.max))
                V.tensor_scalar(sm[:, s, 0:2], sm[:, s, 14:16], -SCALE, None, ALU.mult).then_inc(negmax, 1)
                dve.wait_ge(expd, b * 4 + 4)
                st.add(V.tensor_tensor(sm[:, s, 8:9], sm[:, s, 4:5], sm[:, s, 5:6], ALU.add))
                st.add(V.tensor_tensor(sm[:, s, 9:10], sm[:, s, 6:7], sm[:, s, 7:8], ALU.add))
                st.add(V.reciprocal(sm[:, s, 10:12], sm[:, s, 8:10]))
                st.add(V.tensor_tensor(sm[:, s, 12:14].unsqueeze(2), sm[:, s, 10:12].unsqueeze(2),
                                       GS[:, 1:3, bass.ds(b, 1)], ALU.mult))
                V.tensor_scalar(PR[s][:, 0:NEW + NEWTOK], PR[s][:, 0:NEW + NEWTOK], sm[:, s, 12:13], None, ALU.mult)\
                    .then_inc(weighted, 1)
                V.tensor_scalar(PR[s][:, NEW + NEWTOK:CCOL], PR[s][:, NEW + NEWTOK:CCOL], sm[:, s, 13:14], None, ALU.mult)\
                    .then_inc(weighted, 1)
                V.tensor_copy(PR[s][:, CCOL:NCOL].unsqueeze(1), PC[:, bass.ds(b, 1), :]).then_inc(weighted, 1)
                assert st.n == 9, st.n
                st.add(V.memset(sm[:, s, 3:4], 0.0))

            def seq(b, s, first, last):
                if not last:
                    softmax(b + 1, 1 - s, first and s == 0)
                copy_turned(dve, V.tensor_copy, b, s, 0, first, by_dve, None)
                dve.wait_ge(summed, b + 1)
                for par in range(2):
                    src = ps[6 + s][0:HD, 0:P].rearrange("p (k r t) -> p k r t", r=2, t=STEPS)[:, :, par, :]
                    V.tensor_copy(OT[par * HD:(par + 1) * HD, :, bass.ds(b * STEPS + SEQ, STEPS)], src).then_inc(out, 1)
            softmax(0, 0, True)
            over_sequences(dve, seq)


def attend_prompt(nc, I, M):
    ps, OT, gates = M["ps"], M["XT"], M["gates"]
    QN, QR = view(M, Map.QNT, 2, HPG, SEQ), view(M, Map.QRT, 2, HPG, SEQ)
    KT, CKP = view(M, Map.KTP, 2, 2, SEQ), view(M, Map.CKP, 2, CHUNK)
    VP, CVP = view(M, Map.VP, 2, 2, NKV, 3 * HD), view(M, Map.CVP, NKV, 3 * HD)
    PTC = view(M, Map.PTC, NH, P)
    PTP = view(M, Map.PTP, 2, 4, P)
    PP = view(M, Map.PP, 3, 2, SEQ)
    PCM = view(M, Map.PP + 6 * SEQ, NH, CHUNK)
    sm = view(M, Map.SMALL, 3, 16)
    csm = view(M, Map.SMALL + 64, 4, NH)
    causal = const(M, "causal").rearrange("p (t k) -> p t k", t=2)
    cadd = const(M, "cmpadd").rearrange("p (t k) -> p t k", t=2)
    cmul = const(M, "cmpmul").rearrange("p (t k) -> p t k", t=2)
    ident = const(M, "ident")
    WO = view(M, Map.WO, KD, D)
    units = [(t, hd) for t in range(2) for hd in range(NH)]
    NU = len(units)
    wo_in = M["wo_in"]

    def part(hd):
        g, h = hd // HPG, hd % HPG
        return slice((g % 2) * HD, (g % 2) * HD + HD), g // 2, h

    def v_cols(hd):
        return slice(0, 2 * HD) if hd % 2 else slice(HD, 3 * HD)

    with ExitStack() as ctx:
        sem = lambda n: new_sem(nc, M, "attp_" + n)
        cscore, cprob, cturned, ccopied, cneg, cexp = (sem("cmp_scores_ready"), sem("cmp_probs_ready"), sem("cmp_turned"),
                                                       sem("cmp_copied"), sem("cmp_shifted"), sem("cmp_exp_ready"))
        score, negmax, expd, weighted = sem("scores_ready"), sem("negmax_ready"), sem("exp_ready"), sem("probs_ready")
        masked, turned, copied, summed, out, chain = (sem("scores_masked"), sem("probs_turned"), sem("turned_copied"),
                                                      sem("values_summed"), sem("out_copied"), sem("chain"))
        block = ctx.enter_context(nc.Block())

        @block.sync
        def _(sp):
            sp.dma_start(WO, I["w_o"][0].rearrange("(k p) n -> p k n", p=P)).then_inc(wo_in, 16)

        @block.tensor
        def _(pe):
            def scores(n):
                t, hd = units[n]
                pp, j, h = part(hd)
                if n >= 3:
                    pe.wait_ge(masked, 2 * (n - 2))
                K = P * (t + 1)
                for br in range(2):
                    last = pe.matmul(ps[n % 3][:, br * K:(br + 1) * K], QR[pp, j, h, t * P:(t + 1) * P],
                                     KT[pp, br, j, 0:K], start=True, stop=True)
                last.then_inc(score, 1)

            def turn(n):
                t, hd = units[n]
                pe.wait_ge(weighted, 2 * (n + 1))
                if n >= 2:
                    pe.wait_ge(copied, n - 1)
                m = 0
                for br in range(2):
                    for kt in range(t + 1):
                        last = pe.transpose(ps[3 + n % 2][:, m * P:(m + 1) * P], PP[:, n % 3, br, kt * P:(kt + 1) * P], ident)
                        m += 1
                last.then_inc(turned, 1)

            def values(n):
                t, hd = units[n]
                g, pair = hd // HPG, n // 2
                pe.wait_ge(copied, n + 1)
                if n == 0 or n == NH:
                    pe.wait_ge(ccopied, 4 * (t + 1))
                if hd % 2 == 0 and pair >= 2:
                    pe.wait_ge(out, pair - 1)
                bank = ps[5 + pair % 2][:, 0:P]
                m = 0
                for br in range(2):
                    for kt in range(t + 1):
                        pe.matmul(bank, VP[:, kt, br, g, v_cols(hd)], PTP[:, n % 2, m, :],
                                  start=(hd % 2 == 0 and m == 0), stop=False)
                        m += 1
                pe.matmul(bank, CVP[0:NCP, g, v_cols(hd)], PTC[0:NCP, hd, :], start=False, stop=(hd % 2 == 1))\
                    .then_inc(summed, 1)

            def compressed(t):
                for par in range(2):
                    for hd in [x for x in range(NH) if x // HPG % 2 == par]:
                        pp, j, h = part(hd)
                        last = pe.matmul(ps[7][:, hd * CHUNK:hd * CHUNK + NCP], QN[pp, j, h, t * P:(t + 1) * P],
                                         CKP[pp, j, 0:NCP], start=True, stop=True)
                    last.then_inc(cscore, 1)
                    pe.wait_ge(cscore, 2 * t + par + 1)

            def turn_compressed(t):
                pe.wait_ge(cprob, t + 1)
                if t:
                    pe.wait_ge(summed, NH)
                for q in range(4):
                    if q or t:
                        pe.wait_ge(ccopied, 4 * t + q)
                    for m in range(4):
                        last = pe.transpose(ps[7][0:NCP, m * P:(m + 1) * P], PCM[:, 4 * q + m, 0:NCP], ident)
                    last.then_inc(cturned, 1)

            compressed(0)
            scores(0)
            scores(1)
            turn_compressed(0)
            compressed_at = NH - 2
            for n in range(NU + 1):
                if n + 2 < NU:
                    scores(n + 2)
                if n < NU:
                    turn(n)
                if n >= 1:
                    values(n - 1)
                if n == NH:
                    compressed(1)
                    turn_compressed(1)

        @block.scalar
        def _(act):
            def unit(n):
                t, hd = units[n]
                K = P * (t + 1)
                act.wait_ge(negmax, n + 1)
                for br in range(2):
                    act.activation(PP[:, n % 3, br, 0:K], PP[:, n % 3, br, 0:K], ACT.Exp, bias=sm[:, n % 3, br:br + 1],
                                   scale=SCALE, accum_out=sm[:, n % 3, 4 + br:5 + br]).then_inc(expd, 1)

            def copy_turned(n):
                t, hd = units[n]
                act.wait_ge(turned, n + 1)
                if n >= 2:
                    act.wait_ge(summed, n - 1)
                w = 2 * (t + 1)
                nc.scalar.copy(PTP[:, n % 2, 0:w, :].rearrange("p m q -> p (m q)"), ps[3 + n % 2][:, 0:w * P])\
                    .then_inc(copied, 1)

            def exp_compressed(t):
                act.wait_ge(cneg, t + 1)
                act.activation(PCM[:, :, 0:NCP], PCM[:, :, 0:NCP], ACT.Exp, scale=SCALE).then_inc(cexp, 1)

            def copy_compressed(t):
                for q in range(4):
                    act.wait_ge(cturned, 4 * t + q + 1)
                    nc.scalar.copy(PTC[0:NCP, 4 * q:4 * q + 4, :].rearrange("p m q -> p (m q)"), ps[7][0:NCP, :])\
                        .then_inc(ccopied, 1)

            exp_compressed(0)
            unit(0)
            copy_compressed(0)
            for n in range(NU):
                if n + 1 < NU:
                    unit(n + 1)
                copy_turned(n)
                if n == NH:
                    exp_compressed(1)
                    copy_compressed(1)

        @block.vector
        def _(dve):
            V = nc.vector
            st = Steps(dve, chain)

            def compressed(t):
                dve.wait_ge(cscore, 2 * (t + 1))
                s = ps[7][:, 0:NH * CHUNK].rearrange("p (h c) -> p h c", h=NH)[:, :, 0:NCP]
                x = PCM[:, :, 0:NCP]
                if t:
                    dve.wait_ge(cturned, 4)
                add = cadd[:, t].unsqueeze(1).broadcast_to([P, NH, NCP])
                mul = cmul[:, t].unsqueeze(1).broadcast_to([P, NH, NCP])
                st.add(V.tensor_tensor(x, s, add, ALU.add))
                st.add(V.tensor_reduce(csm[:, 0], x, AX.X, ALU.max))
                V.tensor_tensor(x, x, csm[:, 0].unsqueeze(2).broadcast_to([P, NH, NCP]), ALU.subtract).then_inc(cneg, 1)
                dve.wait_ge(cexp, t + 1)
                st.add(V.tensor_tensor(x, x, mul, ALU.mult))
                st.add(V.tensor_reduce(csm[:, 1], x, AX.X, ALU.add))
                st.add(V.tensor_scalar(csm[:, 1], csm[:, 1], 1e-30, None, ALU.max))
                st.add(V.reciprocal(csm[:, 2], csm[:, 1]))
                st.add(V.tensor_tensor(csm[:, 2], csm[:, 2], gates[:, t, 0:NH], ALU.mult))
                V.tensor_tensor(x, x, csm[:, 2].unsqueeze(2).broadcast_to([P, NH, NCP]), ALU.mult).then_inc(cprob, 1)

            def before(n):
                t, hd = units[n]
                K = P * (t + 1)
                s = n % 3
                dve.wait_ge(score, n + 1)
                if n >= 3:
                    dve.wait_ge(turned, n - 2)
                for br in range(2):
                    V.tensor_tensor_reduce(PP[:, s, br, 0:K], ps[n % 3][:, br * K:(br + 1) * K], causal[:, t, 0:K],
                                           1.0, -3e38, ALU.add, ALU.max, sm[:, s, 2 + br:3 + br]).then_inc(masked, 1)
                dve.wait_ge(masked, 2 * (n + 1))
                V.tensor_scalar(sm[:, s, 0:2], sm[:, s, 2:4], -SCALE, None, ALU.mult).then_inc(negmax, 1)

            def after(n):
                t, hd = units[n]
                K = P * (t + 1)
                s = n % 3
                dve.wait_ge(expd, 2 * (n + 1))
                st.add(V.reciprocal(sm[:, s, 6:8], sm[:, s, 4:6]))
                st.add(V.tensor_tensor(sm[:, s, 8:10], sm[:, s, 6:8], gates[:, t, NH + hd:2 * NH + hd + 1:NH], ALU.mult))
                for br in range(2):
                    V.tensor_scalar(PP[:, s, br, 0:K], PP[:, s, br, 0:K], sm[:, s, 8 + br:9 + br], None, ALU.mult)\
                        .then_inc(weighted, 1)

            def copy_out(n):
                t, hd = units[n]
                if hd % 2:
                    dve.wait_ge(summed, n + 1)
                    V.tensor_copy(OT[:, hd // 2, t * P:(t + 1) * P], ps[5 + (n // 2) % 2][:, 0:P]).then_inc(out, 1)

            compressed(0)
            before(0)
            for n in range(NU + 2):
                if n + 1 < NU:
                    before(n + 1)
                if n < NU:
                    after(n)
                if n >= 2:
                    copy_out(n - 2)
                if n == NH:
                    compressed(1)


def output_projection(nc, M):
    H, OT, ps, WO = M["H"], M["XT"], M["ps"], view(M, Map.WO, KD, D)
    with ExitStack() as ctx:
        sem = lambda n: new_sem(nc, M, "out_" + n)
        product, added = sem("product_ready"), sem("added")
        block = ctx.enter_context(nc.Block())
        parts = [(i, rows, half) for i, rows in enumerate(TILE_ROWS) for half in range(2)]

        @block.tensor
        def _(pe):
            pe.wait_ge(M["wo_in"], 16)
            for n, (i, rows, half) in enumerate(parts):
                for k in range(KD):
                    last = pe.matmul(ps[n][0:rows, :], OT[:, k, i * P:i * P + rows], WO[:, k, half * 512:(half + 1) * 512],
                                     start=(k == 0), stop=(k == KD - 1))
                last.then_inc(product, 1)

        @block.vector
        def _(dve):
            for n, (i, rows, half) in enumerate(parts):
                dve.wait_ge(product, n + 1)
                hv = H[0:rows, i, half * 512:(half + 1) * 512]
                nc.vector.tensor_tensor(hv, ps[n][0:rows, :], hv, ALU.add).then_inc(added, 1)


def constant_tables():
    import numpy as np
    tables = {name: np.zeros((P, n), np.float32) for name, n in NCONST.items()}

    def put(name, a):
        a = np.asarray(a, np.float32)
        a = a.reshape(a.shape[0], -1)
        table, at, w = CONST[name]
        assert a.shape[1] == w
        tables[table][:a.shape[0], at:at + w] = a

    p = np.arange(P)
    put("ident", np.eye(P))
    put("blockones", (p[:, None] // HD == p[None] // HD))
    grp, step = p // (HPG * STEPS), p % STEPS
    put("headsum", (grp[:, None] == grp[None]) & (step[:, None] == step[None]))
    q = np.arange(SEQ).reshape(2, P).T
    put("causal", np.where(np.arange(SEQ)[None, None] <= q[:, :, None], 0.0, NEG))
    ok = (np.arange(NCP) * CHUNK + 2 * CHUNK - 1)[None, None] <= q[:, :, None]
    put("cmpadd", np.where(ok, 0.0, NEG))
    put("cmpmul", ok)
    b, col = np.arange(NSEQ), np.arange(NEWTOK)
    mine = (col[None, None] // STEPS == b[None, :, None]) & (col[None, None] % STEPS <= step[:, None, None])
    put("newmask", np.where(mine, 0.0, NEG))
    put("winmask", np.where(np.arange(STEPS)[None] > step[:, None], 0.0, NEG))
    put("iota", np.tile(np.arange(1, NSB - 2), (P, 1)))
    r = np.arange(NEWTOK)
    put("stepsel", (r[:, None] % STEPS) == np.arange(STEPS)[None])
    put("seqsel", (r[:, None] // STEPS) == np.arange(NSEQ)[None])
    put("first", np.tile(np.arange(NG, 0, -1), (P, 1)))
    put("before", p[:, None] < p[None])
    put("ones", np.ones((P, P)))
    put("slots", np.tile(np.arange(CAP), (P, 1)))
    put("experts", np.tile(np.arange(NE), (P, 1)))
    half = HD // 2
    inv = np.float32(1.0) / (np.float32(10000.0) ** (np.arange(half, dtype=np.float32) * np.float32(2.0 / HD)))
    pos = np.zeros((P, NT), np.float32)
    pos[:, 0], pos[:, 1] = p, p + P
    pos[:NEWTOK, 2] = PAST + r % STEPS
    ang = (pos[:, :, None] * inv[None, None]).astype(np.float32)
    put("cos", np.cos(ang))
    put("sin", np.sin(ang))
    return tables


def pooling_matrices():
    import numpy as np
    m = np.zeros((P, NPOOL, NPM), np.float32)
    for g, w in enumerate(POOL_WINDOWS):
        for t in range(SEQ):
            lo = max(t + 1 - w, 0)
            for s in range(lo, t + 1):
                m[s % P, g, (s // P) * SEQ + t] += np.float32(1.0 / (t + 1 - lo))
            m[t % P, g, (t // P) * SEQ + t] -= 1.0
        for b in range(NSEQ):
            for t in range(STEPS):
                for s in range(STATE + t + 1 - w, STATE + t + 1):
                    if s < STATE:
                        m[b * STATE + s, g, 2 * SEQ + b * STEPS + t] += 1.0 / w
                    else:
                        m[b * STEPS + s - STATE, g, 2 * SEQ + NEWTOK + b * STEPS + t] += 1.0 / w
                m[b * STEPS + t, g, 2 * SEQ + NEWTOK + b * STEPS + t] -= 1.0
    return m


_PLAIN = ["x_prompt", "x_sample", "state_pool", "state_win", "norm_mix", "norm_ffn", "pool_w", "pool_scale", "w_kv", "cmp_w1",
          "cmp_b1", "cmp_w2", "w_qg", "w_o", "router_group", "router_expert", "w_gate_up", "w_down", "k_norm", "q_norm"]
_OUTS = [("y_prompt", (1, SEQ, D)), ("y_sample", (NSEQ, STEPS, D)), ("new_pool_prompt", (1, 1, STATE, D)),
         ("new_pool_sample", (1, NSEQ, STATE, D)), ("new_kv_prompt", (1, SEQ, 4, NKV, HD)),
         ("new_kv_sample", (NSEQ, STEPS, 4, NKV, HD)), ("new_win_prompt", (1, SEQ, 2, NKV, HD)),
         ("new_win_sample", (NSEQ, WIN, 2, NKV, HD))]


def kernel(**inputs):
    import numpy as np
    import concourse.bacc as bacc
    from concourse.bass_utils import run_bass_kernel_spmd

    x = {k: np.asarray(v) for k, v in inputs.items()}
    arrays = {n: x[n] for n in _PLAIN}
    tables = constant_tables()
    arrays["consts"], arrays["attention_consts"] = tables["C"], tables["CA"]
    arrays["pool_mats"] = pooling_matrices()
    gains = [x["norm_mix"][0], x["norm_ffn"][0], x["norm_mix"][1], x["kv_norm"], x["norm_ffn"][1]]
    arrays["gainsT"] = np.stack([g.reshape(KD, P).T for g in gains], axis=1)
    arrays["page_ids"] = x["page_table"].reshape(1, -1)
    pages = x["cache_kv"]
    n = pages.shape[0]
    raw = pages[:, :, 0:2].reshape(n, PAGE // CHUNK, CHUNK // 2, 2, 2, NKV, HD)
    arrays["pages_raw"] = raw.transpose(0, 3, 6, 4, 2, 5, 1).reshape(n, P, -1)
    ksel = pages[:, :, 2].reshape(n, PAGE, 2, P).transpose(0, 3, 2, 1).reshape(n, P, 2 * PAGE)
    arrays["pages_sel"] = np.concatenate([ksel, pages[:, :, 3].reshape(n, PAGE, NKV * HD)], axis=2)
    arrays["win_keysT"] = x["state_win"][:, :, 0].reshape(NSEQ, WIN, 2, P).transpose(0, 3, 2, 1).reshape(NSEQ, P, 2 * WIN)
    arrays["cmp_pe"] = x["cmp_pe"].reshape(2, 2, CHUNK // 2, P).transpose(3, 0, 1, 2)
    arrays["k_gainT"] = np.concatenate([x["k_norm"][0], x["k_norm"][0]]).reshape(P, 1)

    nc = bacc.Bacc("TRN2", target_bir_lowering=False, num_devices=1)
    feed, I, O = {}, {}, {}
    for name, a in arrays.items():
        a = np.ascontiguousarray(a)
        feed[f"in_{name}"] = a
        I[name] = nc.dram_tensor(f"in_{name}", a.shape, mybir.dt.from_np(a.dtype), kind="ExternalInput").ap()
    for name, shape in _OUTS:
        O[name] = nc.dram_tensor(f"out_{name}", shape, F32, kind="ExternalOutput").ap()
    build(nc, I, O)
    r = run_bass_kernel_spmd(nc, [feed], core_ids=[0])
    return tuple(r.results[0][f"out_{name}"] for name, _ in _OUTS)
```

```python
from contextlib import ExitStack, contextmanager

import concourse.bass as bass
from concourse import mybir

F32 = mybir.dt.float32
F32R = mybir.dt.float32r
I32 = mybir.dt.int32
ALU = mybir.AluOpType
ACT = mybir.ActivationFunctionType
AX = mybir.AxisListType

P = 128
D = 1024
KD = D // P
SEQ, NSEQ, STEPS = 256, 8, 8
NEWTOK = NSEQ * STEPS
TOK = SEQ + NEWTOK
TILE_ROWS = (P, P, NEWTOK)
NT = len(TILE_ROWS)
PAST, PAGE = 1024, 128
NPAGE = PAST // PAGE
WIN = 512
POOL_WINDOWS = (2, 4, 8, 16)
NPOOL = len(POOL_WINDOWS)
STATE = max(POOL_WINDOWS) - 1
GD = D // NPOOL
HD, NH, NKV = 64, 16, 4
HPG = NH // NKV
CHUNK = 16
HID = 2 * HD
NCP = SEQ // CHUNK - 1
NCS = PAST // CHUNK - 1
SELB = 64
NSB = PAST // SELB + 1
NE, NG, EPG, FE = 16, 4, 4, 512
CAP = 64
SCALE = HD ** -0.5
EPS = 1e-6
NEG = -1e30

CONST = {}
NCONST = {"C": 0, "CA": 0}
for _table, _name, _w in (("C", "ident", P), ("C", "first", NG), ("C", "before", P), ("C", "ones", P),
                          ("C", "slots", CAP), ("C", "experts", NE),
                          ("CA", "blockones", P), ("CA", "headsum", P), ("CA", "causal", 2 * SEQ),
                          ("CA", "cmpadd", 2 * NCP), ("CA", "cmpmul", 2 * NCP), ("CA", "newmask", NSEQ * NEWTOK),
                          ("CA", "winmask", STEPS), ("CA", "iota", NSB - 3), ("CA", "stepsel", STEPS),
                          ("CA", "seqsel", NSEQ), ("CA", "cos", NT * HD // 2), ("CA", "sin", NT * HD // 2)):
    CONST[_name] = (_table, NCONST[_table], _w)
    NCONST[_table] += _w
NPM = SEQ * 2 + NEWTOK * 2


ARENA = 44288


class Map:
    WKV, WQG = 0, 12288
    HEADS = 20864
    KVROWS = HEADS + NT * 24 * HD
    WINROWS = KVROWS + NT * 4 * NKV * HD
    QROPE = 31248
    XT2 = 35344
    GAIN24 = XT2 + KD * TOK
    SQ = GAIN24 + 24 * HD
    ROT = SQ + 24 * HD
    QNT, QRT = 0, 2048
    QSN, QSR = 4096, 4608
    QB = 5120
    KTP = 8192
    KTN = KTP + 2 * 2 * SEQ
    VP = KTN + 2 * 2 * NEWTOK
    GS = VP + 2 * 2 * NKV * 3 * HD
    CKP = GS + 3 * NSEQ
    CVP = CKP + 2 * CHUNK
    W1 = 13600
    W2 = W1 + 2 * 2 * 8 * HID
    BIAS = W2 + 2 * 3 * HD
    PE = BIAS + 2 * HID
    ONES = PE + 32
    VNEW = 18700
    SMALL = VNEW + NKV * HD
    GATEL = SMALL + 256
    CV = HEADS
    PC = CV + NSEQ * NKV * HD
    BM = PC + NSEQ * HD
    RP = BM + NSEQ * 16
    CHUNKS = QROPE + NT * NH * HD
    RAW = (RP + 2 * 8 * NKV * CHUNK, 33664)
    SEL = (RP, 33664, W1)
    WINB = (RP + NPAGE * 512, 33664 + NPAGE * 512, 33664 + NPAGE * 512 + 4 * WIN)
    HIDB = 30080
    CKB = HIDB + 4 * 256
    PT = 30080
    PROW = (QB + 3 * 2 * P, 41856, PT + 14 * P)
    WO = 33664
    PTC = HEADS
    PTP = PTC + 2 * NH * P
    PP = 30080


class Steps:

    def __init__(self, eng, sem, base=0):
        self.eng, self.sem, self.n, self.base = eng, sem, 0, base

    def add(self, ins):
        ins.then_inc(self.sem, 1)
        self.n += 1
        self.eng.wait_ge(self.sem, self.base + self.n)


def build(nc, I, O):
    with ExitStack() as ctx:
        def sb(name, shape, dtype=F32):
            return ctx.enter_context(nc.sbuf_tensor(name, shape, dtype))

        M = {}
        M["H"] = sb("residual", [P, NT, D])
        M["C"] = sb("constants", [P, NCONST["C"]])
        M["gT"] = sb("gainsT", [P, 5, KD])
        M["stat"] = sb("row_stats", [P, 64])
        M["gates"] = sb("gates", [P, NT, 3 * NH])
        M["pages"] = sb("page_ids", [1, NSEQ * NPAGE], I32)
        M["kgain"] = sb("compressed_key_gain", [P, 1])
        M["sems"] = []
        M["ps"] = [ctx.enter_context(nc.psum_tensor(f"bank{i}", [P, 512], F32)) for i in range(8)]
        M["spill"] = nc.dram_tensor("ffn_input_T", [P, KD * TOK], F32, kind="Internal").ap()

        M["pool_rows_in"], M["pool_mats_in"] = new_sem(nc, M, "pool_rows_landed"), new_sem(nc, M, "pool_mats_landed")
        with region(nc, M, "a", 16384):
            load_constants(nc, I, M)
            pool_mixer(nc, I, O, M)
        ffn(nc, I, M, 0)
        clear_sems(nc, M)
        with region(nc, M, "b", ARENA), nc.sbuf_tensor("attention_constants", [P, NCONST["CA"]], F32) as CA:
            M["CA"] = CA
            M["wo_in"] = new_sem(nc, M, "w_o_landed")
            stage_attention(nc, I, O, M)
        clear_sems(nc, M)
        ffn(nc, I, M, 1)
        store_result(nc, O, M)


@contextmanager
def region(nc, M, tag, words):
    with nc.sbuf_tensor("modelT_" + tag, [P, KD, TOK], F32) as XT, \
            nc.sbuf_tensor("arena_" + tag, [P, words], F32) as A:
        M["XT"], M["A"] = XT, A
        yield
        del M["XT"], M["A"]


def new_sem(nc, M, name):
    M["sems"].append(nc.alloc_semaphore(name))
    return M["sems"][-1]


def clear_sems(nc, M):
    nc.clear_and_free_semaphores(M["sems"])
    M["sems"] = []
    nc.all_engine_barrier()


def const(M, name, rows=P):
    table, at, w = CONST[name]
    return M[table][0:rows, at:at + w]


def load_constants(nc, I, M):
    with ExitStack() as ctx:
        landed = new_sem(nc, M, "constants_landed")
        block = ctx.enter_context(nc.Block())

        @block.sync
        def _(sp):
            sp.dma_start(M["C"][:, :], I["consts"]).then_inc(landed, 16)
            sp.dma_start(M["gT"][:, :, :], I["gainsT"]).then_inc(landed, 16)
            sp.dma_start(M["pages"][:, :], I["page_ids"]).then_inc(landed, 16)
            for i, rows in enumerate(TILE_ROWS):
                src = I["x_prompt"][0, i * P:(i + 1) * P, :] if i < 2 else \
                    I["x_sample"].rearrange("b t d -> (b t) d")
                sp.dma_start(M["H"][0:rows, i, :], src).then_inc(landed, 16)
            gain, pscale, SP, PM, PW = pool_operands(M)
            rows_in, mats_in = M["pool_rows_in"], M["pool_mats_in"]
            sp.dma_start(gain, I["norm_mix"][0:1, :].broadcast_to([P, D])).then_inc(rows_in, 16)
            sp.dma_start(pscale, I["pool_scale"][0:1, :].broadcast_to([P, D])).then_inc(rows_in, 16)
            sp.dma_start(SP[0:STATE * NSEQ, :], I["state_pool"][0].rearrange("b r d -> (b r) d")).then_inc(mats_in, 16)
            sp.dma_start(PM, I["pool_mats"]).then_inc(mats_in, 16)
            sp.dma_start(PW, I["pool_w"][0].rearrange("g (k p) n -> p g k n", p=P)).then_inc(mats_in, 16)
            sp.wait_ge(landed, 16 * 6)

        @block.vector
        def _(dve):
            nc.vector.memset(M["gates"][:, :, :], 0.0)
            nc.vector.memset(M["stat"][:, :], 1.0)


def row_sums(act, scratch, stat, src, summed, rooted, scaled):
    for i, rows in enumerate(TILE_ROWS):
        act.activation(scratch[0:rows, :], src[0:rows, i, :], ACT.Square,
                       accum_out=stat[0:rows, i:i + 1]).then_inc(summed, 1)
        act.wait_ge(summed, i + 1)
    act.wait_ge(scaled, 1)
    act.activation(stat[:, 8:8 + NT], stat[:, 4:4 + NT], ACT.Sqrt).then_inc(rooted, 1)


def pool_operands(M):
    A, at = M["A"], 6 * D
    PM = A[:, at:at + NPOOL * NPM].rearrange("p (g n) -> p g n", g=NPOOL)
    at += NPOOL * NPM
    PW = A[:, at:at + NPOOL * 2 * GD].rearrange("p (g k n) -> p g k n", g=NPOOL, k=2)
    return A[:, 0:D], A[:, D:2 * D], A[:, 5 * D:6 * D], PM, PW


def pool_mixer(nc, I, O, M):
    A, H, XT, ps = M["A"], M["H"], M["XT"], M["ps"]
    gain, pscale, SP, PM, PW = pool_operands(M)
    XN = A[:, 2 * D:5 * D].rearrange("p (i n) -> p i n", i=NT)
    at = 6 * D + NPOOL * NPM + NPOOL * 2 * GD
    scratch = A[:, at:at + D]
    prod = A[:, at + D:at + 2 * D]
    stat = M["stat"]
    S = STATE * NSEQ
    with ExitStack() as ctx:
        sem = lambda n: new_sem(nc, M, n)
        rows_in, mats_in = M["pool_rows_in"], M["pool_mats_in"]
        summed, scaled, rooted = sem("pool_summed"), sem("pool_scaled"), sem("pool_rooted")
        chain, xn_ready = sem("pool_chain"), sem("pool_xn_ready")
        mixed, mix_copied = sem("pool_mixed"), sem("pool_mix_copied")
        projected, added, stored = sem("pool_projected"), sem("pool_added"), sem("pool_stored")
        block = ctx.enter_context(nc.Block())

        @block.sync
        def _(sp):
            sp.dma_start(O["new_pool_sample"][0, :, 0:STATE - STEPS, :],
                         I["state_pool"][0, :, STEPS:STATE, :]).then_inc(stored, 16)
            sp.wait_ge(xn_ready, NT)
            sp.dma_start(O["new_pool_prompt"][0, 0], XN[P - STATE:P, 1, :]).then_inc(stored, 16)
            for b in range(NSEQ):
                sp.dma_start(O["new_pool_sample"][0, b, STATE - STEPS:STATE, :],
                             XN[b * STEPS:(b + 1) * STEPS, 2, :]).then_inc(stored, 16)
            sp.wait_ge(stored, 16 * (2 + NSEQ))

        @block.scalar
        def _(act):
            row_sums(act, scratch, stat, H, summed, rooted, scaled)
            for c in range(KD):
                act.wait_ge(mixed, c + 1)
                nc.scalar.copy(XT[:, c, :], ps[c % 2][:, 0:TOK]).then_inc(mix_copied, 1)

        @block.vector
        def _(dve):
            st = Steps(dve, chain)
            row_rstd(nc, dve, st, stat, summed, scaled, rooted, D)
            dve.wait_ge(rows_in, 32)
            for i, rows in enumerate(TILE_ROWS):
                nc.vector.scalar_tensor_tensor(XN[0:rows, i, :], H[0:rows, i, :], stat[0:rows, 12 + i:13 + i],
                                               gain[0:rows, :], ALU.mult, ALU.mult).then_inc(xn_ready, 1)
            for i, rows in enumerate(TILE_ROWS):
                for half in range(2):
                    dve.wait_ge(projected, 2 * i + half + 1)
                    cols = slice(half * 512, half * 512 + 512)
                    st.add(nc.vector.tensor_tensor(prod[0:rows, cols], ps[2 + (2 * i + half) % 4][0:rows, :],
                                                   pscale[0:rows, cols], ALU.mult))
                    nc.vector.tensor_tensor(H[0:rows, i, cols], H[0:rows, i, cols], prod[0:rows, cols],
                                            ALU.add).then_inc(added, 1)
            dve.wait_ge(added, 2 * NT)

        @block.tensor
        def _(pe):
            pe.wait_ge(mats_in, 48)
            pe.wait_ge(xn_ready, NT)
            for c in range(KD):
                if c >= 2:
                    pe.wait_ge(mix_copied, c - 1)
                cs, g, bank = slice(c * P, c * P + P), c * P // GD, ps[c % 2]
                pe.matmul(bank[:, 0:SEQ], XN[:, 0, cs], PM[:, g, 0:SEQ], start=True, stop=False)
                pe.matmul(bank[:, 0:SEQ], XN[:, 1, cs], PM[:, g, SEQ:2 * SEQ], start=False, stop=True)
                pe.matmul(bank[:, SEQ:TOK], SP[0:S, cs], PM[0:S, g, 2 * SEQ:2 * SEQ + NEWTOK],
                          start=True, stop=False)
                pe.matmul(bank[:, SEQ:TOK], XN[0:NEWTOK, 2, cs], PM[0:NEWTOK, g, 2 * SEQ + NEWTOK:NPM],
                          start=False, stop=True).then_inc(mixed, 1)
            pe.wait_ge(mix_copied, KD)
            for i, rows in enumerate(TILE_ROWS):
                for half in range(2):
                    n = 2 * i + half
                    if n >= 4:
                        pe.wait_ge(added, n - 3)
                    for g in (2 * half, 2 * half + 1):
                        for k in range(2):
                            last = pe.matmul(ps[2 + n % 4][0:rows, (g % 2) * GD:(g % 2 + 1) * GD],
                                             XT[:, 2 * g + k, i * P:i * P + rows], PW[:, g, k, :],
                                             start=(k == 0), stop=(k == 1))
                    last.then_inc(projected, 1)


def row_rstd(nc, dve, st, stat, summed, scaled, rooted, width):
    dve.wait_ge(summed, NT)
    nc.vector.tensor_scalar(stat[:, 4:4 + NT], stat[:, 0:NT], 1.0 / width, EPS, ALU.mult, ALU.add)\
        .then_inc(scaled, 1)
    dve.wait_ge(rooted, 1)
    st.add(nc.vector.reciprocal(stat[:, 12:12 + NT], stat[:, 8:8 + NT]))


def norm_transpose(nc, I, M, tag, targets):
    H, ps, stat, gT = M["H"], M["ps"], M["stat"], M["gT"]
    Z = M["A"][:, 31248:31248 + NT * D].rearrange("p (i n) -> p i n", i=NT)
    scratch = M["A"][:, 31248 + NT * D:31248 + (NT + 1) * D]
    ident = const(M, "ident")
    with ExitStack() as ctx:
        sem = lambda n: new_sem(nc, M, tag + n)
        summed, scaled, rooted, chain = sem("_summed"), sem("_scaled"), sem("_rooted"), sem("_chain")
        z_ready, turned, copied = sem("_z_ready"), sem("_turned"), sem("_copied")
        consts_in = sem("_constants_landed")
        block = ctx.enter_context(nc.Block())

        @block.sync
        def _(sp):
            sp.dma_start(M["CA"][:, :], I["attention_consts"]).then_inc(consts_in, 16)
            load_projections(sp, I, M)
            sp.wait_ge(consts_in, 16)

        @block.scalar
        def _(act):
            row_sums(act, scratch, stat, H, summed, rooted, scaled)

        @block.vector
        def _(dve):
            st = Steps(dve, chain)
            row_rstd(nc, dve, st, stat, summed, scaled, rooted, D)
            for i, rows in enumerate(TILE_ROWS):
                nc.vector.tensor_scalar(Z[0:rows, i, :], H[0:rows, i, :], stat[0:rows, 12 + i:13 + i], None,
                                        ALU.mult).then_inc(z_ready, 1)
            n = 0
            for i, rows in enumerate(TILE_ROWS):
                for half in range(2):
                    dve.wait_ge(turned, n + 1)
                    for gi, T in targets:
                        last = nc.vector.tensor_tensor(
                            T[:, 4 * half:4 * half + 4, i * P:i * P + rows],
                            ps[n % 4][:, 0:4 * rows].rearrange("p (k t) -> p k t", k=4),
                            gT[:, gi, 4 * half:4 * half + 4].unsqueeze(2).broadcast_to([P, 4, rows]), ALU.mult)
                    last.then_inc(copied, 1)
                    n += 1
            dve.wait_ge(copied, n)

        @block.tensor
        def _(pe):
            n = 0
            for i, rows in enumerate(TILE_ROWS):
                pe.wait_ge(z_ready, i + 1)
                for half in range(2):
                    if n >= 4:
                        pe.wait_ge(copied, n - 3)
                    for k in range(4):
                        c = 4 * half + k
                        last = pe.transpose(ps[n % 4][:, k * rows:(k + 1) * rows],
                                            Z[0:rows, i, c * P:(c + 1) * P], ident[0:rows, 0:rows])
                    last.then_inc(turned, 1)
                    n += 1


def route(nc, I, M, R, layer, landed):
    XT, A, ps, comb = M["XT"], M["A"], M["ps"], R["comb"]
    at = [0]

    def take(n, k=1):
        v = A[:, at[0]:at[0] + NT * n * k]
        at[0] += NT * n * k
        return v.rearrange("p (i n) -> p i n", i=NT)

    WR = A[:, WR_AT:WR_AT + KD * (NG + NE)].rearrange("p (k n) -> p k n", k=KD)
    L = take(NG + NE)
    gbest, ghot, gkey, gkmax, gexp, gsum, gval = (take(1), take(NG), take(NG), take(1), take(NG), take(1), take(1))
    le, prod = take(EPG), take(NE)
    m1, m2, hot1, hot2, key, kmax, le2 = take(1), take(1), take(EPG), take(EPG), take(EPG), take(1), take(EPG)
    diff, ratio, den, w1, w2, share = take(1), take(1), take(1), take(1), take(1), take(EPG)
    hot2w = take(EPG)
    first = const(M, "first")

    def wide(x, n):
        return x.broadcast_to([P, NT, n])

    with ExitStack() as ctx:
        sem = lambda n: new_sem(nc, M, f"route{layer}_{n}")
        w_in, logits, chain = R["router_in"], sem("logits_ready"), sem("chain")
        exp_in, exp_out = sem("exp_asked"), sem("exp_done")
        member_in, ranks, spilled = sem("members_ready"), sem("ranks_ready"), sem("spilled")
        block = ctx.enter_context(nc.Block())

        @block.sync
        def _(sp):
            sp.dma_start(M["spill"], XT[:, :, :].rearrange("p k t -> p (k t)")).then_inc(spilled, 16)
            sp.wait_ge(spilled, 16)
            for p in range(STAGES, KD):
                sp.wait_ge(R["low"], p - STAGES + 1)
                load_piece(sp, I, R, layer, landed, 0, p)

        @block.tensor
        def _(pe):
            pe.wait_ge(w_in, 32)
            for i, rows in enumerate(TILE_ROWS):
                for k in range(KD):
                    last = pe.matmul(ps[0][0:rows, 32 * i:32 * i + NG + NE], XT[:, k, i * P:i * P + rows], WR[:, k, :],
                                     start=(k == 0), stop=(k == KD - 1))
            last.then_inc(logits, 1)
            pe.wait_ge(member_in, 1)
            for i in range(NT + 1):
                out = ps[1][:, i * NE:(i + 1) * NE]
                for j in range(min(i, NT - 1) + 1):
                    own = i == j
                    last = pe.matmul(out, const(M, "before" if own and i < NT else "ones"), R["member"][:, j, :],
                                     start=(j == 0), stop=(j == min(i, NT - 1)))
            last.then_inc(ranks, 1)

        @block.scalar
        def _(act):
            for p in range(KD):
                act.wait_ge(landed[p % STAGES], 16 * (1 + p // STAGES))
                split_high(nc, R, p)
            act.wait_ge(exp_in, 1)
            act.activation(gexp, gkey, ACT.Exp).then_inc(exp_out, 1)
            act.wait_ge(exp_in, 2)
            act.activation(ratio, diff, ACT.Exp).then_inc(exp_out, 1)

        @block.vector
        def _(dve):
            for p in range(KD):
                dve.wait_ge(R["high"], p + 1)
                split_low(nc, R, p)
            st = Steps(dve, chain)
            V = nc.vector
            st.add(V.memset(L, 0.0))
            dve.wait_ge(logits, 1)
            for i, rows in enumerate(TILE_ROWS):
                st.add(V.tensor_copy(L[0:rows, i, :], ps[0][0:rows, 32 * i:32 * i + NG + NE]))
            lg = L[:, :, 0:NG]

            def hot_of(out, src, best, keyt, kmaxt, n):
                st.add(V.tensor_reduce(best, src, AX.X, ALU.max))
                st.add(V.tensor_tensor(keyt, src, wide(best, n), ALU.is_equal))
                st.add(V.tensor_tensor(keyt, keyt, first.unsqueeze(1).broadcast_to([P, NT, n]), ALU.mult))
                st.add(V.tensor_reduce(kmaxt, keyt, AX.X, ALU.max))
                st.add(V.tensor_tensor(out, wide(kmaxt, n), first.unsqueeze(1).broadcast_to([P, NT, n]), ALU.is_equal))

            hot_of(ghot, lg, gbest, gkey, gkmax, NG)
            V.tensor_tensor(gkey, lg, wide(gbest, NG), ALU.subtract).then_inc(exp_in, 1)
            dve.wait_ge(exp_out, 1)
            st.add(V.tensor_reduce(gsum, gexp, AX.X, ALU.add))
            st.add(V.reciprocal(gval, gsum))
            st.add(V.tensor_tensor(prod.rearrange("p i (g e) -> p i g e", g=NG),
                                   L[:, :, NG:].rearrange("p i (g e) -> p i g e", g=NG),
                                   ghot.unsqueeze(3).broadcast_to([P, NT, NG, EPG]), ALU.mult))
            st.add(V.tensor_reduce(le, prod.rearrange("p i (g e) -> p i e g", g=NG), AX.X, ALU.add))
            hot_of(hot1, le, m1, key, kmax, EPG)
            st.add(V.tensor_scalar(le2, hot1, NEG, None, ALU.mult))
            st.add(V.tensor_tensor(le2, le2, le, ALU.add))
            hot_of(hot2, le2, m2, key, kmax, EPG)
            V.tensor_tensor(diff, m2, m1, ALU.subtract).then_inc(exp_in, 1)
            dve.wait_ge(exp_out, 2)
            st.add(V.tensor_scalar(den, ratio, 1.0, None, ALU.add))
            st.add(V.reciprocal(den, den))
            st.add(V.tensor_tensor(w1, den, gval, ALU.mult))
            st.add(V.tensor_tensor(w2, w1, ratio, ALU.mult))
            st.add(V.tensor_tensor(share, hot1, wide(w1, EPG), ALU.mult))
            st.add(V.tensor_tensor(hot2w, hot2, wide(w2, EPG), ALU.mult))
            st.add(V.tensor_tensor(share, share, hot2w, ALU.add))
            st.add(V.tensor_tensor(comb[:, :, :].rearrange("p i (g e) -> p i g e", g=NG),
                                   ghot.unsqueeze(3).broadcast_to([P, NT, NG, EPG]),
                                   share.unsqueeze(2).broadcast_to([P, NT, NG, EPG]), ALU.mult))
            member, rank, over = R["member"], R["rank"], R["comb_over"]
            st.add(V.tensor_tensor(le2, hot1, hot2, ALU.add))
            st.add(V.tensor_tensor(member[:, :, :].rearrange("p i (g e) -> p i g e", g=NG),
                                   ghot.unsqueeze(3).broadcast_to([P, NT, NG, EPG]),
                                   le2.unsqueeze(2).broadcast_to([P, NT, NG, EPG]), ALU.mult))
            V.memset(member[NEWTOK:P, NT - 1, :], 0.0).then_inc(member_in, 1)
            st.add(V.tensor_copy(R["combp"][:, :, :, 0], comb[:, :, :]))
            st.add(V.tensor_tensor(R["combp"][:, :, :, 1], comb[:, :, :], R["combp"][:, :, :, 0].bitcast(F32), ALU.subtract))
            dve.wait_ge(ranks, 1)
            pos = ps[1][:, 0:NT * NE].rearrange("p (i e) -> p i e", i=NT)
            st.add(V.tensor_scalar(rank[:, :, :], pos, 1.0, None, ALU.add))
            st.add(V.tensor_tensor(rank[:, :, :], rank[:, :, :], member[:, :, :], ALU.mult))
            st.add(V.tensor_scalar(rank[:, :, :], rank[:, :, :], -1.0, None, ALU.add))
            st.add(V.tensor_scalar(over[:, :, :], rank[:, :, :], float(CAP), None, ALU.is_ge))
            st.add(V.tensor_tensor(over[:, :, :], over[:, :, :], comb[:, :, :], ALU.mult))
            flag, count, hit = R["list"][0:1, 0:NE], R["list"][0:1, NE:2 * NE], A[0:1, 4400:4400 + MAXOVER * NE]
            st.add(V.tensor_scalar(flag, ps[1][0:1, NT * NE:(NT + 1) * NE], float(CAP), None, ALU.is_gt))
            st.add(V.tensor_copy(count, flag))
            step = 1
            while step < NE:
                tmp = A[0:1, 4380:4380 + NE]
                st.add(V.tensor_copy(tmp, count))
                st.add(V.tensor_tensor(count[:, step:], tmp[:, step:], tmp[:, 0:NE - step], ALU.add))
                step *= 2
            hitv = hit.rearrange("p (k e) -> p k e", k=MAXOVER)
            ranked = const(M, "experts", 1)[:, 0:MAXOVER].unsqueeze(2).broadcast_to([1, MAXOVER, NE])
            st.add(V.tensor_tensor(hitv, count.unsqueeze(1).broadcast_to([1, MAXOVER, NE]), ranked, ALU.subtract))
            st.add(V.tensor_scalar(hit, hit, 1.0, None, ALU.is_equal))
            st.add(V.tensor_tensor(hitv, hitv, flag.unsqueeze(1).broadcast_to([1, MAXOVER, NE]), ALU.mult))
            st.add(V.tensor_tensor(hitv, hitv, const(M, "experts", 1).unsqueeze(1).broadcast_to([1, MAXOVER, NE]), ALU.mult))
            ids = R["list"][0:1, 2 * NE:2 * NE + MAXOVER]
            st.add(V.tensor_reduce(ids, hitv, AX.X, ALU.add))
            st.add(V.tensor_copy(R["over"][0:1, 0:MAXOVER], ids))
            st.add(V.tensor_copy(R["over"][0:1, MAXOVER:MAXOVER + 1], count[:, NE - 1:NE]))


MAXOVER = min(NE, 2 * TOK // (CAP + 1))
NF = FE // P
PIECES = KD + NF
STAGES = 6
WR_AT = 5 * D


def ffn(nc, I, M, layer):
    with ExitStack() as ctx:
        def sb(name, shape, dtype=F32):
            return ctx.enter_context(nc.sbuf_tensor(f"ffn{layer}_{name}", shape, dtype))

        R = {
            "comb": sb("weights", [P, NT, NE]), "comb_over": sb("weights_over", [P, NT, NE]),
            "combp": sb("weight_parts", [P, NT, NE, 2], F32R), "member": sb("member", [P, NT, NE]),
            "rank": sb("rank", [P, NT, NE]), "list": sb("over_list", [1, 3 * NE]),
            "over": sb("over_ids", [1, MAXOVER + 1], I32),
            "xp": sb("x_parts", [P, 2, NT, D], F32R),
            "stage": sb("landing", [P, STAGES, D]),
            "router_in": new_sem(nc, M, f"ffn{layer}_router_weights_landed"),
            "high": new_sem(nc, M, f"ffn{layer}_high_part_ready"), "low": new_sem(nc, M, f"ffn{layer}_low_part_ready"),
        }
        landed = [new_sem(nc, M, f"ffn{layer}_piece_landed{n}") for n in range(STAGES)]
        with nc.sbuf_tensor(f"ffn{layer}_piece_parts", [P, PIECES, 2, D], F32R) as R["parts"]:
            with region(nc, M, f"f{layer}", 8192):
                ffn_input(nc, I, M, R, layer, landed)
                route(nc, I, M, R, layer, landed)
            moe(nc, I, M, R, layer, landed)
        moe_over(nc, I, M, R, layer)


def split_high(nc, R, p):
    nc.scalar.copy(R["parts"][:, p, 0, :], R["stage"][:, p % STAGES, :]).then_inc(R["high"], 1)


def split_low(nc, R, p):
    W = R["parts"]
    nc.vector.tensor_tensor(W[:, p, 1, :], R["stage"][:, p % STAGES, :], W[:, p, 0, :].bitcast(F32), ALU.subtract)\
        .then_inc(R["low"], 1)


def load_piece(sp, I, R, layer, landed, e, p):
    if p < KD:
        src = I["w_gate_up"][layer][bass.ds(e, 1), p * P:(p + 1) * P, :]
    else:
        src = I["w_down"][layer][bass.ds(e, 1), (p - KD) * P:(p - KD + 1) * P, :]
    sp.dma_start(R["stage"][:, p % STAGES, :], src.rearrange("a p n -> p (a n)")).then_inc(landed[p % STAGES], 16)


def ffn_input(nc, I, M, R, layer, landed):
    H, XT, ps, stat, XP = M["H"], M["XT"], M["ps"], M["stat"], R["xp"]
    XN = M["A"][:, 0:NT * D].rearrange("p (i n) -> p i n", i=NT)
    scratch, gain = M["A"][:, 3 * D:4 * D], M["A"][:, 4 * D:5 * D]
    ident = const(M, "ident")
    with ExitStack() as ctx:
        sem = lambda n: new_sem(nc, M, f"ffnin{layer}_" + n)
        gain_in, summed, scaled, rooted, chain = (sem("gain_landed"), sem("summed"), sem("scaled"), sem("rooted"),
                                                  sem("chain"))
        xn_ready, high, turned, by_dve, by_act = (sem("xn_ready"), sem("high_ready"), sem("turned"),
                                                  sem("copied_by_dve"), sem("copied_by_act"))
        block = ctx.enter_context(nc.Block())

        @block.sync
        def _(sp):
            sp.dma_start(gain, I["norm_ffn"][layer:layer + 1, :].broadcast_to([P, D])).then_inc(gain_in, 16)
            WR = M["A"][:, WR_AT:WR_AT + KD * (NG + NE)].rearrange("p (k n) -> p k n", k=KD)
            for cols, name in ((slice(0, NG), "router_group"), (slice(NG, NG + NE), "router_expert")):
                sp.dma_start(WR[:, :, cols], I[name][layer].rearrange("(k p) n -> p k n", p=P)).then_inc(R["router_in"], 16)
            for p in range(STAGES):
                load_piece(sp, I, R, layer, landed, 0, p)

        @block.scalar
        def _(act):
            row_sums(act, scratch, stat, H, summed, rooted, scaled)
            for i, rows in enumerate(TILE_ROWS):
                act.wait_ge(xn_ready, i + 1)
                nc.scalar.copy(XP[0:rows, 0, i, :], XN[0:rows, i, :]).then_inc(high, 1)
                act.wait_ge(turned, 2 * i + 2)
                nc.scalar.copy(XT[:, 4:8, i * P:i * P + rows],
                               ps[(2 * i + 1) % 4][:, 0:4 * rows].rearrange("p (k t) -> p k t", k=4)).then_inc(by_act, 1)

        @block.vector
        def _(dve):
            st = Steps(dve, chain)
            row_rstd(nc, dve, st, stat, summed, scaled, rooted, D)
            dve.wait_ge(gain_in, 16)
            for i, rows in enumerate(TILE_ROWS):
                nc.vector.scalar_tensor_tensor(XN[0:rows, i, :], H[0:rows, i, :], stat[0:rows, 12 + i:13 + i],
                                               gain[0:rows, :], ALU.mult, ALU.mult).then_inc(xn_ready, 1)
            for i, rows in enumerate(TILE_ROWS):
                dve.wait_ge(turned, 2 * i + 1)
                nc.vector.tensor_copy(XT[:, 0:4, i * P:i * P + rows],
                                      ps[(2 * i) % 4][:, 0:4 * rows].rearrange("p (k t) -> p k t", k=4)).then_inc(by_dve, 1)
                dve.wait_ge(high, i + 1)
                nc.vector.tensor_tensor(XP[0:rows, 1, i, :], XN[0:rows, i, :], XP[0:rows, 0, i, :].bitcast(F32),
                                        ALU.subtract)

        @block.tensor
        def _(pe):
            n = 0
            for i, rows in enumerate(TILE_ROWS):
                pe.wait_ge(xn_ready, i + 1)
                for half in range(2):
                    if n >= 4:
                        pe.wait_ge((by_dve, by_act)[half], i - 1)
                    for k in range(4):
                        c = 4 * half + k
                        last = pe.transpose(ps[n % 4][:, k * rows:(k + 1) * rows],
                                            XN[0:rows, i, c * P:(c + 1) * P], ident[0:rows, 0:rows])
                    last.then_inc(turned, 1)
                    n += 1


def reach(eng, sem, value):
    if not isinstance(value, int) or value > 0:
        eng.wait_ge(sem, value)


def over_experts(eng, body):
    for e in (0, 1):
        body(e, e % 2)
    with eng.Fori(1, NE // 2 - 1) as i:
        for s in range(2):
            body(i * 2 + s, s)
    for e in (NE - 2, NE - 1):
        body(e, e % 2)


def moe(nc, I, M, R, layer, landed):
    H, ps, XP = M["H"], M["ps"], R["xp"]
    ident, slots = const(M, "ident"), const(M, "slots")
    real = lambda e: not isinstance(e, int) or 0 <= e < NE
    with ExitStack() as ctx:
        def sb(name, shape, dtype=F32):
            return ctx.enter_context(nc.sbuf_tensor(f"moe{layer}_{name}", shape, dtype))

        W = R["parts"]
        SG = sb("gather", [P, 2, NT, 4 * CAP], F32R)
        XE = sb("gathered_rows", [P, D])
        XS = sb("gatheredT", [P, KD, P], F32R)
        GE = sb("gate_up_rows", [P, D])
        GT = sb("gate_upT", [P, 2, NF * CAP])
        SIL, HR = sb("silu", [P, NF * CAP]), sb("hidden", [P, NF * CAP])
        HT = sb("hidden_parts", [P, NF, P], F32R)
        ST = sb("scatter", [P, 2, TOK], F32R)
        YP = sb("down_parts", [P, 2, 2, D], F32R)
        WS = sb("slot_weight", [P, 2])
        sem = lambda n: new_sem(nc, M, f"moe{layer}_{n}")
        high, low, used = R["high"], R["low"], sem("piece_used")
        sg, gathered, xe, xturned, xs = (sem("gather_ready"), sem("rows_gathered"), sem("rows_copied"),
                                         sem("rows_turned"), sem("gatheredT_ready"))
        ge, gturned, gate, up, silu, hidden = (sem("gate_up_copied"), sem("gate_up_turned"), sem("gate_summed"),
                                               sem("up_summed"), sem("silu_ready"), sem("hidden_ready"))
        hh, hl, sturned, st_ready, wsum, ws = (sem("hidden_high"), sem("hidden_low"), sem("scatter_turned"),
                                               sem("scatter_ready"), sem("slot_weight_summed"), sem("slot_weight_ready"))
        yh, yl, scattered, added = sem("down_high"), sem("down_low"), sem("scattered"), sem("added")
        NY = 2 * NT
        BROUGHT = 16 * PIECES // STAGES
        block = ctx.enter_context(nc.Block())

        def taken(e, p):
            if p < KD:
                return p + 1 if isinstance(e, int) and e == 0 else e * PIECES + (p + 1 - NF)
            return e * PIECES + (p + 1 + KD - (KD if isinstance(e, int) and e == NE - 1 else 0))

        def landings(e, p):
            if p < KD:
                more = 1 + p // STAGES
                if p % STAGES >= KD - STAGES and not (isinstance(e, int) and e == 0):
                    more -= 1
                return e * BROUGHT + 16 * more
            return e * BROUGHT + 16 * (2 if isinstance(e, int) and e == NE - 1 else 3)

        @block.sync
        def _(sp):
            def gate_up_pieces(e):
                for p in range(KD):
                    if p >= STAGES:
                        before = taken(e, p - STAGES)
                    elif p + STAGES < KD:
                        before = taken(e - 1, p + STAGES)
                    elif isinstance(e, int) and e == 1:
                        before = taken(0, p)
                    else:
                        before = taken(e - 2, p + STAGES)
                    sp.wait_ge(low, before)
                    load_piece(sp, I, R, layer, landed, e, p)

            def down_pieces(e):
                for p in range(KD, PIECES):
                    sp.wait_ge(low, taken(e + 1, p - STAGES) if real(e + 1) else taken(e - 1, p))
                    load_piece(sp, I, R, layer, landed, e, p)

            def step(e, s):
                if real(e + 1):
                    gate_up_pieces(e + 1)
                down_pieces(e)
            over_experts(sp, step)

        @block.tensor
        def _(pe):
            def gather(e, s):
                pe.wait_ge(sg, e + 1)
                for half in range(2):
                    reach(pe, (gate, up)[half], e - 1)
                    if s == 0 and not (isinstance(e, int) and e <= 2):
                        pe.wait_ge(added, (e - 2) * NT + (half - 1))
                    for part in range(2):
                        for i, rows in enumerate(TILE_ROWS):
                            lo = P if part == 0 else 0
                            last = pe.matmul(ps[2 + half][:, :], SG[0:rows, s, i, lo:lo + P],
                                             XP[0:rows, part, i, half * 512:(half + 1) * 512],
                                             start=(part == 0 and i == 0), stop=(part == 1 and i == NT - 1))
                    last.then_inc(gathered, 1)

            def turn_gathered(e):
                for half in range(2):
                    pe.wait_ge(xe, e * 2 + half + 1)
                    reach(pe, xs, e * 2)
                    for k in range(4):
                        c = 4 * half + k
                        last = pe.transpose(ps[4 + half][:, k * P:(k + 1) * P], XE[:, c * P:(c + 1) * P], ident)
                    last.then_inc(xturned, 1)

            def gate_up(e, quarter):
                pe.wait_ge(xs, e * 2 + quarter + 1)
                if quarter == 0:
                    reach(pe, ge, e * 2)
                for k in range(4 * quarter, 4 * quarter + 4):
                    pe.wait_ge(low, taken(e, k))
                    for part in range(2):
                        for half in range(2):
                            last = pe.matmul(ps[half][:, :], XS[:, k, :], W[:, k, part, half * 512:(half + 1) * 512],
                                             start=(k == 0 and part == 0), stop=(k == KD - 1 and part == 1))
                    last.then_inc(used, 1)

            def scatter(e):
                turned = NE if isinstance(e, int) and e == NE else e + 1
                pe.wait_ge(yl, e * 2)
                for t, rows in enumerate(TILE_ROWS):
                    for half in range(2):
                        m = 2 * t + half
                        if m < 2:
                            pe.wait_ge((gate, up)[m], turned)
                        elif m < 4:
                            pe.wait_ge(xs, 2 * NE if isinstance(e, int) and e == NE else e * 2 + 4)
                        else:
                            pe.wait_ge(added, e * NT + (m - 3 - NY))
                        for x in range(2):
                            for part in range(2):
                                last = pe.matmul(ps[2 + m % 4][0:rows, :], ST[:, x, t * P:t * P + rows],
                                                 YP[:, x, part, half * 512:(half + 1) * 512],
                                                 start=(x + part == 0), stop=(x + part == 2))
                        last.then_inc(scattered, 1)

            def turn_gate_up(e):
                for half in range(2):
                    pe.wait_ge(ge, e * 2 + half + 1)
                    if real(e + 1):
                        pe.wait_ge(xe, e * 2 + (half + 3))
                    else:
                        pe.wait_ge(added, (e - 1) * NT)
                    for f in range(NF):
                        last = pe.transpose(ps[2 + half][:, f * P:(f + 1) * P],
                                            GE[:, half * 512 + f * P:half * 512 + (f + 1) * P], ident)
                    last.then_inc(gturned, 1)

            def turn_scatter(e, s):
                reach(pe, yl, e * 2)
                for i, rows in enumerate(TILE_ROWS):
                    last = pe.transpose(ps[6][:, i * P:i * P + rows], SG[0:rows, s, i, CAP:3 * CAP].bitcast(F32),
                                        ident[0:rows, 0:rows])
                last.then_inc(sturned, 1)
                for i, rows in enumerate(TILE_ROWS):
                    rhs = R["combp"][0:rows, i, bass.ds(e, 1), :].rearrange("p a b -> p (a b)")
                    last = pe.matmul(ps[7][:, 0:2], SG[0:rows, s, i, CAP:3 * CAP], rhs, start=(i == 0), stop=(i == NT - 1))
                last.then_inc(wsum, 1)

            def down(e):
                pe.wait_ge(hh, e + 1)
                pe.wait_ge(hl, e + 1)
                pe.wait_ge(st_ready, e + 1)
                pe.wait_ge(ws, e + 1)
                for f in range(NF):
                    pe.wait_ge(low, taken(e, KD + f))
                    for part in range(2):
                        for half in range(2):
                            last = pe.matmul(ps[6 + half][:, :], HT[:, f, :],
                                             W[:, KD + f, part, half * 512:(half + 1) * 512],
                                             start=(f == 0 and part == 0), stop=(f == NF - 1 and part == 1))
                    last.then_inc(used, 1)

            def step(e, s):
                if real(e):
                    gate_up(e, 0)
                if s == 1 and not (isinstance(e, int) and e == 1):
                    scatter(e - 1)
                if real(e - 1):
                    turn_scatter(e - 1, 1 - s)
                if real(e):
                    gate_up(e, 1)
                if real(e) and real(e + 1):
                    gather(e + 1, 1 - s)
                if real(e - 1):
                    down(e - 1)
                if real(e) and real(e + 1):
                    turn_gathered(e + 1)
                if real(e):
                    turn_gate_up(e)

            gather(0, 0)
            turn_gathered(0)
            over_experts(pe, step)
            step(NE, 0)
            scatter(NE)

        @block.scalar
        def _(act):
            A = nc.scalar

            def high_part(e, p):
                act.wait_ge(landed[p % STAGES], landings(e, p))
                if real(e - 1):
                    act.wait_ge(used, taken(e - 1, p))
                split_high(nc, R, p)

            def copy_gathered(e):
                for half in range(2):
                    act.wait_ge(gathered, e * 2 + half + 1)
                    reach(act, xturned, e * 2)
                    A.copy(XE[:, half * 512:(half + 1) * 512], ps[2 + half][:, :]).then_inc(xe, 1)

            def copy_turned(e):
                for half in range(2):
                    act.wait_ge(xturned, e * 2 + half + 1)
                    if half == 0 and real(e - 1):
                        act.wait_ge(used, taken(e - 1, KD - 1))
                    A.copy(XS[:, 4 * half:4 * half + 4, :].rearrange("p k t -> p (k t)"), ps[4 + half][:, :])\
                        .then_inc(xs, 1)

            def down_high(e, s):
                for half in range(2):
                    act.wait_ge(used, taken(e, PIECES - 1))
                    if s == 0:
                        reach(act, scattered, e * NT)
                    A.activation(YP[:, s, 0, half * 512:(half + 1) * 512], ps[6 + half][:, :], ACT.Copy,
                                 scale=WS[:, s:s + 1]).then_inc(yh, 1)

            def silu_of(e):
                act.wait_ge(gate, e + 1)
                reach(act, hidden, e)
                act.activation(SIL[:, :], GT[:, 0, :], ACT.Silu).then_inc(silu, 1)

            def hidden_high(e):
                act.wait_ge(hidden, e + 1)
                if real(e - 1):
                    act.wait_ge(used, taken(e - 1, PIECES - 1))
                A.copy(HT[:, :, 0:CAP], HR[:, :].rearrange("p (f t) -> p f t", f=NF)).then_inc(hh, 1)

            def copy_scatter(e, s):
                act.wait_ge(sturned, e + 1)
                reach(act, scattered, (e - s) * NT)
                A.copy(ST[:, s, :], ps[6][:, 0:TOK]).then_inc(st_ready, 1)

            def copy_gate_up(e):
                for half in range(2):
                    act.wait_ge(used, taken(e, KD - 1))
                    reach(act, gturned, e * 2)
                    A.copy(GE[:, half * 512:(half + 1) * 512], ps[half][:, :]).then_inc(ge, 1)

            def step(e, s):
                more = real(e) and real(e + 1)
                if real(e - 1):
                    high_part(e - 1, KD)
                    silu_of(e - 1)
                    high_part(e - 1, KD + 1)
                    hidden_high(e - 1)
                    high_part(e - 1, KD + 2)
                    high_part(e - 1, KD + 3)
                if more:
                    for p in range(4):
                        high_part(e + 1, p)
                if real(e - 1):
                    copy_scatter(e - 1, 1 - s)
                if more:
                    high_part(e + 1, 4)
                if real(e):
                    copy_gate_up(e)
                if more:
                    high_part(e + 1, 5)
                    copy_gathered(e + 1)
                    high_part(e + 1, 6)
                    high_part(e + 1, 7)
                if real(e - 1):
                    down_high(e - 1, 1 - s)
                if more:
                    copy_turned(e + 1)

            copy_gathered(0)
            copy_turned(0)
            over_experts(act, step)
            step(NE, 0)

        @block.vector
        def _(dve):
            V = nc.vector

            def low_part(e, p):
                dve.wait_ge(high, taken(e, p))
                split_low(nc, R, p)

            def build_gather(e, s):
                reach(dve, sturned, e - 1)
                reach(dve, wsum, e - 1)
                V.tensor_tensor(SG[:, s, :, CAP:3 * CAP].rearrange("p i (r k) -> p i r k", r=2),
                                slots.unsqueeze(1).unsqueeze(1).broadcast_to([P, NT, 2, CAP]),
                                R["rank"][:, :, bass.ds(e, 1)].unsqueeze(2).broadcast_to([P, NT, 2, CAP]),
                                ALU.is_equal).then_inc(sg, 1)

            def sum_turned(e):
                for half in range(2):
                    dve.wait_ge(gturned, e * 2 + half + 1)
                    if half == 0:
                        reach(dve, hidden, e)
                    V.tensor_reduce(GT[:, half, :].rearrange("p (f t) -> p f t", f=NF),
                                    ps[2 + half][:, :].rearrange("p (f a t) -> p f t a", f=NF, a=2), AX.X, ALU.add)\
                        .then_inc((gate, up)[half], 1)

            def hidden_of(e):
                dve.wait_ge(silu, e + 1)
                dve.wait_ge(up, e + 1)
                reach(dve, hl, e)
                reach(dve, hh, e)
                V.tensor_tensor(HR[:, :], SIL[:, :], GT[:, 1, :], ALU.mult).then_inc(hidden, 1)

            def hidden_low(e):
                dve.wait_ge(hh, e + 1)
                V.tensor_tensor(HT[:, :, CAP:2 * CAP], HR[:, :].rearrange("p (f t) -> p f t", f=NF),
                                HT[:, :, 0:CAP].bitcast(F32), ALU.subtract).then_inc(hl, 1)

            def slot_weights(e, s):
                dve.wait_ge(wsum, e + 1)
                if real(e - 2):
                    dve.wait_ge(yl, e * 2 - 2)
                V.tensor_reduce(WS[:, s:s + 1], ps[7][:, 0:2], AX.X, ALU.add).then_inc(ws, 1)

            def down_low(e, s):
                for half in range(2):
                    dve.wait_ge(yh, e * 2 + half + 1)
                    cols = slice(half * 512, (half + 1) * 512)
                    V.scalar_tensor_tensor(YP[:, s, 1, cols], ps[6 + half][:, :], WS[:, s:s + 1],
                                           YP[:, s, 0, cols].bitcast(F32), ALU.mult, ALU.subtract).then_inc(yl, 1)

            def add_sums(e):
                for t, rows in enumerate(TILE_ROWS):
                    for half in range(2):
                        m = 2 * t + half
                        dve.wait_ge(scattered, e * NT + (m + 1 - NY))
                        hv = H[0:rows, t, half * 512:(half + 1) * 512]
                        V.tensor_tensor(hv, ps[2 + m % 4][0:rows, :], hv, ALU.add).then_inc(added, 1)

            def step(e, s):
                more = real(e) and real(e + 1)
                if real(e - 1):
                    sum_turned(e - 1)
                    low_part(e - 1, KD)
                    hidden_of(e - 1)
                    low_part(e - 1, KD + 1)
                    hidden_low(e - 1)
                    low_part(e - 1, KD + 2)
                if s == 1 and not (isinstance(e, int) and e == 1):
                    add_sums(e - 1)
                if real(e - 1):
                    low_part(e - 1, KD + 3)
                if more:
                    low_part(e + 1, 0)
                if real(e - 1):
                    slot_weights(e - 1, 1 - s)
                    if more:
                        build_gather(e + 1, 1 - s)
                if more:
                    for p in range(1, KD):
                        low_part(e + 1, p)
                if real(e - 1):
                    down_low(e - 1, 1 - s)

            zeroed = new_sem(nc, M, f"moe{layer}_zeroed")
            V.memset(SG[:, :, :, 0:CAP].bitcast(F32), 0.0).then_inc(zeroed, 1)
            V.memset(SG[:, :, :, 3 * CAP:].bitcast(F32), 0.0).then_inc(zeroed, 1)
            dve.wait_ge(zeroed, 2)
            build_gather(0, 0)
            build_gather(1, 1)
            over_experts(dve, step)
            step(NE, 0)
            add_sums(NE)
            dve.wait_ge(added, NE // 2 * NY)


def moe_over(nc, I, M, R, layer):
    H, ps, comb = M["H"], M["ps"], R["comb_over"]
    with ExitStack() as ctx:
        def sb(name, shape, dtype=F32):
            return ctx.enter_context(nc.sbuf_tensor(f"over{layer}_{name}", shape, dtype))

        XT, GU, DN = sb("xT", [P, KD, TOK]), sb("gate_up", [P, KD, 2 * FE]), sb("down", [P, NF, D])
        SIL, HDN = sb("silu", [P, NF, TOK]), sb("hidden", [P, NF, TOK])
        sem = lambda n: new_sem(nc, M, f"over{layer}_{n}")
        x_in, w_in, turn = sem("x_landed"), sem("weights_landed"), sem("expert_turn")
        pair, silu, hid, y_ready, y_added = (sem("gate_up_ready"), sem("silu_ready"), sem("hidden_ready"),
                                             sem("y_ready"), sem("y_added"))
        block = ctx.enter_context(nc.Block())

        def over_list(eng, body, before=None):
            n = eng.value_load(R["over"][0:1, MAXOVER:MAXOVER + 1], min_val=0, max_val=MAXOVER)
            with eng.If(n > 0):
                if before:
                    before()
                with eng.Fori(0, MAXOVER) as k:
                    with eng.If(n > k):
                        e = eng.value_load(R["over"][0:1, bass.ds(k, 1)], min_val=0, max_val=NE - 1)
                        body(k, e)

        @block.sync
        def _(sp):
            def load_x():
                sp.dma_start(XT[:, :, :].rearrange("p k t -> p (k t)"), M["spill"]).then_inc(x_in, 16)

            def load(k, e):
                sp.wait_ge(turn, k + 1)
                sp.dma_start(GU[:, :, :], I["w_gate_up"][layer][bass.ds(e, 1)].rearrange("a (k p) n -> p (a k) n", p=P))\
                    .then_inc(w_in, 16)
                sp.dma_start(DN[:, :, :], I["w_down"][layer][bass.ds(e, 1)].rearrange("a (k p) n -> p (a k) n", p=P))\
                    .then_inc(w_in, 16)
            over_list(sp, load, load_x)

        @block.tensor
        def _(pe):
            def expert(k, e):
                pe.wait_ge(turn, k + 1)
                pe.wait_ge(x_in, 16)
                pe.wait_ge(w_in, k * 32 + 32)
                for f in range(NF):
                    for u in range(2):
                        for c in range(KD):
                            last = pe.matmul(ps[2 * f + u][:, 0:TOK], GU[:, c, u * FE + f * P:u * FE + (f + 1) * P],
                                             XT[:, c, :], start=(c == 0), stop=(c == KD - 1))
                    last.then_inc(pair, 1)
                pe.wait_ge(hid, k * NF + NF)
                for t, rows in enumerate(TILE_ROWS):
                    for half in range(2):
                        for f in range(NF):
                            last = pe.matmul(ps[2 * t + half][0:rows, :], HDN[:, f, t * P:t * P + rows],
                                             DN[:, f, half * 512:(half + 1) * 512], start=(f == 0), stop=(f == NF - 1))
                        last.then_inc(y_ready, 1)
            over_list(pe, expert)

        @block.scalar
        def _(act):
            def expert(k, e):
                for f in range(NF):
                    act.wait_ge(pair, k * NF + (f + 1))
                    act.activation(SIL[:, f, :], ps[2 * f][:, 0:TOK], ACT.Silu).then_inc(silu, 1)
            over_list(act, expert)

        @block.vector
        def _(dve):
            def expert(k, e):
                for f in range(NF):
                    dve.wait_ge(silu, k * NF + (f + 1))
                    nc.vector.tensor_tensor(HDN[:, f, :], ps[2 * f + 1][:, 0:TOK], SIL[:, f, :], ALU.mult).then_inc(hid, 1)
                for t, rows in enumerate(TILE_ROWS):
                    for half in range(2):
                        dve.wait_ge(y_ready, k * (2 * NT) + (2 * t + half + 1))
                        hv = H[0:rows, t, half * 512:(half + 1) * 512]
                        c = comb[0:rows, t, bass.ds(e, 1)]
                        nc.vector.scalar_tensor_tensor(hv, ps[2 * t + half][0:rows, :], c, hv, ALU.mult, ALU.add)\
                            .then_inc(y_added, 1)
                dve.wait_ge(y_added, k * (2 * NT) + 2 * NT)
                nc.vector.memset(SIL[0:1, 0, 0:1], 0.0).then_inc(turn, 1)

            def first_turn():
                nc.vector.memset(SIL[0:1, 0, 0:1], 0.0).then_inc(turn, 1)
            over_list(dve, expert, first_turn)


def store_result(nc, O, M):
    with ExitStack() as ctx:
        stored = new_sem(nc, M, "y_stored")
        block = ctx.enter_context(nc.Block())

        @block.sync
        def _(sp):
            for i, rows in enumerate(TILE_ROWS):
                dst = O["y_prompt"][0, i * P:(i + 1) * P, :] if i < 2 else O["y_sample"].rearrange("b t d -> (b t) d")
                sp.dma_start(dst, M["H"][0:rows, i, :]).then_inc(stored, 16)
            sp.wait_ge(stored, 16 * NT)


def view(M, at, *dims):
    n = 1
    for d in dims:
        n *= d
    names = "abcd"[:len(dims)]
    v = M["A"][:, at:at + n]
    if len(dims) == 1:
        return v
    return v.rearrange(f"p ({' '.join(names)}) -> p {' '.join(names)}", **dict(zip(names, dims)))


def stage_attention(nc, I, O, M):
    M["weights_in"] = [new_sem(nc, M, f"projection_weights_landed{c}") for c in range(5)]
    M["rows_stored"] = new_sem(nc, M, "projection_rows_stored")
    M["cmp_weights_in"], M["cmp_rows_in"] = new_sem(nc, M, "compression_weights_landed"), new_sem(nc, M, "chunk_rows_landed")
    M["raw_in"] = [new_sem(nc, M, f"raw_pages_landed{s}") for s in range(2)]
    M["sequence_in"] = [new_sem(nc, M, f"sequence_landed{s}") for s in range(3)]
    norm_transpose(nc, I, M, "mix1", [(2, M["XT"]), (3, view(M, Map.XT2, KD, TOK))])
    project(nc, I, O, M)
    turn_heads(nc, I, O, M)
    compress_prompt(nc, I, O, M)
    compress_samples(nc, I, M)
    attend_samples(nc, I, M)
    attend_prompt(nc, I, M)
    output_projection(nc, M)


def load_projections(sp, I, M):
    WKV, WQG = view(M, Map.WKV, KD, 6 * NKV * HD), view(M, Map.WQG, KD, NH * HD + 3 * NH)
    for W, name, width in ((WKV, I["w_kv"], 6 * NKV * HD), (WQG, I["w_qg"][0], NH * HD + 3 * NH)):
        for at in range(0, width - width % 512, 512):
            end = at + 512 if width - at - 512 >= 512 else width
            sp.dma_start(W[:, :, at:end], name.rearrange("(k p) n -> p k n", p=P)[:, :, at:end])\
                .then_inc(M["weights_in"][at // 512 + (3 if W is WQG else 0)], 16)


def project(nc, I, O, M):
    XT, XT2, ps, stat = M["XT"], view(M, Map.XT2, KD, TOK), M["ps"], M["stat"]
    WKV, WQG = view(M, Map.WKV, KD, 6 * NKV * HD), view(M, Map.WQG, KD, NH * HD + 3 * NH)
    HEADS = view(M, Map.HEADS, NT, 24, HD)
    KV, WN = view(M, Map.KVROWS, NT, 4 * NKV * HD), view(M, Map.WINROWS, NT, 2 * NKV * HD)
    QR = view(M, Map.QROPE, NT, NH, HD)
    GAIN, SQ = view(M, Map.GAIN24, 24, HD), view(M, Map.SQ, 24, HD)
    t1, t2 = view(M, Map.ROT, 24, HD // 2), view(M, Map.ROT + 24 * HD // 2, 24, HD // 2)
    gates = M["gates"]
    cos = const(M, "cos").rearrange("p (i d) -> p i d", i=NT)
    sin = const(M, "sin").rearrange("p (i d) -> p i d", i=NT)
    KW = NKV * HD
    chunks = [(XT2, WKV, 0, 512), (XT2, WKV, 512, 512), (XT2, WKV, 1024, 512),
              (XT, WQG, 0, 512), (XT, WQG, 512, 512), (XT, WQG, 1024, 3 * NH)]
    NC = len(chunks)
    orders = [range(NC)] * (NT - 1) + [(1, 2, 3, 4, 0, 5)]
    heads_from = [NC] * (NT - 1) + [4]
    with ExitStack() as ctx:
        sem = lambda n: new_sem(nc, M, "proj_" + n)
        weights_in, gains_in = M["weights_in"], sem("gains_landed")
        product, copied, parts = sem("product_ready"), sem("product_copied"), sem("part_copied")
        squared, scaled, rooted = sem("squares_ready"), sem("mean_ready"), sem("root_ready")
        chain, roped, kv_stored, stored = sem("chain"), sem("rows_roped"), sem("prompt_rows_stored"), M["rows_stored"]
        block = ctx.enter_context(nc.Block())

        @block.sync
        def _(sp):
            for lo, hi, src in ((0, 4, I["k_norm"][1:2, :]), (4, 8, I["k_norm"][2:3, :]), (8, 24, I["q_norm"][0:1, :])):
                sp.dma_start(GAIN[:, lo:hi, :], src.unsqueeze(1).broadcast_to([1, hi - lo, HD])
                             .broadcast_to([P, hi - lo, HD])).then_inc(gains_in, 16)
            sp.dma_start(O["new_win_sample"][:, 0:WIN - STEPS], I["state_win"][:, STEPS:WIN]).then_inc(stored, 16)
            for i in range(NT):
                sp.wait_ge(roped, i + 1)
                if i < 2:
                    sp.dma_start(O["new_kv_prompt"][0, i * P:(i + 1) * P].rearrange("t s g d -> t (s g d)"),
                                 KV[:, i, :]).then_inc(kv_stored, 16)
                    sp.dma_start(O["new_win_prompt"][0, i * P:(i + 1) * P].rearrange("t s g d -> t (s g d)"),
                                 WN[:, i, :]).then_inc(stored, 16)
                else:
                    sp.wait_ge(copied, NT * NC)
                    sp.dma_start(O["new_kv_sample"].rearrange("b t s g d -> (b t) (s g d)"),
                                 KV[0:NEWTOK, i, :]).then_inc(stored, 16)
                    for b in range(NSEQ):
                        sp.dma_start(O["new_win_sample"][b, WIN - STEPS:WIN].rearrange("t s g d -> t (s g d)"),
                                     WN[b * STEPS:(b + 1) * STEPS, i, :]).then_inc(stored, 16)
            sp.wait_ge(kv_stored, 32)

        @block.tensor
        def _(pe):
            n = 0
            for i, rows in enumerate(TILE_ROWS):
                for c in orders[i]:
                    T, W, at, w = chunks[c]
                    if i == 0 and c < NC - 1:
                        pe.wait_ge(weights_in[c], 16)
                    if n >= 8:
                        pe.wait_ge(copied, n - 7)
                    for k in range(KD):
                        last = pe.matmul(ps[n % 8][0:rows, 0:w], T[:, k, i * P:i * P + rows], W[:, k, at:at + w],
                                         start=(k == 0), stop=(k == KD - 1))
                    last.then_inc(product, 1)
                    n += 1

        @block.scalar
        def _(act):
            def square_heads(i, rows, flat):
                act.wait_ge(copied, i * NC + heads_from[i])
                act.wait_ge(parts, 2 * (i + 1))
                if i:
                    act.wait_ge(scaled, i)
                act.activation(SQ[0:rows].rearrange("p h d -> p (h d)"), flat, ACT.Square).then_inc(squared, 1)
                act.wait_ge(scaled, i + 1)
                act.activation(stat[0:rows, 16:40], stat[0:rows, 40:64], ACT.Sqrt).then_inc(rooted, 1)

            for i, rows in enumerate(TILE_ROWS):
                flat = HEADS[0:rows, i].rearrange("p h d -> p (h d)")
                dests = [[(KV[0:rows, i, 0:512], 0)],
                         [(flat[:, 0:KW], 0), (KV[0:rows, i, 3 * KW:4 * KW], KW)],
                         [(flat[:, KW:2 * KW], 0), (WN[0:rows, i, KW:2 * KW], KW)],
                         [(HEADS[0:rows, i, 8:16].rearrange("p (h g) d -> p g h d", g=2), 0)],
                         [(HEADS[0:rows, i, 16:24].rearrange("p (h g) d -> p g h d", g=2), 0)],
                         [(gates[0:rows, i, :], 0)]]
                for m, c in enumerate(orders[i]):
                    if m == heads_from[i]:
                        square_heads(i, rows, flat)
                    n = i * NC + m
                    act.wait_ge(product, n + 1)
                    for last, (dst, at) in zip((len(dests[c]) == 1, True), dests[c]):
                        if len(dst.shape) == 4:
                            src = ps[n % 8][0:rows, :].rearrange("p (g h d) -> p g h d", g=2, h=HPG)
                        else:
                            src = ps[n % 8][0:rows, at:at + dst.shape[1]]
                        nc.scalar.copy(dst, src).then_inc(copied if last else parts, 1)
                if heads_from[i] == NC:
                    square_heads(i, rows, flat)
            act.wait_ge(copied, NT * NC)
            act.activation(gates[:, :, :], gates[:, :, :], ACT.Sigmoid).then_inc(parts, 1)

        @block.vector
        def _(dve):
            V = nc.vector
            st = Steps(dve, chain)
            dve.wait_ge(gains_in, 48)
            for i, rows in enumerate(TILE_ROWS):
                r = slice(0, rows)
                dve.wait_ge(squared, i + 1)
                st.add(V.tensor_reduce(stat[r, 16:40], SQ[r], AX.X, ALU.add))
                V.tensor_scalar(stat[r, 40:64], stat[r, 16:40], 1.0 / HD, EPS, ALU.mult, ALU.add).then_inc(scaled, 1)
                dve.wait_ge(rooted, i + 1)
                st.add(V.reciprocal(stat[r, 40:64], stat[r, 16:40]))
                x = HEADS[r, i]
                st.add(V.tensor_tensor(x, x, stat[r, 40:64].unsqueeze(2).broadcast_to([rows, 24, HD]), ALU.mult))
                st.add(V.tensor_tensor(x, x, GAIN[r], ALU.mult))
                x1, x2 = x[:, :, 0:HD // 2], x[:, :, HD // 2:HD]
                c = cos[r, i].unsqueeze(1).broadcast_to([rows, 24, HD // 2])
                s = sin[r, i].unsqueeze(1).broadcast_to([rows, 24, HD // 2])
                dst = [(0, 4, KV[r, i, 2 * KW:3 * KW].rearrange("p (g d) -> p g d", g=NKV)),
                       (4, 8, WN[r, i, 0:KW].rearrange("p (g d) -> p g d", g=NKV)), (8, 24, QR[r, i])]
                for lo, first, second, op in ((0, x1, x2, ALU.subtract), (HD // 2, x2, x1, ALU.add)):
                    st.add(V.tensor_tensor(t1[r], first, c, ALU.mult))
                    st.add(V.tensor_tensor(t2[r], second, s, ALU.mult))
                    for m, (a, b, d) in enumerate(dst):
                        ins = V.tensor_tensor(d[:, :, lo:lo + HD // 2], t1[r, a:b], t2[r, a:b], op)
                        if lo and m == 2:
                            ins.then_inc(roped, 1)
                            dve.wait_ge(roped, i + 1)
                        else:
                            st.add(ins)


def turn_heads(nc, I, O, M):
    ps, gates = M["ps"], M["gates"]
    HEADS, QR = view(M, Map.HEADS, NT, 24, HD), view(M, Map.QROPE, NT, NH, HD)
    KV, WN = view(M, Map.KVROWS, NT, 4, NKV * HD), view(M, Map.WINROWS, NT, 2, NKV * HD)
    QT = [view(M, Map.QNT, 2, HPG, SEQ), view(M, Map.QRT, 2, HPG, SEQ)]
    QS = [view(M, Map.QSN, 2, HPG, NEWTOK), view(M, Map.QSR, 2, HPG, NEWTOK)]
    KTP, KTN = view(M, Map.KTP, 4, SEQ), view(M, Map.KTN, 4, NEWTOK)
    VP, VNEW = view(M, Map.VP, 2, 2, NKV, 3 * HD), view(M, Map.VNEW, NKV * HD)
    GS, GL = view(M, Map.GS, 3, NSEQ), view(M, Map.GATEL, 3, NH, STEPS)
    ident, stepsel, seqsel = const(M, "ident"), const(M, "stepsel", NEWTOK), const(M, "seqsel", NEWTOK)

    def query_pair(which, i, j, h):
        rows = TILE_ROWS[i]
        src, at = ((HEADS, 8), (QR, 0))[which]
        a = at + 2 * HPG * j + 2 * h
        return src[0:rows, i, a:a + 2, :].rearrange("p g d -> p (g d)")

    def key_pair(br, i, j):
        rows = TILE_ROWS[i]
        src = KV[0:rows, i, 2] if br == 0 else WN[0:rows, i, 0]
        return src[:, j * P:(j + 1) * P]

    batches = []
    for i in range(2):
        for which in range(2):
            for j in range(2):
                batches.append(([query_pair(which, i, j, h) for h in range(HPG)], P,
                                QT[which][:, j, :, i * P:(i + 1) * P]))
        batches.append(([key_pair(br, i, j) for br in range(2) for j in range(2)], P, KTP[:, :, i * P:(i + 1) * P]))
    for which in range(2):
        for j in range(2):
            batches.append(([query_pair(which, 2, j, h) for h in range(HPG)], NEWTOK, QS[which][:, j]))
    batches.append(([key_pair(br, 2, j) for br in range(2) for j in range(2)], NEWTOK, KTN))
    NB = len(batches)
    with ExitStack() as ctx:
        sem = lambda n: new_sem(nc, M, "turn_" + n)
        turned, by_dve, by_act = sem("batch_turned"), sem("copied_by_dve"), sem("copied_by_act")
        zeroed, gl, gsum = sem("zeroed"), sem("gate_rows_spread"), sem("gates_summed")
        block = ctx.enter_context(nc.Block())

        @block.sync
        def _(sp):
            W1 = view(M, Map.W1, 2, 2, 8, HID)
            CR = view(M, Map.CHUNKS, 2, 8 * NKV, 2, HD)
            src = O["new_kv_prompt"][0].rearrange("(c i r) k g d -> k r c i g d", r=2, i=CHUNK // 2)
            for kind in range(2):
                for r in range(2):
                    sp.dma_start(CR[0:NCP + 1, kind, :, r, :].rearrange("c (i g) d -> c i g d", g=NKV), src[kind, r])\
                        .then_inc(M["cmp_rows_in"], 16)
            for kind in range(2):
                sp.dma_start(W1[:, kind], I["cmp_w1"][kind].rearrange("(h i p) n -> p h i n", p=P, h=2))\
                    .then_inc(M["cmp_weights_in"], 16)
            sp.wait_ge(M["rows_stored"], 16 * (4 + NSEQ))

        @block.tensor
        def _(pe):
            for n, (srcs, w, dst) in enumerate(batches):
                if n >= 6:
                    pe.wait_ge(by_act if n % 2 else by_dve, (n - 6) // 2 + 1)
                for m, src in enumerate(srcs):
                    last = pe.transpose(ps[n % 6][:, m * w:(m + 1) * w], src, ident[0:w, 0:w])
                last.then_inc(turned, 1)
            pe.wait_ge(gl, 3)
            for br in range(3):
                last = pe.matmul(ps[6][:, br * NSEQ:(br + 1) * NSEQ], GL[0:NEWTOK, br].rearrange("p h t -> p (h t)"),
                                 seqsel, start=True, stop=True)
            last.then_inc(gsum, 1)

        def copy(n, on_act):
            srcs, w, dst = batches[n]
            src = ps[n % 6][:, 0:4 * w].rearrange("p (m t) -> p m t", m=4)
            return nc.scalar.copy(dst, src) if on_act else nc.vector.tensor_copy(dst, src)

        @block.scalar
        def _(act):
            for n in range(1, NB, 2):
                act.wait_ge(turned, n + 1)
                copy(n, True).then_inc(by_act, 1)

        @block.vector
        def _(dve):
            for br in range(3):
                nc.vector.tensor_tensor(GL[0:NEWTOK, br], gates[0:NEWTOK, 2, br * NH:(br + 1) * NH].unsqueeze(2)
                                        .broadcast_to([NEWTOK, NH, STEPS]),
                                        stepsel.unsqueeze(1).broadcast_to([NEWTOK, NH, STEPS]), ALU.mult)\
                    .then_inc(gl, 1)
            for n in range(0, NB, 2):
                dve.wait_ge(turned, n + 1)
                copy(n, False).then_inc(by_dve, 1)
            dve.wait_ge(gsum, 1)
            nc.vector.tensor_copy(GS, ps[6][:, 0:3 * NSEQ].rearrange("p (a b) -> p a b", a=3))
            nc.vector.tensor_copy(VNEW[0:NEWTOK], KV[0:NEWTOK, 2, 3])
            nc.vector.tensor_copy(VNEW[NEWTOK:P], WN[0:NEWTOK, 2, 1])

        @block.gpsimd
        def _(pool):
            nc.gpsimd.memset(view(M, Map.QB, 3 * 2 * P), 0.0)
            nc.gpsimd.memset(view(M, Map.W2, 2 * 3 * HD), 0.0)
            nc.gpsimd.memset(view(M, Map.ONES, 260), 1.0)
            nc.gpsimd.memset(view(M, Map.CVP, NKV * 3 * HD), 0.0)
            nc.gpsimd.memset(view(M, Map.VP, 2 * 2 * NKV * 3 * HD), 0.0).then_inc(zeroed, 1)
            pool.wait_ge(zeroed, 1)
            for i in range(2):
                nc.gpsimd.tensor_copy(VP[:, i, 0, :, HD:2 * HD], KV[:, i, 3].rearrange("p (g d) -> p g d", g=NKV))
                nc.gpsimd.tensor_copy(VP[:, i, 1, :, HD:2 * HD], WN[:, i, 1].rearrange("p (g d) -> p g d", g=NKV))


def page_id(sp, I, M, b, pg, name):
    return sp.value_load(M["pages"][0:1, bass.ds(b * NPAGE + pg, 1)], min_val=0, max_val=I[name].shape[0] - 1)


def load_raw_pages(sp, I, M, b, s):
    RAW = view(M, Map.RAW[s], NPAGE, 2 * 256)
    for pg in range(NPAGE):
        which = page_id(sp, I, M, b, pg, "pages_raw")
        sp.dma_start(RAW[:, pg], I["pages_raw"][bass.ds(which, 1)].rearrange("a p n -> p (a n)")).then_inc(M["raw_in"][s], 16)


def load_sequence(sp, I, M, b, s):
    W, S = view(M, Map.WINB[s], 4 * WIN), view(M, Map.SEL[s], NPAGE, 512)
    sp.dma_start(W[:, 0:2 * WIN], I["win_keysT"][bass.ds(b, 1)].rearrange("a p n -> p (a n)")).then_inc(M["sequence_in"][s], 16)
    sp.dma_start(W[:, 2 * WIN:].rearrange("p (k n) -> p k n", k=WIN // P),
                 I["state_win"][bass.ds(b, 1), :, 1].rearrange("a (k p) g d -> p (a k) (g d)", p=P))\
        .then_inc(M["sequence_in"][s], 16)
    for pg in range(NPAGE):
        which = page_id(sp, I, M, b, pg, "pages_sel")
        sp.dma_start(S[:, pg], I["pages_sel"][bass.ds(which, 1)].rearrange("a p n -> p (a n)")).then_inc(M["sequence_in"][s], 16)


def compress_prompt(nc, I, O, M):
    ps = M["ps"]
    W1, W2 = view(M, Map.W1, 2, 2, 8, HID), view(M, Map.W2, 2, 3 * HD)
    PEC, BIAS, ONES = view(M, Map.PE, 2, 2, 8), view(M, Map.BIAS, 2, HID), view(M, Map.ONES, 260)
    CR = view(M, Map.CHUNKS, 2, 8 * NKV, 2, HD)
    RP = view(M, Map.RP, 2, 8, NKV, CHUNK)
    HIDP = view(M, Map.HIDB, 2, NKV, NCP)
    CKP, CVP = view(M, Map.CKP, 2, CHUNK), view(M, Map.CVP, NKV, 3 * HD)
    SQ, RS = view(M, Map.CKB, 2, NCP), view(M, Map.CKB + 64, 2, NCP)
    B1 = view(M, Map.CKB + 128, 2, HID)
    KG = M["kgain"]
    ident, blockones = const(M, "ident"), const(M, "blockones")
    NCH = NCP + 1
    with ExitStack() as ctx:
        sem = lambda n: new_sem(nc, M, "cmpp_" + n)
        w_in, rows_in, small_in = M["cmp_weights_in"], M["cmp_rows_in"], sem("small_landed")
        turned, copied, biased = sem("rows_turned"), sem("rows_copied"), sem("bias_ready")
        product, gelu, ck, sq, ss = sem("hidden_ready"), sem("gelu_ready"), sem("ck_ready"), sem("ck_squared"), sem("ck_summed")
        cv, mean, root, chain, bias_mm = sem("cv_ready"), sem("mean_ready"), sem("root_ready"), sem("chain"), sem("bias_summed")
        block = ctx.enter_context(nc.Block())

        @block.sync
        def _(sp):
            sp.dma_start(W2[:, :, HD:2 * HD], I["cmp_w2"].rearrange("k p n -> p k n")).then_inc(small_in, 16)
            sp.dma_start(PEC, I["cmp_pe"]).then_inc(small_in, 16)
            sp.dma_start(B1[0:1], I["cmp_b1"].unsqueeze(0)).then_inc(small_in, 16)
            sp.dma_start(KG[:, :], I["k_gainT"]).then_inc(small_in, 16)
            load_raw_pages(sp, I, M, 0, 0)

        @block.tensor
        def _(pe):
            pe.wait_ge(rows_in, 64)
            for kind in range(2):
                for i in range(8):
                    for g in range(NKV):
                        last = pe.transpose(ps[kind][:, (i * NKV + g) * NCH:(i * NKV + g + 1) * NCH],
                                            CR[0:NCH, kind, i * NKV + g].rearrange("c r d -> c (r d)"),
                                            ident[0:NCH, 0:NCH])
                last.then_inc(turned, 1)
            pe.wait_ge(w_in, 32)
            pe.wait_ge(small_in, 64)
            for kind in range(2):
                for half in range(2):
                    for i in range(8):
                        last = pe.matmul(ps[2][0:1, kind * HID:(kind + 1) * HID], PEC[:, kind, half, i:i + 1],
                                         W1[:, kind, half, i, :], start=(half + i == 0), stop=(half + i == 8))
            last.then_inc(bias_mm, 1)
            pe.wait_ge(biased, 1)
            pe.wait_ge(copied, 2)
            for kind in range(2):
                bank = ps[3 + kind][:, 0:NKV * NCP].rearrange("p (g c) -> p g c", g=NKV)
                pe.matmul(ps[3 + kind][:, 0:NKV * NCP], BIAS[0:1, kind, :], ONES[0:1, 0:NKV * NCP], start=True, stop=False)
                for half in range(2):
                    for i in range(8):
                        last = pe.matmul(bank, W1[:, kind, half, i, :], RP[:, kind, i, :, half:half + NCP],
                                         start=False, stop=(half + i == 8))
                last.then_inc(product, 1)
            pe.wait_ge(gelu, 2)
            for j in range(2):
                out = ps[5][:, j * NCP:(j + 1) * NCP]
                pe.matmul(out, W2[:, 0, HD:3 * HD], HIDP[:, 0, 2 * j, :], start=True, stop=False)
                last = pe.matmul(out, W2[:, 0, 0:2 * HD], HIDP[:, 0, 2 * j + 1, :], start=False, stop=True)
            last.then_inc(ck, 1)
            for g in range(NKV):
                last = pe.matmul(ps[6][0:NCP, g * HD:(g + 1) * HD], HIDP[:, 1, g, :], W2[:, 1, HD:2 * HD],
                                 start=True, stop=True)
            last.then_inc(cv, 1)
            pe.wait_ge(sq, 1)
            pe.matmul(ps[7][:, 0:2 * NCP], blockones, SQ.rearrange("p j c -> p (j c)"), start=True, stop=True).then_inc(ss, 1)

        @block.scalar
        def _(act):
            for kind in range(2):
                act.wait_ge(product, kind + 1)
                act.activation(HIDP[:, kind].rearrange("p g c -> p (g c)"), ps[3 + kind][:, 0:NKV * NCP],
                               ACT.Gelu_apprx_tanh).then_inc(gelu, 1)
            act.wait_ge(ck, 1)
            act.activation(SQ.rearrange("p j c -> p (j c)"), ps[5][:, 0:2 * NCP], ACT.Square).then_inc(sq, 1)
            act.wait_ge(mean, 1)
            act.activation(RS, RS, ACT.Sqrt).then_inc(root, 1)

        @block.vector
        def _(dve):
            V = nc.vector
            st = Steps(dve, chain)
            for kind in range(2):
                dve.wait_ge(turned, kind + 1)
                V.tensor_copy(RP[:, kind].rearrange("p i g c -> p (i g c)"), ps[kind][:, :]).then_inc(copied, 1)
            dve.wait_ge(bias_mm, 1)
            dve.wait_ge(small_in, 64)
            V.tensor_tensor(BIAS[0:1].rearrange("p k n -> p (k n)"), ps[2][0:1, 0:2 * HID],
                            B1[0:1].rearrange("p k n -> p (k n)"), ALU.add).then_inc(biased, 1)
            dve.wait_ge(cv, 1)
            st.add(V.tensor_copy(CVP[0:NCP, :, HD:2 * HD], ps[6][0:NCP, 0:NKV * HD].rearrange("p (g d) -> p g d", g=NKV)))
            dve.wait_ge(ss, 1)
            V.tensor_scalar(RS, ps[7][:, 0:2 * NCP].rearrange("p (j c) -> p j c", j=2), 1.0 / HD, EPS, ALU.mult, ALU.add)\
                .then_inc(mean, 1)
            dve.wait_ge(root, 1)
            st.add(V.reciprocal(RS, RS))
            st.add(V.scalar_tensor_tensor(CKP[:, :, 0:NCP], ps[5][:, 0:2 * NCP].rearrange("p (j c) -> p j c", j=2),
                                          KG[:, 0:1], RS, ALU.mult, ALU.mult))


def queries_of(nc, QS, QB, b, s, done):
    for par in range(2):
        half = slice(par * HD, (par + 1) * HD)
        for j in range(2):
            at = (2 * j + par) * HPG * STEPS
            dst = QB[half, s, j, at:at + HPG * STEPS].rearrange("p (h t) -> p h t", h=HPG)
            nc.gpsimd.tensor_copy(dst, QS[half, j, :, bass.ds(b * STEPS, STEPS)]).then_inc(done, 1)


def compress_samples(nc, I, M):
    ps = M["ps"]
    W1, W2 = view(M, Map.W1, 2, 2, 8, HID), view(M, Map.W2, 2, 3 * HD)
    BIAS, ONES, KG = view(M, Map.BIAS, 2, HID), view(M, Map.ONES, 260), M["kgain"]
    RAW = [view(M, at, NPAGE, 2, 256) for at in Map.RAW]
    HIDB = view(M, Map.HIDB, 2, 2, 256)
    NB = NCS + 1
    SQ = view(M, Map.CKB, 2, NB)
    RS = view(M, Map.CKB + 128, 2, NB)
    CKT = view(M, Map.CKB + 256, 2, NB)
    PR = view(M, Map.CKB + 384, NB)
    SCORE, KEY = view(M, Map.CKB + 448, NSB - 3), view(M, Map.CKB + 464, NSB - 3)
    CV, PC, BM = view(M, Map.CV, NSEQ, NKV * HD), view(M, Map.PC, NSEQ, NB), view(M, Map.BM, NSEQ, 16)
    GS = view(M, Map.GS, 3, NSEQ)
    QS, QB = view(M, Map.QSN, 2, HPG, NEWTOK), view(M, Map.QB, 2, 2, P)
    sm = view(M, Map.SMALL, 16)
    blockones, headsum, iota = const(M, "blockones"), const(M, "headsum"), const(M, "iota")
    NBLK = NPAGE * (PAGE // CHUNK) * NKV
    with ExitStack() as ctx:
        sem = lambda n: new_sem(nc, M, "cmps_" + n)
        raw_in = M["raw_in"]
        hidden, gelu, ck, cv = sem("hidden_ready"), sem("gelu_ready"), sem("ck_ready"), sem("cv_ready")
        squared, ss, mean, root, ckt = sem("ck_squared"), sem("ck_summed"), sem("mean_ready"), sem("root_ready"), sem("ckT_ready")
        cv_out, qb, score, negmax = sem("cv_copied"), sem("queries_ready"), sem("scores_ready"), sem("negmax_ready")
        expd, prob, pooled, chain = sem("exp_ready"), sem("probs_ready"), sem("group_sums_ready"), sem("chain")
        chosen = sem("blocks_chosen")
        block = ctx.enter_context(nc.Block())
        DCH = 10

        def over_sequences(eng, body):
            for s in range(2):
                body(s, s, True, False)
            with eng.Fori(1, NSEQ // 2 - 1) as i:
                for s in range(2):
                    body(i * 2 + s, s, False, False)
            for s in range(2):
                body(NSEQ - 2 + s, s, False, s == 1)

        @block.sync
        def _(sp):
            def load(b, s, first, last):
                if first and s == 0:
                    return
                if not first:
                    sp.wait_ge(hidden, b * 2 - 2)
                load_raw_pages(sp, I, M, b, s)
            over_sequences(sp, load)
            sp.wait_ge(hidden, 2 * (NSEQ - 1))
            load_sequence(sp, I, M, 0, 0)

        @block.gpsimd
        def _(pool):
            def queries(b, s, first, last):
                if not first:
                    pool.wait_ge(score, b - 1)
                queries_of(nc, QS, QB, b, s, qb)
            over_sequences(pool, queries)

        @block.tensor
        def _(pe):
            def hide(b, s, kind, half):
                bank = ps[2 * s + kind]
                out = bank[:, 1 - half:1 - half + NBLK].rearrange("p (g n c) -> p g n c", g=NKV, n=NPAGE)
                for i in range(8):
                    rhs = RAW[s][:, :, kind, i * 32:(i + 1) * 32].rearrange("p n (g c) -> p g n c", g=NKV)
                    pe.matmul(out, W1[:, kind, half, i, :], rhs, start=(half + i == 0), stop=False,
                              skip_group_check=True)
                if half == 1:
                    pe.matmul(bank[:, 1:1 + NBLK], BIAS[0:1, kind, :], ONES[0:1, 0:NBLK], start=False, stop=True,
                              skip_group_check=True).then_inc(hidden, 1)

            def hide_after(b, s, kind, half, first):
                if kind == 0 and half == 0:
                    pe.wait_ge(raw_in[s], landed_pages(b, s))
                if half == 0 and not first:
                    pe.wait_ge(gelu, b * 2 + (kind - 3))
                hide(b, s, kind, half)

            def landed_pages(b, s):
                return (b - s) * (16 * NPAGE // 2) + 16 * NPAGE

            def seq(b, s, first, last):
                nxt = lambda kind, half: None if last else hide_after(b + 1, 1 - s, kind, half, first and s == 0)
                nxt(0, 0)
                pe.wait_ge(gelu, b * 2 + 2)
                if not (first and s == 0):
                    pe.wait_ge(ckt, b)
                    pe.wait_ge(cv_out, b)
                for j in range(2):
                    out = ps[4][:, j * NB:(j + 1) * NB]
                    pe.matmul(out, W2[:, 0, HD:3 * HD], HIDB[:, s, 0, 2 * j * NB:(2 * j + 1) * NB], start=True, stop=False)
                    last_mm = pe.matmul(out, W2[:, 0, 0:2 * HD], HIDB[:, s, 0, (2 * j + 1) * NB:(2 * j + 2) * NB],
                                        start=False, stop=True)
                last_mm.then_inc(ck, 1)
                for g in range(NKV):
                    last_mm = pe.matmul(ps[5][0:NB, g * HD:(g + 1) * HD], HIDB[:, s, 1, g * NB:(g + 1) * NB],
                                        W2[:, 1, HD:2 * HD], start=True, stop=True)
                last_mm.then_inc(cv, 1)
                nxt(0, 1)
                pe.wait_ge(squared, b + 1)
                pe.matmul(ps[4][:, 2 * NB:4 * NB], blockones, SQ.rearrange("p j c -> p (j c)"), start=True, stop=True)\
                    .then_inc(ss, 1)
                nxt(1, 0)
                pe.wait_ge(ckt, b + 1)
                pe.wait_ge(qb, b * 4 + 4)
                if not (first and s == 0):
                    pe.wait_ge(chosen, b)
                for j in range(2):
                    last_mm = pe.matmul(ps[6][:, 0:NB], QB[:, s, j, :], CKT[:, j, :], start=(j == 0), stop=(j == 1))
                last_mm.then_inc(score, 1)
                nxt(1, 1)
                pe.wait_ge(prob, b + 1)
                pe.matmul(ps[6][:, NB:2 * NB], headsum, PR, start=True, stop=True).then_inc(pooled, 1)

            for kind in range(2):
                for half in range(2):
                    hide_after(0, 0, kind, half, True)
            over_sequences(pe, seq)

        @block.scalar
        def _(act):
            def take_gelu(b, s, first):
                for kind in range(2):
                    act.wait_ge(hidden, b * 2 + (kind + 1))
                    if not first:
                        act.wait_ge(cv, b - 1)
                    act.activation(HIDB[:, s, kind, :], ps[2 * s + kind][:, 1:NBLK + 1], ACT.Gelu_apprx_tanh)\
                        .then_inc(gelu, 1)

            def seq(b, s, first, last):
                act.wait_ge(ck, b + 1)
                if not (first and s == 0):
                    act.wait_ge(ss, b)
                act.activation(SQ.rearrange("p j c -> p (j c)"), ps[4][:, 0:2 * NB], ACT.Square).then_inc(squared, 1)
                act.wait_ge(mean, b + 1)
                act.activation(RS, RS, ACT.Sqrt).then_inc(root, 1)
                act.wait_ge(negmax, b + 1)
                act.activation(PR, ps[6][:, 0:NB], ACT.Exp, bias=sm[:, 0:1], scale=SCALE,).then_inc(expd, 1)
                if not last:
                    take_gelu(b + 1, 1 - s, first and s == 0)
            take_gelu(0, 0, True)
            over_sequences(act, seq)

        @block.vector
        def _(dve):
            V = nc.vector

            def seq(b, s, first, last):
                st = Steps(dve, chain, b * DCH)
                dve.wait_ge(cv, b + 1)
                V.tensor_copy(CV[0:NB, bass.ds(b, 1), :], ps[5][0:NB, 0:NKV * HD].unsqueeze(1)).then_inc(cv_out, 1)
                dve.wait_ge(ss, b + 1)
                V.tensor_scalar(RS, ps[4][:, 2 * NB:4 * NB].rearrange("p (j c) -> p j c", j=2), 1.0 / HD, EPS,
                                ALU.mult, ALU.add).then_inc(mean, 1)
                dve.wait_ge(root, b + 1)
                st.add(V.reciprocal(RS, RS))
                if not (first and s == 0):
                    dve.wait_ge(score, b)
                V.scalar_tensor_tensor(CKT, ps[4][:, 0:2 * NB].rearrange("p (j c) -> p j c", j=2), KG[:, 0:1], RS,
                                       ALU.mult, ALU.mult).then_inc(ckt, 1)
                dve.wait_ge(score, b + 1)
                st.add(V.tensor_reduce(sm[:, 1:2], ps[6][:, 0:NCS], AX.X, ALU.max))
                V.tensor_scalar(sm[:, 0:1], sm[:, 1:2], -SCALE, None, ALU.mult).then_inc(negmax, 1)
                dve.wait_ge(expd, b + 1)
                st.add(V.tensor_reduce(sm[:, 2:3], PR[:, 0:NCS], AX.X, ALU.add))
                st.add(V.reciprocal(sm[:, 3:4], sm[:, 2:3]))
                V.tensor_scalar(PR, PR, sm[:, 3:4], None, ALU.mult).then_inc(prob, 1)
                dve.wait_ge(prob, b + 1)
                V.tensor_scalar(PC[:, bass.ds(b, 1), :], PR.unsqueeze(1), GS[:, 0, bass.ds(b, 1)], None, ALU.mult)
                dve.wait_ge(pooled, b + 1)
                pg = ps[6][:, NB + 4:NB + 4 * (NSB - 2)].rearrange("p (j o) -> p j o", o=4)
                prev = ps[6][:, NB + 3:NB + 3 + 4 * (NSB - 3)].rearrange("p (j o) -> p j o", o=4)[:, :, 0]
                st.add(V.tensor_reduce(SCORE, pg, AX.X, ALU.add))
                st.add(V.tensor_tensor(SCORE, SCORE, prev, ALU.add))
                st.add(V.tensor_reduce(sm[:, 4:5], SCORE, AX.X, ALU.min))
                st.add(V.scalar_tensor_tensor(KEY, SCORE, sm[:, 4:5], iota, ALU.is_equal, ALU.mult))
                st.add(V.tensor_reduce(sm[:, 5:6], KEY, AX.X, ALU.max))
                st.add(V.tensor_scalar(KEY, iota, sm[:, 5:6], NEG, ALU.is_equal, ALU.mult))
                V.tensor_copy(BM[:, bass.ds(b, 1), 1:NSB - 2], KEY.unsqueeze(1)).then_inc(chosen, 1)
                assert st.n == DCH, st.n

            over_sequences(dve, seq)

    with ExitStack() as ctx:
        block = ctx.enter_context(nc.Block())

        @block.vector
        def _(dve):
            nc.vector.memset(BM[:, :, 0:1], 0.0)
            nc.vector.memset(BM[:, :, NSB - 2:16], 0.0)


def attend_samples(nc, I, M):
    ps, OT = M["ps"], M["XT"]
    SEL = [view(M, at, NPAGE, 512) for at in Map.SEL]
    WB = [view(M, at, 4 * WIN) for at in Map.WINB]
    QS, QB = view(M, Map.QSR, 2, HPG, NEWTOK), view(M, Map.QB, 3, 2, P)
    KTN = view(M, Map.KTN, 2, 2, NEWTOK)
    VNEW = view(M, Map.VNEW, NKV * HD)
    CV, PC, BM = view(M, Map.CV, NSEQ, NKV * HD), view(M, Map.PC, NSEQ, NCS + 1), view(M, Map.BM, NSEQ, 16)
    GS = view(M, Map.GS, 3, NSEQ)
    NEW = PAST
    WCOL = PAST + 2 * NEWTOK
    CCOL = WCOL + WIN
    NCOL = CCOL + NCS + 1
    NTILE = 14
    PR, PT = [view(M, at, NCOL) for at in Map.PROW], view(M, Map.PT, NTILE, P)
    sm, OWN = view(M, Map.SMALL, 3, 32), view(M, Map.SMALL + 128, HD)
    newmask = const(M, "newmask").rearrange("p (b t) -> p b t", b=NSEQ)
    winmask, ident = const(M, "winmask"), const(M, "ident")
    tiles = [(i * P, P) for i in range(NPAGE + 1)] + [(WCOL + i * P, P) for i in range(WIN // P)] + [(CCOL, NCS)]
    LANDED = 16 * (NPAGE + 2)
    with ExitStack() as ctx:
        sem = lambda n: new_sem(nc, M, "atts_" + n)
        sequence_in = M["sequence_in"]
        qb, bmb = sem("queries_ready"), sem("blockmask_ready")
        score, masked, negmax, expd = sem("scores_ready"), sem("scores_read"), sem("negmax_ready"), sem("exp_ready")
        weighted, turned, by_dve, by_act = sem("probs_ready"), sem("probs_turned"), sem("turned_by_dve"), sem("turned_by_act")
        summed, own, oturned, out, chain = (sem("values_summed"), sem("own_values_copied"), sem("out_turned"),
                                            sem("out_copied"), sem("chain"))
        tail = sem("tail_copied")
        block = ctx.enter_context(nc.Block())
        DCH = 9

        def over_sequences(eng, body, first=1):
            with eng.Fori(0, 2) as i:
                for u in range(first, first + 3):
                    body(i * 3 + u, u % 3, i + u // 3)

        @block.sync
        def _(sp):
            def load(b, s, r):
                sp.wait_ge(turned, b * 4 - 7)
                load_sequence(sp, I, M, b, s)
            load_sequence(sp, I, M, 1, 1)
            over_sequences(sp, load, 2)

        @block.gpsimd
        def _(pool):
            def prepare(b, s, r):
                if not isinstance(b, int):
                    pool.wait_ge(score, b - 1)
                queries_of(nc, QS, QB, b, s, qb)
                pool.wait_ge(qb, b * 4 + 4)
                if not isinstance(b, int):
                    pool.wait_ge(masked, b * 4 - 4)
                nc.gpsimd.tensor_copy(sm[:, s, 16:32].unsqueeze(1), BM[:, bass.ds(b, 1), :]).then_inc(bmb, 1)
                pool.wait_ge(bmb, b + 1)
            prepare(0, 0, 0)
            prepare(1, 1, 0)
            over_sequences(pool, prepare, 2)

        @block.tensor
        def _(pe):
            def scores(b, s, r):
                pe.wait_ge(qb, b * 4 + 4)
                pe.wait_ge(sequence_in[s], r * LANDED + LANDED)
                if not (isinstance(b, int) and b == 0):
                    pe.wait_ge(masked, b * 4)
                    pe.wait_ge(expd, b * 4)
                for bank in range(2):
                    for j in range(2):
                        pe.matmul(ps[bank][:, :], QB[:, s, j, :],
                                  SEL[s][:, 4 * bank:4 * bank + 4, j * PAGE:(j + 1) * PAGE], start=(j == 0), stop=(j == 1))
                for j in range(2):
                    pe.matmul(ps[3][:, 0:2 * NEWTOK].rearrange("p (r t) -> p r t", r=2), QB[:, s, j, :], KTN[:, :, j, :],
                              start=(j == 0), stop=(j == 1))
                for j in range(2):
                    last = pe.matmul(ps[2][:, :], QB[:, s, j, :], WB[s][:, j * WIN:(j + 1) * WIN], start=(j == 0), stop=(j == 1))
                last.then_inc(score, 1)

            def turn(b, s, q):
                later = not (isinstance(b, int) and b == 0)
                if q == 0:
                    pe.wait_ge(weighted, b * 3 + 3)
                if q == 1 and later:
                    pe.wait_ge(own, b * NKV)
                if q >= 2:
                    pe.wait_ge(*((by_dve, b + 1), (by_act, b * 3 + 1))[q % 2])
                elif later:
                    pe.wait_ge(by_act, b * 3)
                for m, (at, w) in enumerate(tiles[4 * q:4 * q + 4]):
                    last = pe.transpose(ps[4 + q % 2][0:w, m * P:(m + 1) * P], PR[s][:, at:at + w], ident)
                    if q == 1 and m == 0 and later:
                        turn_out()
                last.then_inc(turned, 1)

            def turn_out():
                pe.transpose(ps[7][0:HD, 0:P], OWN, ident).then_inc(oturned, 1)

            def values(b, s, r):
                pe.wait_ge(by_dve, b + 1)
                pe.wait_ge(by_act, b * 3 + 3)
                for t in range(NTILE):
                    if t < NPAGE:
                        v = SEL[s][:, t, 2 * PAGE:]
                    elif t == NPAGE:
                        v = VNEW
                    elif t < NTILE - 1:
                        at = 2 * WIN + (t - NPAGE - 1) * NKV * HD
                        v = WB[s][:, at:at + NKV * HD]
                    else:
                        v = CV[0:NCS, bass.ds(b, 1), :].rearrange("p a n -> p (a n)")
                    k = NCS if t == NTILE - 1 else P
                    last = pe.matmul(ps[6][:, 0:NKV * HD], PT[0:k, t, :], v, start=(t == 0), stop=(t == NTILE - 1))
                last.then_inc(summed, 1)

            def seq(b, s, r):
                turn(b, s, 0)
                turn(b, s, 1)
                if not (isinstance(b, int) and b == NSEQ - 1):
                    scores(b + 1, (s + 1) % 3, r + (s + 1) // 3)
                turn(b, s, 2)
                turn(b, s, 3)
                values(b, s, r)
            scores(0, 0, 0)
            seq(0, 0, 0)
            over_sequences(pe, seq)
            seq(NSEQ - 1, (NSEQ - 1) % 3, (NSEQ - 1) // 3)
            pe.wait_ge(own, NSEQ * NKV)
            turn_out()

        @block.scalar
        def _(act):
            def softmax(b, s):
                act.wait_ge(negmax, b + 1)
                for n, (dst, src, br) in enumerate(((slice(0, PAST), PR[s][:, 0:PAST], 0),
                                                    (slice(NEW, NEW + NEWTOK), PR[s][:, NEW:NEW + NEWTOK], 0),
                                                    (slice(NEW + NEWTOK, WCOL), PR[s][:, NEW + NEWTOK:WCOL], 1),
                                                    (slice(WCOL, CCOL), ps[2][:, :], 1))):
                    act.activation(PR[s][:, dst], src, ACT.Exp, bias=sm[:, s, br:br + 1], scale=SCALE,
                                   accum_out=sm[:, s, 4 + n:5 + n]).then_inc(expd, 1)

            def seq(b, s, r):
                for q in range(1, 4):
                    act.wait_ge(turned, b * 4 + (q + 1))
                    bank = ps[4 + q % 2]
                    if q < 3:
                        nc.scalar.copy(PT[:, 4 * q:4 * q + 4, :].rearrange("p m t -> p (m t)"), bank[:, :]).then_inc(by_act, 1)
                    else:
                        nc.scalar.copy(PT[0:NCS, 13, :], bank[0:NCS, P:2 * P]).then_inc(tail, 1)
                        nc.scalar.copy(PT[:, 12, :], bank[:, 0:P]).then_inc(by_act, 1)
                if not (isinstance(b, int) and b == NSEQ - 1):
                    softmax(b + 1, (s + 1) % 3)
            softmax(0, 0)
            seq(0, 0, 0)
            over_sequences(act, seq)
            seq(NSEQ - 1, (NSEQ - 1) % 3, (NSEQ - 1) // 3)

        @block.vector
        def _(dve):
            V = nc.vector

            def maxima(b, s):
                st = Steps(dve, chain, b * DCH)
                dve.wait_ge(score, b + 1)
                dve.wait_ge(bmb, b + 1)
                V.tensor_tensor(PR[s][:, NEW:WCOL].rearrange("p (r t) -> p r t", r=2),
                                ps[3][:, 0:2 * NEWTOK].rearrange("p (r t) -> p r t", r=2),
                                newmask[:, bass.ds(b, 1), :].broadcast_to([P, 2, NEWTOK]), ALU.add).then_inc(masked, 1)
                for bank in range(2):
                    V.tensor_tensor_reduce(
                        PR[s][:, bank * 512:(bank + 1) * 512].rearrange("p (k c) -> p k c", c=SELB),
                        ps[bank][:, :].rearrange("p (k c) -> p k c", c=SELB),
                        sm[:, s, 16 + 8 * bank:24 + 8 * bank].unsqueeze(2).broadcast_to([P, 8, SELB]),
                        1.0, -3e38, ALU.add, ALU.max, sm[:, s, 8 + bank:9 + bank]).then_inc(masked, 1)
                V.tensor_tensor(ps[2][:, 0:STEPS], ps[2][:, 0:STEPS], winmask, ALU.add).then_inc(masked, 1)
                dve.wait_ge(masked, b * 4 + 4)
                st.add(V.tensor_reduce(sm[:, s, 10:12], PR[s][:, NEW:WCOL].rearrange("p (r t) -> p r t", r=2), AX.X, ALU.max))
                st.add(V.tensor_reduce(sm[:, s, 12:13], ps[2][:, :], AX.X, ALU.max))
                st.add(V.tensor_tensor(sm[:, s, 13:14], sm[:, s, 8:9], sm[:, s, 9:10], ALU.max))
                st.add(V.tensor_tensor(sm[:, s, 14:15], sm[:, s, 10:11], sm[:, s, 13:14], ALU.max))
                st.add(V.tensor_tensor(sm[:, s, 15:16], sm[:, s, 11:12], sm[:, s, 12:13], ALU.max))
                V.tensor_scalar(sm[:, s, 0:2], sm[:, s, 14:16], -SCALE, None, ALU.mult).then_inc(negmax, 1)
                return st

            def weights(b, s, st):
                dve.wait_ge(expd, b * 4 + 4)
                st.add(V.tensor_tensor(sm[:, s, 8:9], sm[:, s, 4:5], sm[:, s, 5:6], ALU.add))
                st.add(V.tensor_tensor(sm[:, s, 9:10], sm[:, s, 6:7], sm[:, s, 7:8], ALU.add))
                st.add(V.reciprocal(sm[:, s, 10:12], sm[:, s, 8:10]))
                st.add(V.tensor_tensor(sm[:, s, 12:14].unsqueeze(2), sm[:, s, 10:12].unsqueeze(2),
                                       GS[:, 1:3, bass.ds(b, 1)], ALU.mult))
                V.tensor_scalar(PR[s][:, 0:NEW + NEWTOK], PR[s][:, 0:NEW + NEWTOK], sm[:, s, 12:13], None, ALU.mult)\
                    .then_inc(weighted, 1)
                V.tensor_scalar(PR[s][:, NEW + NEWTOK:CCOL], PR[s][:, NEW + NEWTOK:CCOL], sm[:, s, 13:14], None, ALU.mult)\
                    .then_inc(weighted, 1)
                V.tensor_copy(PR[s][:, CCOL:NCOL].unsqueeze(1), PC[:, bass.ds(b, 1), :]).then_inc(weighted, 1)
                assert st.n == DCH, st.n

            def seq(b, s, r):
                dve.wait_ge(turned, b * 4 + 1)
                V.tensor_copy(PT[:, 0:4, :].rearrange("p m t -> p (m t)"), ps[4][:, :]).then_inc(by_dve, 1)
                if not (isinstance(b, int) and b == 0):
                    copy_out(b - 1)
                if not (isinstance(b, int) and b == NSEQ - 1):
                    weights(b + 1, (s + 1) % 3, maxima(b + 1, (s + 1) % 3))
                dve.wait_ge(summed, b + 1)
                for g in range(NKV):
                    r = slice(g * HPG * STEPS, (g + 1) * HPG * STEPS)
                    V.tensor_copy(OWN[r, :], ps[6][r, g * HD:(g + 1) * HD]).then_inc(own, 1)

            def copy_out(b):
                dve.wait_ge(oturned, b + 1)
                for par in range(2):
                    src = ps[7][0:HD, 0:P].rearrange("p (k r t) -> p k r t", r=2, t=STEPS)[:, :, par, :]
                    V.tensor_copy(OT[par * HD:(par + 1) * HD, :, bass.ds(b * STEPS + SEQ, STEPS)], src).then_inc(out, 1)
            weights(0, 0, maxima(0, 0))
            seq(0, 0, 0)
            over_sequences(dve, seq)
            seq(NSEQ - 1, (NSEQ - 1) % 3, (NSEQ - 1) // 3)
            copy_out(NSEQ - 1)


def attend_prompt(nc, I, M):
    ps, OT, gates = M["ps"], M["XT"], M["gates"]
    QN, QR = view(M, Map.QNT, 2, HPG, SEQ), view(M, Map.QRT, 2, HPG, SEQ)
    KT, CKP = view(M, Map.KTP, 2, 2, SEQ), view(M, Map.CKP, 2, CHUNK)
    VP, CVP = view(M, Map.VP, 2, 2, NKV, 3 * HD), view(M, Map.CVP, NKV, 3 * HD)
    PTC = view(M, Map.PTC, 2, NH, P)
    PTP = view(M, Map.PTP, 2, 4, P)
    PP = view(M, Map.PP, 3, 2, SEQ)
    PCM = view(M, Map.PP + 6 * SEQ, NH, CHUNK)
    sm = view(M, Map.SMALL, 3, 16)
    csm = view(M, Map.SMALL + 64, 4, NH)
    causal = const(M, "causal").rearrange("p (t k) -> p t k", t=2)
    cadd = const(M, "cmpadd").rearrange("p (t k) -> p t k", t=2)
    cmul = const(M, "cmpmul").rearrange("p (t k) -> p t k", t=2)
    ident = const(M, "ident")
    WO = view(M, Map.WO, KD, D)
    units = [(t, hd) for t in range(2) for hd in range(NH)]
    NU = len(units)
    wo_in = M["wo_in"]

    def part(hd):
        g, h = hd // HPG, hd % HPG
        return slice((g % 2) * HD, (g % 2) * HD + HD), g // 2, h

    def v_cols(hd):
        return slice(0, 2 * HD) if hd % 2 else slice(HD, 3 * HD)

    with ExitStack() as ctx:
        sem = lambda n: new_sem(nc, M, "attp_" + n)
        cscore, cprob, cturned, ccopied, cneg, cexp = (sem("cmp_scores_ready"), sem("cmp_probs_ready"), sem("cmp_turned"),
                                                       sem("cmp_copied"), sem("cmp_shifted"), sem("cmp_exp_ready"))
        score, negmax, expd, weighted = sem("scores_ready"), sem("negmax_ready"), sem("exp_ready"), sem("probs_ready")
        masked, turned, copied, summed, out, chain = (sem("scores_masked"), sem("probs_turned"), sem("turned_copied"),
                                                      sem("values_summed"), sem("out_copied"), sem("chain"))
        product, added = sem("out_product_ready"), sem("out_product_added")
        turns = {0: 0, 1: 1, 2: 2, 3: 3, 7: 4, 8: 5, 9: 6, 10: 7}
        SCORES1, EXP1 = 4, 5
        share, adds = {}, {}
        for at, tile, half in ((11, 2, 0), (16, 2, 1), (21, 0, 0), (26, 0, 1)):
            for k in range(KD):
                share.setdefault(at + k // 2, []).append((tile, half, k))
            adds[at + KD // 2] = (tile, half)
        block = ctx.enter_context(nc.Block())

        @block.sync
        def _(sp):
            sp.dma_start(WO, I["w_o"][0].rearrange("(k p) n -> p k n", p=P)).then_inc(wo_in, 16)

        @block.tensor
        def _(pe):
            def scores(n):
                t, hd = units[n]
                pp, j, h = part(hd)
                if n >= 3:
                    pe.wait_ge(masked, 2 * (n - 2))
                K = P * (t + 1)
                for br in range(2):
                    last = pe.matmul(ps[n % 3][:, br * K:(br + 1) * K], QR[pp, j, h, t * P:(t + 1) * P],
                                     KT[pp, br, j, 0:K], start=True, stop=True)
                last.then_inc(score, 1)

            def turn(n):
                t, hd = units[n]
                pe.wait_ge(weighted, 2 * (n + 1))
                if n >= 2:
                    pe.wait_ge(copied, n - 1)
                m = 0
                for br in range(2):
                    for kt in range(t + 1):
                        last = pe.transpose(ps[3 + n % 2][:, m * P:(m + 1) * P], PP[:, n % 3, br, kt * P:(kt + 1) * P], ident)
                        m += 1
                last.then_inc(turned, 1)

            def values(n):
                t, hd = units[n]
                g, h, pair = hd // HPG, hd % HPG, n // 2
                pe.wait_ge(copied, n + 1)
                if h == 0:
                    pe.wait_ge(ccopied, 4 * t + g + 1)
                if hd % 2 == 0 and pair >= 2:
                    pe.wait_ge(out, pair - 1)
                bank = ps[5 + pair % 2][:, 0:P]
                m = 0
                for br in range(2):
                    for kt in range(t + 1):
                        pe.matmul(bank, VP[:, kt, br, g, v_cols(hd)], PTP[:, n % 2, m, :],
                                  start=(hd % 2 == 0 and m == 0), stop=False)
                        m += 1
                pe.matmul(bank, CVP[0:NCP, g, v_cols(hd)], PTC[0:NCP, t, hd, :], start=False, stop=(hd % 2 == 1))\
                    .then_inc(summed, 1)

            def project_out(tile, half, k):
                if k == 0:
                    done = 2 * (tile == 0) + half
                    if done == 0:
                        pe.wait_ge(wo_in, 16)
                        pe.wait_ge(ccopied, 8)
                    else:
                        pe.wait_ge(added, done)
                    if done == 2:
                        pe.wait_ge(out, NH // 2)
                rows = TILE_ROWS[tile]
                last = pe.matmul(ps[7][0:rows, :], OT[:, k, tile * P:tile * P + rows], WO[:, k, half * 512:(half + 1) * 512],
                                 start=(k == 0), stop=(k == KD - 1))
                if k == KD - 1:
                    last.then_inc(product, 1)

            def compressed(t):
                if t:
                    pe.wait_ge(ccopied, 4)
                for par in range(2):
                    for hd in [x for x in range(NH) if x // HPG % 2 == par]:
                        pp, j, h = part(hd)
                        last = pe.matmul(ps[7][:, hd * CHUNK:hd * CHUNK + NCP], QN[pp, j, h, t * P:(t + 1) * P],
                                         CKP[pp, j, 0:NCP], start=True, stop=True)
                    last.then_inc(cscore, 1)
                    pe.wait_ge(cscore, 2 * t + par + 1)

            def turn_compressed(t, q):
                pe.wait_ge(cprob, t + 1)
                if q:
                    pe.wait_ge(ccopied, 4 * t + q)
                for m in range(4):
                    last = pe.transpose(ps[7][0:NCP, m * P:(m + 1) * P], PCM[:, 4 * q + m, 0:NCP], ident)
                last.then_inc(cturned, 1)

            compressed(0)
            scores(0)
            scores(1)
            for n in range(NU + 1):
                if n + 2 < NU:
                    scores(n + 2)
                if n < NU:
                    turn(n)
                if n in turns:
                    turn_compressed(turns[n] // 4, turns[n] % 4)
                if n >= 1:
                    values(n - 1)
                for tile, half, k in share.get(n, []):
                    project_out(tile, half, k)
                if n == SCORES1:
                    compressed(1)

        @block.scalar
        def _(act):
            def unit(n):
                t, hd = units[n]
                K = P * (t + 1)
                act.wait_ge(negmax, n + 1)
                for br in range(2):
                    act.activation(PP[:, n % 3, br, 0:K], PP[:, n % 3, br, 0:K], ACT.Exp, bias=sm[:, n % 3, br:br + 1],
                                   scale=SCALE, accum_out=sm[:, n % 3, 4 + br:5 + br]).then_inc(expd, 1)

            def copy_turned(n):
                t, hd = units[n]
                act.wait_ge(turned, n + 1)
                if n >= 2:
                    act.wait_ge(summed, n - 1)
                w = 2 * (t + 1)
                nc.scalar.copy(PTP[:, n % 2, 0:w, :].rearrange("p m q -> p (m q)"), ps[3 + n % 2][:, 0:w * P])\
                    .then_inc(copied, 1)

            def exp_compressed(t):
                act.wait_ge(cneg, t + 1)
                act.activation(PCM[:, :, 0:NCP], PCM[:, :, 0:NCP], ACT.Exp, scale=SCALE).then_inc(cexp, 1)

            def copy_compressed(t, q):
                act.wait_ge(cturned, 4 * t + q + 1)
                nc.scalar.copy(PTC[0:NCP, t, 4 * q:4 * q + 4, :].rearrange("p m q -> p (m q)"), ps[7][0:NCP, :])\
                    .then_inc(ccopied, 1)

            exp_compressed(0)
            unit(0)
            for n in range(NU):
                if n + 1 < NU:
                    unit(n + 1)
                copy_turned(n)
                if n in turns:
                    copy_compressed(turns[n] // 4, turns[n] % 4)
                if n == EXP1:
                    exp_compressed(1)

        @block.vector
        def _(dve):
            V = nc.vector
            st = Steps(dve, chain)

            def compressed(t):
                dve.wait_ge(cscore, 2 * (t + 1))
                s = ps[7][:, 0:NH * CHUNK].rearrange("p (h c) -> p h c", h=NH)[:, :, 0:NCP]
                x = PCM[:, :, 0:NCP]
                if t:
                    dve.wait_ge(cturned, 4)
                add = cadd[:, t].unsqueeze(1).broadcast_to([P, NH, NCP])
                mul = cmul[:, t].unsqueeze(1).broadcast_to([P, NH, NCP])
                st.add(V.tensor_tensor(x, s, add, ALU.add))
                st.add(V.tensor_reduce(csm[:, 0], x, AX.X, ALU.max))
                V.tensor_tensor(x, x, csm[:, 0].unsqueeze(2).broadcast_to([P, NH, NCP]), ALU.subtract).then_inc(cneg, 1)
                dve.wait_ge(cexp, t + 1)
                st.add(V.tensor_tensor(x, x, mul, ALU.mult))
                st.add(V.tensor_reduce(csm[:, 1], x, AX.X, ALU.add))
                st.add(V.tensor_scalar(csm[:, 1], csm[:, 1], 1e-30, None, ALU.max))
                st.add(V.reciprocal(csm[:, 2], csm[:, 1]))
                st.add(V.tensor_tensor(csm[:, 2], csm[:, 2], gates[:, t, 0:NH], ALU.mult))
                V.tensor_tensor(x, x, csm[:, 2].unsqueeze(2).broadcast_to([P, NH, NCP]), ALU.mult).then_inc(cprob, 1)

            def before(n):
                t, hd = units[n]
                K = P * (t + 1)
                s = n % 3
                dve.wait_ge(score, n + 1)
                if n >= 3:
                    dve.wait_ge(turned, n - 2)
                for br in range(2):
                    V.tensor_tensor_reduce(PP[:, s, br, 0:K], ps[n % 3][:, br * K:(br + 1) * K], causal[:, t, 0:K],
                                           1.0, -3e38, ALU.add, ALU.max, sm[:, s, 2 + br:3 + br]).then_inc(masked, 1)
                dve.wait_ge(masked, 2 * (n + 1))
                V.tensor_scalar(sm[:, s, 0:2], sm[:, s, 2:4], -SCALE, None, ALU.mult).then_inc(negmax, 1)

            def after(n):
                t, hd = units[n]
                K = P * (t + 1)
                s = n % 3
                dve.wait_ge(expd, 2 * (n + 1))
                st.add(V.reciprocal(sm[:, s, 6:8], sm[:, s, 4:6]))
                st.add(V.tensor_tensor(sm[:, s, 8:10], sm[:, s, 6:8], gates[:, t, NH + hd:2 * NH + hd + 1:NH], ALU.mult))
                for br in range(2):
                    V.tensor_scalar(PP[:, s, br, 0:K], PP[:, s, br, 0:K], sm[:, s, 8 + br:9 + br], None, ALU.mult)\
                        .then_inc(weighted, 1)

            def add_product(n):
                tile, half = adds[n]
                rows = TILE_ROWS[tile]
                dve.wait_ge(product, 2 * (tile == 0) + half + 1)
                hv = M["H"][0:rows, tile, half * 512:(half + 1) * 512]
                V.tensor_tensor(hv, ps[7][0:rows, :], hv, ALU.add).then_inc(added, 1)

            def copy_out(n):
                t, hd = units[n]
                if hd % 2:
                    dve.wait_ge(summed, n + 1)
                    V.tensor_copy(OT[:, hd // 2, t * P:(t + 1) * P], ps[5 + (n // 2) % 2][:, 0:P]).then_inc(out, 1)

            compressed(0)
            before(0)
            for n in range(NU + 2):
                if n + 1 < NU:
                    before(n + 1)
                if n < NU:
                    after(n)
                if n >= 2:
                    copy_out(n - 2)
                if n in adds:
                    add_product(n)
                if n == EXP1:
                    compressed(1)


def output_projection(nc, M):
    H, OT, ps, WO = M["H"], M["XT"], M["ps"], view(M, Map.WO, KD, D)
    with ExitStack() as ctx:
        sem = lambda n: new_sem(nc, M, "out_" + n)
        product, added = sem("product_ready"), sem("added")
        block = ctx.enter_context(nc.Block())
        parts = [(1, P, half) for half in range(2)]

        @block.tensor
        def _(pe):
            for n, (i, rows, half) in enumerate(parts):
                for k in range(KD):
                    last = pe.matmul(ps[n][0:rows, :], OT[:, k, i * P:i * P + rows], WO[:, k, half * 512:(half + 1) * 512],
                                     start=(k == 0), stop=(k == KD - 1))
                last.then_inc(product, 1)

        @block.vector
        def _(dve):
            for n, (i, rows, half) in enumerate(parts):
                dve.wait_ge(product, n + 1)
                hv = H[0:rows, i, half * 512:(half + 1) * 512]
                nc.vector.tensor_tensor(hv, ps[n][0:rows, :], hv, ALU.add).then_inc(added, 1)


def constant_tables():
    import numpy as np
    tables = {name: np.zeros((P, n), np.float32) for name, n in NCONST.items()}

    def put(name, a):
        a = np.asarray(a, np.float32)
        a = a.reshape(a.shape[0], -1)
        table, at, w = CONST[name]
        assert a.shape[1] == w
        tables[table][:a.shape[0], at:at + w] = a

    p = np.arange(P)
    put("ident", np.eye(P))
    put("blockones", (p[:, None] // HD == p[None] // HD))
    grp, step = p // (HPG * STEPS), p % STEPS
    put("headsum", (grp[:, None] == grp[None]) & (step[:, None] == step[None]))
    q = np.arange(SEQ).reshape(2, P).T
    put("causal", np.where(np.arange(SEQ)[None, None] <= q[:, :, None], 0.0, NEG))
    ok = (np.arange(NCP) * CHUNK + 2 * CHUNK - 1)[None, None] <= q[:, :, None]
    put("cmpadd", np.where(ok, 0.0, NEG))
    put("cmpmul", ok)
    b, col = np.arange(NSEQ), np.arange(NEWTOK)
    mine = (col[None, None] // STEPS == b[None, :, None]) & (col[None, None] % STEPS <= step[:, None, None])
    put("newmask", np.where(mine, 0.0, NEG))
    put("winmask", np.where(np.arange(STEPS)[None] > step[:, None], 0.0, NEG))
    put("iota", np.tile(np.arange(1, NSB - 2), (P, 1)))
    r = np.arange(NEWTOK)
    put("stepsel", (r[:, None] % STEPS) == np.arange(STEPS)[None])
    put("seqsel", (r[:, None] // STEPS) == np.arange(NSEQ)[None])
    put("first", np.tile(np.arange(NG, 0, -1), (P, 1)))
    put("before", p[:, None] < p[None])
    put("ones", np.ones((P, P)))
    put("slots", np.tile(np.arange(CAP), (P, 1)))
    put("experts", np.tile(np.arange(NE), (P, 1)))
    half = HD // 2
    inv = np.float32(1.0) / (np.float32(10000.0) ** (np.arange(half, dtype=np.float32) * np.float32(2.0 / HD)))
    pos = np.zeros((P, NT), np.float32)
    pos[:, 0], pos[:, 1] = p, p + P
    pos[:NEWTOK, 2] = PAST + r % STEPS
    ang = (pos[:, :, None] * inv[None, None]).astype(np.float32)
    put("cos", np.cos(ang))
    put("sin", np.sin(ang))
    return tables


def pooling_matrices():
    import numpy as np
    m = np.zeros((P, NPOOL, NPM), np.float32)
    for g, w in enumerate(POOL_WINDOWS):
        for t in range(SEQ):
            lo = max(t + 1 - w, 0)
            for s in range(lo, t + 1):
                m[s % P, g, (s // P) * SEQ + t] += np.float32(1.0 / (t + 1 - lo))
            m[t % P, g, (t // P) * SEQ + t] -= 1.0
        for b in range(NSEQ):
            for t in range(STEPS):
                for s in range(STATE + t + 1 - w, STATE + t + 1):
                    if s < STATE:
                        m[b * STATE + s, g, 2 * SEQ + b * STEPS + t] += 1.0 / w
                    else:
                        m[b * STEPS + s - STATE, g, 2 * SEQ + NEWTOK + b * STEPS + t] += 1.0 / w
                m[b * STEPS + t, g, 2 * SEQ + NEWTOK + b * STEPS + t] -= 1.0
    return m


_PLAIN = ["x_prompt", "x_sample", "state_pool", "state_win", "norm_mix", "norm_ffn", "pool_w", "pool_scale", "w_kv", "cmp_w1",
          "cmp_b1", "cmp_w2", "w_qg", "w_o", "router_group", "router_expert", "w_gate_up", "w_down", "k_norm", "q_norm"]
_OUTS = [("y_prompt", (1, SEQ, D)), ("y_sample", (NSEQ, STEPS, D)), ("new_pool_prompt", (1, 1, STATE, D)),
         ("new_pool_sample", (1, NSEQ, STATE, D)), ("new_kv_prompt", (1, SEQ, 4, NKV, HD)),
         ("new_kv_sample", (NSEQ, STEPS, 4, NKV, HD)), ("new_win_prompt", (1, SEQ, 2, NKV, HD)),
         ("new_win_sample", (NSEQ, WIN, 2, NKV, HD))]


def kernel(**inputs):
    import numpy as np
    import concourse.bacc as bacc
    from concourse.bass_utils import run_bass_kernel_spmd

    x = {k: np.asarray(v) for k, v in inputs.items()}
    arrays = {n: x[n] for n in _PLAIN}
    tables = constant_tables()
    arrays["consts"], arrays["attention_consts"] = tables["C"], tables["CA"]
    arrays["pool_mats"] = pooling_matrices()
    gains = [x["norm_mix"][0], x["norm_ffn"][0], x["norm_mix"][1], x["kv_norm"], x["norm_ffn"][1]]
    arrays["gainsT"] = np.stack([g.reshape(KD, P).T for g in gains], axis=1)
    arrays["page_ids"] = x["page_table"].reshape(1, -1)
    pages = x["cache_kv"]
    n = pages.shape[0]
    raw = pages[:, :, 0:2].reshape(n, PAGE // CHUNK, CHUNK // 2, 2, 2, NKV, HD)
    arrays["pages_raw"] = raw.transpose(0, 3, 6, 4, 2, 5, 1).reshape(n, P, -1)
    ksel = pages[:, :, 2].reshape(n, PAGE, 2, P).transpose(0, 3, 2, 1).reshape(n, P, 2 * PAGE)
    arrays["pages_sel"] = np.concatenate([ksel, pages[:, :, 3].reshape(n, PAGE, NKV * HD)], axis=2)
    arrays["win_keysT"] = x["state_win"][:, :, 0].reshape(NSEQ, WIN, 2, P).transpose(0, 3, 2, 1).reshape(NSEQ, P, 2 * WIN)
    arrays["cmp_pe"] = x["cmp_pe"].reshape(2, 2, CHUNK // 2, P).transpose(3, 0, 1, 2)
    arrays["k_gainT"] = np.concatenate([x["k_norm"][0], x["k_norm"][0]]).reshape(P, 1)

    nc = bacc.Bacc("TRN2", target_bir_lowering=False, num_devices=1)
    feed, I, O = {}, {}, {}
    for name, a in arrays.items():
        a = np.ascontiguousarray(a)
        feed[f"in_{name}"] = a
        I[name] = nc.dram_tensor(f"in_{name}", a.shape, mybir.dt.from_np(a.dtype), kind="ExternalInput").ap()
    for name, shape in _OUTS:
        O[name] = nc.dram_tensor(f"out_{name}", shape, F32, kind="ExternalOutput").ap()
    build(nc, I, O)
    r = run_bass_kernel_spmd(nc, [feed], core_ids=[0])
    return tuple(r.results[0][f"out_{name}"] for name, _ in _OUTS)
```
